# Optimizing a Trainium2 kernel written in Bass

```python
import jax, jax.numpy as jnp
from jax import lax
import numpy as np

D_MODEL = 1024
BATCH = 1
SEQ = 1024
DEPTH = 1
DEC_BATCH = 8
DEC_SEQ = 16
PAST_LEN = 1024

CHUNK = 64
D_RNN = 1024
N_LRU_BLOCKS = 16
LRU_BLOCK = D_RNN // N_LRU_BLOCKS
CONV_W = 4
LRU_C = 8.0
SB_HEADS = 4
SB_HEAD_DIM = 128
SB_WIDTH = SB_HEADS * SB_HEAD_DIM
Q_BLOCK = 128
KEY_BLOCK = 128
ML_HEADS = 4
ML_QK_DIM = 64
ML_V_DIM = 128
ML_QK_WIDTH = ML_HEADS * ML_QK_DIM
ML_V_WIDTH = ML_HEADS * ML_V_DIM
N_BRANCH = 3
N_EXPERTS = 32
TOP_K = 4
D_FF = 512
SWIGLU_LIMIT = 7.0
SWIGLU_ALPHA = 1.702
MAX_GROUP_BLOCK = 1024
D_PLE = 256
DN_ALPHA = (2 * DEPTH) ** 0.25
DN_BETA = (8 * DEPTH) ** -0.25
LN_EPS = 1e-5
IN_WIDTHS = (D_RNN, D_RNN, SB_WIDTH, SB_WIDTH, SB_WIDTH, ML_QK_WIDTH, ML_QK_WIDTH,
             ML_V_WIDTH, ML_V_WIDTH, ML_HEADS, ML_HEADS, N_BRANCH * D_MODEL)
N_IN = sum(IN_WIDTHS)
F_GATE_OFF = sum(IN_WIDTHS[:10])
F32 = jnp.float32

kernel_name = 'hybrid_streaming_encoder_step'

def _layer_norm(x, g, b):
    xf = x.astype(F32)
    mu = jnp.mean(xf, axis=-1, keepdims=True)
    var = jnp.mean(jnp.square(xf - mu), axis=-1, keepdims=True)
    return ((xf - mu) * lax.rsqrt(var + LN_EPS) * g.astype(F32) + b.astype(F32)).astype(x.dtype)

def _causal_conv(u, buf, w, b):
    L = u.shape[1]
    ext = jnp.concatenate([buf.astype(u.dtype), u], axis=1)
    y = b + ext[:, 0:L] * w[0]
    for j in range(1, CONV_W):
        y = y + ext[:, j:j + L] * w[j]
    return y, ext[:, L:]

def _block_diag(u, w, b):
    ub = u.reshape(u.shape[:-1] + (N_LRU_BLOCKS, LRU_BLOCK))
    return jnp.einsum('blnc,ncd->blnd', ub, w).reshape(u.shape) + b

def _rg_lru(u, h0, wr, br, wi, bi, lam, first_frame):
    uf = u.astype(F32)
    r = jax.nn.sigmoid(_block_diag(uf, wr.astype(F32), br.astype(F32)))
    i = jax.nn.sigmoid(_block_diag(uf, wi.astype(F32), bi.astype(F32)))
    log_a = -LRU_C * r * jax.nn.softplus(-lam.astype(F32))
    a = jnp.exp(log_a)
    mult = jnp.sqrt(-jnp.expm1(2.0 * log_a))
    if first_frame:
        mult = mult.at[:, 0].set(1.0)
    bx = mult * (i * uf)
    bx = bx.at[:, 0].add(a[:, 0] * h0.astype(F32))

    def combine(e1, e2):
        a1, b1 = e1
        a2, b2 = e2
        return a1 * a2, a2 * b1 + b2

    _, h = lax.associative_scan(combine, (a, bx), axis=1)
    return h, h[:, -1]

def _stick_breaking(q, k, v, q_pos, k_pos):
    B, Tk, H, d = k.shape
    Tq = q.shape[1]
    nkb = Tk // KEY_BLOCK
    z = jnp.einsum('bqhd,bkhd->bhqk', q, k).astype(F32).reshape(B, H, Tq, nkb, KEY_BLOCK)
    earlier = (k_pos[None, :] < q_pos[:, None]).reshape(Tq, nkb, KEY_BLOCK)
    u = jnp.where(earlier, jnp.maximum(z, 0.0) + jnp.log1p(jnp.exp(-jnp.abs(z))), 0.0)
    strict = jnp.triu(jnp.ones((KEY_BLOCK, KEY_BLOCK), F32), 1)
    within = jnp.einsum('bhqnj,jl->bhqnl', u, strict)
    blk = jnp.sum(u, axis=-1)
    rest = jnp.sum(blk, axis=-1, keepdims=True) - (jnp.cumsum(blk, axis=-1) - blk)
    w = jnp.where(earlier, jnp.exp(z + within - rest[..., None]), 0.0)
    vb = v.reshape(B, nkb, KEY_BLOCK, H, d)
    return jnp.einsum('bhqnk,bnkhd->bqhd', w.astype(v.dtype), vb)

def _sb_prompt(q, k, v):
    S = q.shape[1]
    outs = []
    for qb in range(S // Q_BLOCK):
        lo, hi = qb * Q_BLOCK, (qb + 1) * Q_BLOCK
        outs.append(_stick_breaking(q[:, lo:hi], k[:, :hi], v[:, :hi], jnp.arange(lo, hi), jnp.arange(hi)))
    return jnp.concatenate(outs, axis=1)

def _mlstm_block(q, k, v, ig, lf, c, n, m):
    L = q.shape[2]
    b = jnp.cumsum(lf, axis=-1)
    causal = jnp.tril(jnp.ones((L, L), dtype=bool))
    dmat = jnp.where(causal, b[..., :, None] - b[..., None, :] + ig[..., None, :], -jnp.inf)
    inter = b + m[..., None]
    m_t = jnp.maximum(inter, jnp.max(dmat, axis=-1))
    s_inter = jnp.exp(inter - m_t)
    wqk = jnp.exp(dmat - m_t[..., None]) * jnp.einsum('bhtd,bhsd->bhts', q, k)
    num = s_inter[..., None] * jnp.einsum('bhtd,bhde->bhte', q, c) + jnp.einsum('bhts,bhse->bhte', wqk, v)
    den = s_inter * jnp.einsum('bhtd,bhd->bht', q, n) + jnp.sum(wqk, axis=-1)
    h = num / jnp.maximum(jnp.abs(den), jnp.exp(-m_t))[..., None]
    b_end = b[..., -1]
    g = b_end[..., None] - b + ig
    m_new = jnp.maximum(b_end + m, jnp.max(g, axis=-1))
    s_old = jnp.exp(b_end + m - m_new)
    wg = jnp.exp(g - m_new[..., None])
    c_new = s_old[..., None, None] * c + jnp.einsum('bhs,bhsd,bhse->bhde', wg, k, v)
    n_new = s_old[..., None] * n + jnp.einsum('bhs,bhsd->bhd', wg, k)
    return h, (c_new, n_new, m_new)

def _mlstm_prompt(q, k, v, ig, lf):
    B, H, S, _ = q.shape
    nc = S // CHUNK

    def chunks(t):
        return jnp.moveaxis(t.reshape(t.shape[:2] + (nc, CHUNK) + t.shape[3:]), 2, 0)

    init = (jnp.zeros((B, H, ML_QK_DIM, ML_V_DIM), F32), jnp.zeros((B, H, ML_QK_DIM), F32),
            jnp.zeros((B, H), F32))

    def step(carry, xs):
        h, new = _mlstm_block(*xs, *carry)
        return new, h

    state, hs = lax.scan(step, init, (chunks(q), chunks(k), chunks(v), chunks(ig), chunks(lf)))
    return jnp.moveaxis(hs, 0, 2).reshape(B, H, S, ML_V_DIM), state

def _moe(x, rw, rb, w1, b1, w2, b2):
    B, L, D = x.shape
    T = B * L
    t = x.reshape(T, D)
    logits = (t @ rw + rb).astype(F32)
    top_v, top_i = lax.top_k(logits, TOP_K)
    gate = jax.nn.softmax(top_v, axis=-1)
    TK = T * TOP_K
    M = max(8, min(MAX_GROUP_BLOCK, TK // N_EXPERTS))
    NB = -(-TK // M) + N_EXPERTS
    R = NB * M
    e_flat = top_i.reshape(TK).astype(jnp.int32)
    order = jnp.argsort(e_flat).astype(jnp.int32)
    e_sorted = e_flat[order]
    tok_sorted = order // TOP_K
    g_sorted = gate.reshape(TK)[order].astype(t.dtype)
    counts = jnp.zeros((N_EXPERTS,), jnp.int32).at[e_flat].add(1)
    padded = (counts + (M - 1)) // M * M
    pend = jnp.cumsum(padded)
    shift = (pend - padded) - (jnp.cumsum(counts) - counts)
    dest = jnp.arange(TK, dtype=jnp.int32) + shift[e_sorted]
    xs = jnp.zeros((R, D), t.dtype).at[dest].set(t[tok_sorted])
    gs = jnp.zeros((R,), t.dtype).at[dest].set(g_sorted)
    ts = jnp.zeros((R,), jnp.int32).at[dest].set(tok_sorted)
    block_e = jnp.minimum(jnp.searchsorted(pend, jnp.arange(NB, dtype=jnp.int32) * M, side='right'),
                          N_EXPERTS - 1)
    gu = jnp.einsum('nmd,ndf->nmf', xs.reshape(NB, M, D), w1[block_e]) + b1[block_e][:, None]
    g_ = jnp.minimum(gu[..., :D_FF], SWIGLU_LIMIT)
    up = jnp.clip(gu[..., D_FF:], -SWIGLU_LIMIT, SWIGLU_LIMIT)
    act = (up + 1.0) * g_ * jax.nn.sigmoid(SWIGLU_ALPHA * g_)
    y = jnp.einsum('nmf,nfd->nmd', act, w2[block_e]) + b2[block_e][:, None]
    y = y.reshape(R, D) * gs[:, None]
    out = jax.ops.segment_sum(y, ts, num_segments=T)
    return out.reshape(B, L, D)

def _layer(x, p, lw, conv_buf, lru_h, ml_c, ml_n, ml_m, k_past, v_past, prompt):
    (w_in, b_in, conv_w, conv_b, lru_wr, lru_br, lru_wi, lru_bi, lru_lambda, ml_norm_g,
     w_pa, w_pb, w_pc, w_out, ln1_g, ln1_b, router_w, router_b,
     exp_w1, exp_b1, exp_w2, exp_b2, ple_w, ple_gate_w, ple_gate_b, ln2_g, ln2_b) = lw
    B, L, _ = x.shape
    z = x @ w_in + b_in
    offs = [int(o) for o in np.cumsum(IN_WIDTHS)[:-1]]
    (a_x, a_g, sb_q, sb_k, sb_v, ml_q, ml_k, ml_v, ml_o, ml_i, ml_f, mg) = jnp.split(z, offs, axis=-1)

    ua, conv_new = _causal_conv(a_x, conv_buf, conv_w, conv_b)
    ha, lru_new = _rg_lru(ua, lru_h, lru_wr, lru_br, lru_wi, lru_bi, lru_lambda, prompt)
    ya = ha.astype(x.dtype) * jax.nn.gelu(a_g)

    q = sb_q.reshape(B, L, SB_HEADS, SB_HEAD_DIM) * (SB_HEAD_DIM ** -0.5)
    k = sb_k.reshape(B, L, SB_HEADS, SB_HEAD_DIM)
    v = sb_v.reshape(B, L, SB_HEADS, SB_HEAD_DIM)
    if prompt:
        yb = _sb_prompt(q, k, v)
    else:
        P = k_past.shape[1]
        pad = (-(P + L)) % KEY_BLOCK
        zpad = jnp.zeros((B, pad, SB_HEADS, SB_HEAD_DIM), k.dtype)
        k_all = jnp.concatenate([k_past.astype(k.dtype), k, zpad], axis=1)
        v_all = jnp.concatenate([v_past.astype(v.dtype), v, zpad], axis=1)
        yb = _stick_breaking(q, k_all, v_all, P + jnp.arange(L), jnp.arange(P + L + pad))
    yb = yb.reshape(B, L, SB_WIDTH)

    def heads(t, d):
        return t.reshape(B, L, ML_HEADS, d).transpose(0, 2, 1, 3).astype(F32)

    mq = heads(ml_q, ML_QK_DIM)
    mk = heads(ml_k, ML_QK_DIM) * (ML_QK_DIM ** -0.5)
    mv = heads(ml_v, ML_V_DIM)
    ig = ml_i.astype(F32).transpose(0, 2, 1)
    lf = jax.nn.log_sigmoid(ml_f.astype(F32)).transpose(0, 2, 1)
    if prompt:
        hc, (c_new, n_new, m_new) = _mlstm_prompt(mq, mk, mv, ig, lf)
    else:
        hc, (c_new, n_new, m_new) = _mlstm_block(mq, mk, mv, ig, lf, ml_c.astype(F32),
                                                 ml_n.astype(F32), ml_m.astype(F32))
    mu = jnp.mean(hc, axis=-1, keepdims=True)
    var = jnp.mean(jnp.square(hc - mu), axis=-1, keepdims=True)
    hc = ((hc - mu) * lax.rsqrt(var + LN_EPS)).transpose(0, 2, 1, 3).reshape(B, L, ML_V_WIDTH)
    yc = (hc * ml_norm_g.astype(F32)).astype(x.dtype) * jax.nn.sigmoid(ml_o)

    g = jax.nn.sigmoid(mg).reshape(B, L, N_BRANCH, D_MODEL)
    mixed = g[:, :, 0] * (ya @ w_pa) + g[:, :, 1] * (yb @ w_pb) + g[:, :, 2] * (yc @ w_pc)
    x = _layer_norm(DN_ALPHA * x + mixed @ w_out, ln1_g, ln1_b)

    f = _moe(x, router_w, router_b, exp_w1, exp_b1, exp_w2, exp_b2)
    ple = jax.nn.sigmoid(x @ ple_gate_w + ple_gate_b) * (p @ ple_w)
    x = _layer_norm(DN_ALPHA * x + f + ple, ln2_g, ln2_b)
    return x, (k, v, conv_new, lru_new, c_new, n_new, m_new)

def setup_inputs(seed: int = 0) -> dict:
    key = jax.random.key(seed)
    ks = iter(jax.random.split(key, 64))

    def nrm(shape, scale=1.0):
        return jax.random.normal(next(ks), shape, F32) * scale

    L = DEPTH
    x_prompt = nrm((BATCH, SEQ, D_MODEL))
    x_sample = nrm((DEC_BATCH, DEC_SEQ, D_MODEL))
    cache_sb_k = nrm((L, DEC_BATCH, PAST_LEN, SB_HEADS, SB_HEAD_DIM))
    cache_sb_v = nrm((L, DEC_BATCH, PAST_LEN, SB_HEADS, SB_HEAD_DIM))
    state_conv = nrm((L, DEC_BATCH, CONV_W - 1, D_RNN))
    state_lru = nrm((L, DEC_BATCH, D_RNN), 0.5)
    state_mlstm_c = nrm((L, DEC_BATCH, ML_HEADS, ML_QK_DIM, ML_V_DIM), 0.5)
    state_mlstm_n = nrm((L, DEC_BATCH, ML_HEADS, ML_QK_DIM), 0.5)
    state_mlstm_m = nrm((L, DEC_BATCH, ML_HEADS))
    p_prompt = nrm((L, BATCH, SEQ, D_PLE))
    p_sample = nrm((L, DEC_BATCH, DEC_SEQ, D_PLE))
    w_in = nrm((L, D_MODEL, N_IN), D_MODEL ** -0.5)
    b_in = nrm((L, N_IN), 0.01)
    b_in = b_in.at[:, F_GATE_OFF:F_GATE_OFF + ML_HEADS].add(jnp.linspace(3.0, 6.0, ML_HEADS))
    conv_w = nrm((L, CONV_W, D_RNN), CONV_W ** -0.5)
    conv_b = nrm((L, D_RNN), 0.01)
    lru_wr = nrm((L, N_LRU_BLOCKS, LRU_BLOCK, LRU_BLOCK), LRU_BLOCK ** -0.5)
    lru_br = nrm((L, D_RNN), 0.01)
    lru_wi = nrm((L, N_LRU_BLOCKS, LRU_BLOCK, LRU_BLOCK), LRU_BLOCK ** -0.5)
    lru_bi = nrm((L, D_RNN), 0.01)
    a_c = jax.random.uniform(next(ks), (L, D_RNN), F32, 0.9, 0.999)
    s = a_c ** (1.0 / LRU_C)
    lru_lambda = jnp.log(s) - jnp.log1p(-s)
    ml_norm_g = 1.0 + nrm((L, ML_V_WIDTH), 0.02)
    w_pa = nrm((L, D_RNN, D_MODEL), DN_BETA * D_RNN ** -0.5)
    w_pb = nrm((L, SB_WIDTH, D_MODEL), DN_BETA * SB_WIDTH ** -0.5)
    w_pc = nrm((L, ML_V_WIDTH, D_MODEL), DN_BETA * ML_V_WIDTH ** -0.5)
    w_out = nrm((L, D_MODEL, D_MODEL), DN_BETA * D_MODEL ** -0.5)
    ln1_g = 1.0 + nrm((L, D_MODEL), 0.02)
    ln1_b = nrm((L, D_MODEL), 0.01)
    router_w = nrm((L, D_MODEL, N_EXPERTS), D_MODEL ** -0.5)
    router_b = nrm((L, N_EXPERTS), 0.01)
    exp_w1 = nrm((L, N_EXPERTS, D_MODEL, 2 * D_FF), D_MODEL ** -0.5)
    exp_b1 = nrm((L, N_EXPERTS, 2 * D_FF), 0.01)
    exp_w2 = nrm((L, N_EXPERTS, D_FF, D_MODEL), DN_BETA * D_FF ** -0.5)
    exp_b2 = nrm((L, N_EXPERTS, D_MODEL), 0.01)
    ple_w = nrm((L, D_PLE, D_MODEL), DN_BETA * D_PLE ** -0.5)
    ple_gate_w = nrm((L, D_MODEL, D_MODEL), D_MODEL ** -0.5)
    ple_gate_b = nrm((L, D_MODEL), 0.01)
    ln2_g = 1.0 + nrm((L, D_MODEL), 0.02)
    ln2_b = nrm((L, D_MODEL), 0.01)
    return {'x_prompt': x_prompt, 'x_sample': x_sample, 'cache_sb_k': cache_sb_k, 'cache_sb_v': cache_sb_v,
            'state_conv': state_conv, 'state_lru': state_lru, 'state_mlstm_c': state_mlstm_c,
            'state_mlstm_n': state_mlstm_n, 'state_mlstm_m': state_mlstm_m,
            'p_prompt': p_prompt, 'p_sample': p_sample,
            'w_in': w_in, 'b_in': b_in, 'conv_w': conv_w, 'conv_b': conv_b,
            'lru_wr': lru_wr, 'lru_br': lru_br, 'lru_wi': lru_wi, 'lru_bi': lru_bi, 'lru_lambda': lru_lambda,
            'ml_norm_g': ml_norm_g, 'w_pa': w_pa, 'w_pb': w_pb, 'w_pc': w_pc, 'w_out': w_out,
            'ln1_g': ln1_g, 'ln1_b': ln1_b, 'router_w': router_w, 'router_b': router_b,
            'exp_w1': exp_w1, 'exp_b1': exp_b1, 'exp_w2': exp_w2, 'exp_b2': exp_b2,
            'ple_w': ple_w, 'ple_gate_w': ple_gate_w, 'ple_gate_b': ple_gate_b,
            'ln2_g': ln2_g, 'ln2_b': ln2_b}

def reference(x_prompt, x_sample, cache_sb_k, cache_sb_v, state_conv, state_lru,
              state_mlstm_c, state_mlstm_n, state_mlstm_m, p_prompt, p_sample,
              w_in, b_in, conv_w, conv_b, lru_wr, lru_br, lru_wi, lru_bi, lru_lambda,
              ml_norm_g, w_pa, w_pb, w_pc, w_out, ln1_g, ln1_b, router_w, router_b,
              exp_w1, exp_b1, exp_w2, exp_b2, ple_w, ple_gate_w, ple_gate_b, ln2_g, ln2_b):
    B = x_prompt.shape[0]
    y_prompt = x_prompt
    y_sample = x_sample
    st_p = []
    st_s = []
    for i in range(DEPTH):
        lw = (w_in[i], b_in[i], conv_w[i], conv_b[i], lru_wr[i], lru_br[i], lru_wi[i], lru_bi[i],
              lru_lambda[i], ml_norm_g[i], w_pa[i], w_pb[i], w_pc[i], w_out[i], ln1_g[i], ln1_b[i],
              router_w[i], router_b[i], exp_w1[i], exp_b1[i], exp_w2[i], exp_b2[i],
              ple_w[i], ple_gate_w[i], ple_gate_b[i], ln2_g[i], ln2_b[i])
        y_prompt, sp = _layer(y_prompt, p_prompt[i], lw,
                              jnp.zeros((B, CONV_W - 1, D_RNN), x_prompt.dtype),
                              jnp.zeros((B, D_RNN), F32),
                              jnp.zeros((B, ML_HEADS, ML_QK_DIM, ML_V_DIM), F32),
                              jnp.zeros((B, ML_HEADS, ML_QK_DIM), F32),
                              jnp.zeros((B, ML_HEADS), F32), None, None, True)
        y_sample, ss = _layer(y_sample, p_sample[i], lw, state_conv[i], state_lru[i],
                              state_mlstm_c[i], state_mlstm_n[i], state_mlstm_m[i],
                              cache_sb_k[i], cache_sb_v[i], False)
        st_p.append(sp)
        st_s.append(ss)
    k_p, v_p, conv_p, lru_p, c_p, n_p, m_p = [jnp.stack(s) for s in zip(*st_p)]
    k_s, v_s, conv_s, lru_s, c_s, n_s, m_s = [jnp.stack(s) for s in zip(*st_s)]
    return (y_prompt, y_sample, k_p, v_p, conv_p, lru_p, c_p, n_p, m_p,
            k_s, v_s, conv_s, lru_s, c_s, n_s, m_s)


_drawn_inputs = setup_inputs


def setup_inputs(seed=0):
    import zlib

    import numpy as np

    out = dict(_drawn_inputs(seed))
    spreads = {}
    factors = {'cache_sb_k': 3.199,
     'lru_br': 23.885,
     'lru_bi': 8.0,
     'ml_norm_g': 8.0,
     'ln1_b': 2.914,
     'router_b': 2.97,
     'exp_b1': 8.0,
     'exp_b2': 8.0,
     'ple_gate_b': 59.279,
     'ln2_g': 7.166,
     'ln2_b': 14.572}
    for name, (base, spread) in spreads.items():
        noise = np.random.default_rng([zlib.crc32(name.encode()), seed]).standard_normal(out[name].shape)
        drawn = base * np.exp(spread * noise) if base else spread * noise
        out[name] = __import__('jax').numpy.asarray(drawn.astype(out[name].dtype))
    for name, factor in factors.items():
        out[name] = (out[name] * factor).astype(out[name].dtype)
    return out
```

```python
from contextlib import ExitStack, contextmanager

import numpy as np

import concourse.bass as bass
from concourse import mybir

F32 = mybir.dt.float32
I32 = mybir.dt.int32
U32 = mybir.dt.uint32
F32R = mybir.dt.float32r
ALU = mybir.AluOpType
ACT = mybir.ActivationFunctionType
AX_X = mybir.AxisListType.X

P = 128
D = 1024
DT = D // P
TP = 1024
NB, LS = 8, 16
TS = NB * LS
T = TP + TS
NT = T // P
CHUNKS = ((0, 512), (512, 1024), (1024, T))
CW = 4
H = 4
HD = 128
QD = 64
PAST = 1024
KB = PAST // P
NE, TOPK, FF = 32, 4, 512
FT = FF // P
PLE = 256
ALPHA = 2.0 ** 0.25
LN_EPS = 1e-5
NEG = -1e30
SB_SCALE = float(HD) ** -0.5
ML_SCALE = float(QD) ** -0.5
O_AX, O_AG, O_SQ, O_SK, O_SV, O_MQ, O_MK, O_MV, O_MO, O_MI, O_MF, O_MG = (
    0, 1024, 2048, 2560, 3072, 3584, 3840, 4096, 4608, 5120, 5124, 5128)
V_BIN, V_BMG, V_CW, V_CB, V_BR, V_BI, V_LAM = 0, 40, 64, 96, 104, 112, 120
SLOTS = 192
NSLOT = T * TOPK + NE * SLOTS
MAXBLK = NSLOT // SLOTS
NBLK = MAXBLK + 2


class Shared:
    pass


@contextmanager
def stage_semaphores(nc):
    owned = []

    def sem(name):
        owned.append(nc.alloc_semaphore(name))
        return owned[-1]

    yield sem
    nc.clear_and_free_semaphores(owned)
    nc.all_engine_barrier()


def banks(nc, ctx):
    return [ctx.enter_context(nc.psum_tensor(f"bank{i}", [P, 512], F32)) for i in range(8)]


def stage_constants(nc, g):
    with ExitStack() as ctx:
        sem = ctx.enter_context(stage_semaphores(nc))
        rows = ctx.enter_context(nc.sbuf_tensor("vector_rows", [P, P], F32))
        state_rows = ctx.enter_context(nc.sbuf_tensor("state_rows", [32, D], F32))
        sp_e = ctx.enter_context(nc.sbuf_tensor("lambda_exp", [P, DT], F32))
        ident_ready = sem("c_ident_ready")
        filled = sem("c_filled")
        masks = sem("c_masks")
        rows_in = sem("c_rows_in")
        turned = sem("c_turned")
        copied = sem("c_copied")
        lam_abs = sem("c_lam_abs")
        lam_exp = sem("c_lam_exp")
        lam_ln = sem("c_lam_ln")
        lam_sp = sem("c_lam_sp")
        block = ctx.enter_context(nc.Block())
        loads = [
            (rows[V_BIN:V_BIN + 40, :], g.b_in[0, 0:5120].rearrange("(r p) -> r p", p=P)),
            (rows[V_BMG:V_BMG + 24, :], g.b_in[0, O_MG:O_MG + 3072].rearrange("(r p) -> r p", p=P)),
            (rows[V_CW:V_CW + 32, :], g.conv_w[0].rearrange("j (r p) -> (j r) p", p=P)),
            (rows[V_CB:V_CB + 8, :], g.conv_b[0].rearrange("(r p) -> r p", p=P)),
            (rows[V_BR:V_BR + 8, :], g.lru_br[0].rearrange("(r p) -> r p", p=P)),
            (rows[V_BI:V_BI + 8, :], g.lru_bi[0].rearrange("(r p) -> r p", p=P)),
            (rows[V_LAM:V_LAM + 8, :], g.lru_lambda[0].rearrange("(r p) -> r p", p=P)),
            (state_rows[0:24, :], g.state_conv[0].rearrange("b j d -> (b j) d")),
            (state_rows[24:32, :], g.state_lru[0]),
        ]

        @block.sync
        def _(sp):
            for dst, src in loads:
                sp.dma_start(dst, src).then_inc(rows_in, 16)

        @block.gpsimd
        def _(pool):
            fills = ((g.ident, 0.0), (g.tri_neg, -1.0), (g.ones, 1.0), (g.neg_ones, -1.0),
                     (g.strict, 1.0), (g.strict_s, 1.0), (g.causal, 0.0), (g.causal_s, 0.0),
                     (g.tri_before, 1.0), (g.eps, LN_EPS))
            for tile, value in fills:
                pool.memset(tile[:], value).then_inc(filled, 1)
            pool.memset(g.sel[:], 0.0).then_inc(filled, 1)
            pool.wait_ge(filled, len(fills) + 1)
            pool.affine_select(out=g.ident[:], in_=g.ident[:], compare_op=ALU.not_equal, fill=1.0,
                               base=0, pattern=[[-1, P]], channel_multiplier=1).then_inc(ident_ready, 1)
            pool.affine_select(out=g.tri_neg[:], in_=g.tri_neg[:], compare_op=ALU.is_ge, fill=0.0,
                               base=0, pattern=[[-1, P]], channel_multiplier=1)
            pool.affine_select(out=g.tri_before[:], in_=g.tri_before[:], compare_op=ALU.is_ge, fill=0.0,
                               base=-1, pattern=[[1, P]], channel_multiplier=-1)
            pool.affine_select(out=g.strict[:], in_=g.strict[:], compare_op=ALU.is_ge, fill=0.0,
                               base=-1, pattern=[[1, P]], channel_multiplier=-1)
            pool.affine_select(out=g.strict_s[:], in_=g.strict_s[:], compare_op=ALU.is_ge, fill=0.0,
                               base=-1, pattern=[[1, P]], channel_multiplier=-1).then_inc(masks, 1)
            pool.affine_select(out=g.causal[:], in_=g.causal[:], compare_op=ALU.is_ge, fill=NEG,
                               base=0, pattern=[[1, P]], channel_multiplier=-1)
            pool.affine_select(out=g.causal_s[:], in_=g.causal_s[:], compare_op=ALU.is_ge, fill=NEG,
                               base=0, pattern=[[1, P]], channel_multiplier=-1).then_inc(masks, 1)
            pool.affine_select(out=g.sel[:], in_=g.sel[:], compare_op=ALU.not_equal, fill=1.0,
                               base=0, pattern=[[-1, H], [0, P]], channel_multiplier=1)
            pool.wait_ge(masks, 2)
            for tile, fill in ((g.strict_s, 0.0), (g.causal_s, NEG)):
                view = tile[:].rearrange("s (b t) -> s b t", t=LS)
                pool.affine_select(out=view, in_=view, compare_op=ALU.is_ge, fill=fill, base=0,
                                   pattern=[[-LS, NB], [0, LS]], channel_multiplier=1)

        @block.tensor
        def _(pe):
            pe.wait_ge(ident_ready, 1)
            pe.wait_ge(rows_in, 16 * len(loads))
            nc.tensor.transpose(g.bank[0][:, 0:P], rows[:], g.ident[:]).then_inc(turned, 1)
            for m in range(DT):
                last = nc.tensor.transpose(g.bank[1][:, m * 32:(m + 1) * 32],
                                           state_rows[:, m * P:(m + 1) * P], g.ident[0:32, 0:32])
            last.then_inc(turned, 1)

        @block.vector
        def _(dve):
            dve.wait_ge(turned, 2)
            nc.vector.tensor_copy(g.vec[:], g.bank[0][:, 0:P]).then_inc(copied, 1)
            nc.vector.tensor_copy(g.state[:], g.bank[1][:, 0:DT * 32].rearrange("p (m r) -> p m r", m=DT)
                                  ).then_inc(copied, 1)
            dve.wait_ge(copied, 2)
            lam = g.vec[:, V_LAM:V_LAM + DT]
            nc.vector.tensor_scalar(sp_e[:], lam, -1.0, None, ALU.mult).then_inc(lam_abs, 1)
            dve.wait_ge(lam_abs, 1)
            nc.vector.tensor_tensor(sp_e[:], sp_e[:], lam, ALU.max).then_inc(lam_abs, 1)
            nc.vector.tensor_scalar(g.coef[:], lam, 0.0, None, ALU.min).then_inc(lam_sp, 1)
            nc.vector.tensor_scalar(g.qbias[:], g.vec[:, O_SQ // P:O_SQ // P + H], SB_SCALE, None, ALU.mult)
            nc.vector.tensor_scalar(g.mkbias[:], g.vec[:, O_MK // P:O_MK // P + 2], ML_SCALE, None, ALU.mult)
            nc.vector.tensor_scalar(g.half_b[:], g.vec[:, V_BR:V_BR + 2 * DT], 0.5, None, ALU.mult)
            dve.wait_ge(lam_ln, 1)
            dve.wait_ge(lam_sp, 1)
            nc.vector.tensor_tensor(g.coef[:], g.coef[:], sp_e[:], ALU.subtract).then_inc(lam_sp, 1)
            dve.wait_ge(lam_sp, 2)
            nc.vector.tensor_scalar(g.coef[:], g.coef[:], 4.0, None, ALU.mult)

        @block.scalar
        def _(act):
            act.wait_ge(lam_abs, 2)
            nc.scalar.activation(sp_e[:], sp_e[:], ACT.Exp, scale=-1.0).then_inc(lam_exp, 1)
            act.wait_ge(lam_exp, 1)
            nc.scalar.activation(sp_e[:], sp_e[:], ACT.Ln, bias=1.0).then_inc(lam_ln, 1)


def stage_transpose_x(nc, g, xT):
    with ExitStack() as ctx:
        sem = ctx.enter_context(stage_semaphores(nc))
        x = ctx.enter_context(nc.sbuf_tensor("x_tokens", [P, NT, D], F32))
        x_in = [sem(f"x_in{i}") for i in range(3)]
        turned = sem("x_turned")
        moved = [sem("x_moved_act"), sem("x_moved_dve")]
        block = ctx.enter_context(nc.Block())
        units = [(i, q) for i in range(NT) for q in range(2)]

        @block.sync
        def _(sp):
            xp = g.x_prompt[0].rearrange("(i p) d -> p i d", p=P)
            sp.dma_start(x[:, 0:4, :], xp[:, 0:4, :]).then_inc(x_in[0], 16)
            sp.dma_start(x[:, 4:8, :], xp[:, 4:8, :]).then_inc(x_in[1], 16)
            sp.dma_start(x[:, 8, :], g.x_sample.rearrange("b t d -> (b t) d")).then_inc(x_in[2], 16)

        @block.tensor
        def _(pe):
            for n, (i, q) in enumerate(units):
                pe.wait_ge(x_in[i // 4], 16)
                if n >= 8:
                    pe.wait_ge(moved[n % 2], (n - 8) // 2 + 1)
                for k in range(4):
                    last = nc.tensor.transpose(g.bank[n % 8][:, k * P:(k + 1) * P],
                                               x[:, i, (4 * q + k) * P:(4 * q + k + 1) * P], g.ident[:])
                last.then_inc(turned, 1)

        def move(eng, copy, parity):
            for n, (i, q) in enumerate(units):
                if n % 2 == parity:
                    eng.wait_ge(turned, n + 1)
                    copy(xT[:, 4 * q:4 * q + 4, i * P:(i + 1) * P],
                         g.bank[n % 8][:].rearrange("p (k t) -> p k t", k=4)).then_inc(moved[parity], 1)

        @block.scalar
        def _(act):
            move(act, nc.scalar.copy, 0)

        @block.vector
        def _(dve):
            move(dve, nc.vector.tensor_copy, 1)


def stage_lru(nc, g, xT):
    with ExitStack() as ctx:
        sem = ctx.enter_context(stage_semaphores(nc))
        def sb(name, shape):
            return ctx.enter_context(nc.sbuf_tensor(name, shape, F32))

        GRP = 256
        wx = sb("w_ax", [P, 2, DT, GRP])
        wg = sb("w_ag", [P, 2, DT, GRP])
        gate_w = sb("lru_gate_w", [P, DT, 2, P])
        ext_p = sb("ext_prompt", [P, DT, CW - 1 + TP])
        ext_s = sb("ext_sample", [P, DT, NB, CW - 1 + LS])
        ua = sb("ua", [P, 2, T])
        gl = sb("gelu_gate", [P, 2, T])
        tr = sb("tanh_r", [P, T])
        ti = sb("tanh_i", [P, T])
        aa = sb("decay", [P, T])
        th = sb("tanh_log_a", [P, T])
        mu = sb("input_scale", [P, T])
        hh = sb("lru_h", [P, 2, T])
        pack = sb("state_pack", [P, DT, 36])
        outrow = sb("state_out_rows", [36, D])
        tmp8 = sb("start_terms", [P, NB])
        w_in_x = [sem(f"a_wx{i}") for i in range(4)]
        w_in_g = [sem(f"a_wg{i}") for i in range(4)]
        zeroed = sem("a_zeroed")
        gate_in = sem("a_gate_in")
        ax_ready = sem("a_ax_ready")
        ax_moved = sem("a_ax_moved")
        ag_ready = sem("a_ag_ready")
        ag_moved = sem("a_ag_moved")
        states_in = sem("a_states_in")
        conv_step = sem("a_conv_step")
        ua_ready = sem("a_ua_ready")
        ri_ready = sem("a_ri_ready")
        ri_moved = sem("a_ri_moved")
        a_ready = sem("a_decay_ready")
        square_ready = sem("a_square_ready")
        mult_ready = sem("a_mult_ready")
        bx_step = sem("a_bx_step")
        h_ready = sem("a_h_ready")
        ya_ready = sem("a_ya_ready")
        ya_out = [sem("a_ya_out0"), sem("a_ya_out1")]
        packed = sem("a_packed")
        pack_turned = sem("a_pack_turned")
        rows_ready = sem("a_rows_ready")
        states_out = sem("a_states_out")
        block = ctx.enter_context(nc.Block())
        w_in_t = g.w_in[0].rearrange("(k p) n -> p k n", p=P)

        @block.sync
        def _(sp):
            for q in range(4):
                if q >= 2:
                    sp.wait_ge(ax_ready, 2 * (q - 1))
                sp.dma_start(wx[:, q % 2], w_in_t[:, :, O_AX + q * GRP:O_AX + (q + 1) * GRP]).then_inc(w_in_x[q], 16)
                if q >= 2:
                    sp.wait_ge(ag_ready, 2 * (q - 1))
                sp.dma_start(wg[:, q % 2], w_in_t[:, :, O_AG + q * GRP:O_AG + (q + 1) * GRP]).then_inc(w_in_g[q], 16)
            for m in range(DT):
                sp.wait_ge(ya_ready, m + 1)
                sp.dma_start(g.yaT_d[m], hh[:, m % 2]).then_inc(ya_out[m % 2], 16)
            sp.wait_ge(rows_ready, 2)
            sp.dma_start(g.o_conv_p[0, 0], outrow[0:3, :]).then_inc(states_out, 16)
            sp.dma_start(g.o_conv_s[0].rearrange("b j d -> (b j) d"), outrow[3:27, :]).then_inc(states_out, 16)
            sp.dma_start(g.o_lru_p[0], outrow[27:28, :]).then_inc(states_out, 16)
            sp.dma_start(g.o_lru_s[0], outrow[28:36, :]).then_inc(states_out, 16)
            for s in ya_out:
                sp.wait_ge(s, 16 * DT // 2)
            sp.wait_ge(states_out, 64)

        @block.gpsimd
        def _(pool):
            pool.memset(gate_w[:], 0.0).then_inc(zeroed, 1)
            pool.memset(ext_p[:, :, 0:CW - 1], 0.0).then_inc(states_in, 1)
            pool.tensor_copy(ext_s[:, :, :, 0:CW - 1],
                             g.state[:, :, 0:24].rearrange("p m (b j) -> p m b j", b=NB)).then_inc(states_in, 1)
            pool.wait_ge(zeroed, 1)
            for r, w in enumerate((g.lru_wr, g.lru_wi)):
                pairs = w[0].rearrange("(m two) c d -> two c m d", two=2)
                for half in range(2):
                    lo = half * 64
                    pool.dma_start(gate_w[lo:lo + 64, :, r, lo:lo + 64], pairs[half]).then_inc(gate_in, 16)

        @block.tensor
        def _(pe):
            def project(w, bank0):
                for k in range(DT):
                    for c, (lo, hi) in enumerate(CHUNKS):
                        last = nc.tensor.matmul(g.bank[bank0 + c][:, 0:hi - lo], w[:, k, :], xT[:, k, lo:hi],
                                                start=(k == 0), stop=(k == DT - 1))
                return last

            def gates(m):
                pe.wait_ge(ua_ready, m + 1)
                for c, (lo, hi) in enumerate(CHUNKS):
                    if m or c:
                        pe.wait_ge(ri_moved, 3 * m + c)
                    nc.tensor.matmul(g.bank[6][:, 0:hi - lo], gate_w[:, m, 0, :], ua[:, m % 2, lo:hi],
                                     start=True, stop=True)
                    nc.tensor.matmul(g.bank[7][:, 0:hi - lo], gate_w[:, m, 1, :], ua[:, m % 2, lo:hi],
                                     start=True, stop=True).then_inc(ri_ready, 1)

            for m in range(DT):
                off = (m % 2) * P
                pe.wait_ge(w_in_x[m // 2], 16)
                if m:
                    pe.wait_ge(ax_moved, m)
                project(wx[:, m // 2 % 2, :, off:off + P], 0).then_inc(ax_ready, 1)
                if m == 1:
                    pe.wait_ge(gate_in, 64)
                if m:
                    gates(m - 1)
                pe.wait_ge(w_in_g[m // 2], 16)
                if m:
                    pe.wait_ge(ag_moved, m)
                project(wg[:, m // 2 % 2, :, off:off + P], 3).then_inc(ag_ready, 1)
            gates(DT - 1)
            pe.wait_ge(packed, DT + 2)
            pe.wait_ge(ri_moved, 3 * DT)
            for half in range(2):
                for k in range(4):
                    last = nc.tensor.transpose(g.bank[6 + half][0:36, k * P:(k + 1) * P],
                                               pack[:, 4 * half + k, :], g.ident[:])
                last.then_inc(pack_turned, 1)

        @block.scalar
        def _(act):
            def lru_gates(m):
                for c, (lo, hi) in enumerate(CHUNKS):
                    act.wait_ge(ri_ready, 3 * m + c + 1)
                    if m and c == 0:
                        act.wait_ge(h_ready, m)
                    nc.scalar.activation(tr[:, lo:hi], g.bank[6][:, 0:hi - lo], ACT.Tanh,
                                         bias=g.half_b[:, m:m + 1], scale=0.5)
                    nc.scalar.activation(ti[:, lo:hi], g.bank[7][:, 0:hi - lo], ACT.Tanh,
                                         bias=g.half_b[:, DT + m:DT + m + 1], scale=0.5).then_inc(ri_moved, 1)
                act.wait_ge(ri_moved, 3 * m + 3)
                nc.scalar.activation(aa[:], tr[:], ACT.Exp, bias=g.coef[:, m:m + 1], scale=g.coef[:, m:m + 1])
                nc.scalar.activation(th[:], tr[:], ACT.Tanh, bias=g.coef[:, m:m + 1],
                                     scale=g.coef[:, m:m + 1]).then_inc(a_ready, 1)
                act.wait_ge(square_ready, 2 * m + 2)
                nc.scalar.activation(mu[:], mu[:], ACT.Sqrt, scale=-1.0).then_inc(mult_ready, 1)

            for m in range(DT):
                act.wait_ge(ax_ready, m + 1)
                bias = g.vec[:, V_BIN + m:V_BIN + m + 1]
                nc.scalar.activation(ext_p[:, m, 3:3 + 512], g.bank[0][:], ACT.Identity, bias=bias)
                nc.scalar.activation(ext_p[:, m, 3 + 512:3 + 1024], g.bank[1][:], ACT.Identity, bias=bias)
                nc.scalar.activation(ext_s[:, m, :, 3:], g.bank[2][:, 0:TS].rearrange("p (b t) -> p b t", b=NB),
                                     ACT.Identity, bias=bias).then_inc(ax_moved, 1)
                if m:
                    lru_gates(m - 1)
                act.wait_ge(ag_ready, m + 1)
                if m >= 2:
                    act.wait_ge(ya_ready, m - 1)
                bias = g.vec[:, 8 + m:9 + m]
                for c, (lo, hi) in enumerate(CHUNKS):
                    last = nc.scalar.activation(gl[:, m % 2, lo:hi], g.bank[3 + c][:, 0:hi - lo],
                                                ACT.Gelu_apprx_tanh, bias=bias)
                last.then_inc(ag_moved, 1)
            lru_gates(DT - 1)

        @block.vector
        def _(dve):
            def conv(m):
                dve.wait_ge(ax_moved, m + 1)
                if m == 0:
                    dve.wait_ge(states_in, 2)
                for j in range(CW):
                    w = g.vec[:, V_CW + j * DT + m:V_CW + j * DT + m + 1]
                    up = ua[:, m % 2, 0:TP]
                    us = ua[:, m % 2, TP:T].rearrange("p (b t) -> p b t", b=NB)
                    ep, es = ext_p[:, m, j:j + TP], ext_s[:, m, :, j:j + LS]
                    if j == 0:
                        cb = g.vec[:, V_CB + m:V_CB + m + 1]
                        nc.vector.tensor_scalar(up, ep, w, cb, ALU.mult, ALU.add)
                        last = nc.vector.tensor_scalar(us, es, w, cb, ALU.mult, ALU.add)
                    else:
                        dve.wait_ge(conv_step, 3 * m + j)
                        nc.vector.scalar_tensor_tensor(out=up, in0=ep, scalar=w, in1=up, op0=ALU.mult, op1=ALU.add)
                        last = nc.vector.scalar_tensor_tensor(out=us, in0=es, scalar=w, in1=us,
                                                              op0=ALU.mult, op1=ALU.add)
                    last.then_inc(conv_step if j < CW - 1 else ua_ready, 1)

            def scan(m):
                s = m % 2
                starts = slice(TP, T, LS)
                dve.wait_ge(a_ready, m + 1)
                nc.vector.tensor_tensor(mu[:], aa[:], aa[:], ALU.mult).then_inc(square_ready, 1)
                dve.wait_ge(ua_ready, m + 1)
                nc.vector.scalar_tensor_tensor(out=ti[:], in0=ti[:], scalar=1.0, in1=ua[:, s], op0=ALU.add,
                                               op1=ALU.mult).then_inc(bx_step, 1)
                nc.vector.tensor_tensor(tmp8[:], aa[:, starts], g.state[:, m, 24:32], ALU.mult).then_inc(bx_step, 1)
                dve.wait_ge(square_ready, 2 * m + 1)
                nc.vector.scalar_tensor_tensor(out=mu[:], in0=mu[:], scalar=1.0, in1=th[:], op0=ALU.add,
                                               op1=ALU.mult).then_inc(square_ready, 1)
                dve.wait_ge(bx_step, 6 * m + 2)
                nc.vector.memset(aa[:, starts], 0.0).then_inc(bx_step, 1)
                dve.wait_ge(mult_ready, m + 1)
                nc.vector.memset(mu[:, 0:1], 1.0).then_inc(bx_step, 1)
                dve.wait_ge(bx_step, 6 * m + 4)
                nc.vector.scalar_tensor_tensor(out=ti[:], in0=ti[:], scalar=0.5, in1=mu[:], op0=ALU.mult,
                                               op1=ALU.mult).then_inc(bx_step, 1)
                dve.wait_ge(bx_step, 6 * m + 5)
                nc.vector.tensor_tensor(ti[:, starts], ti[:, starts], tmp8[:], ALU.add).then_inc(bx_step, 1)
                dve.wait_ge(bx_step, 6 * m + 6)
                if m >= 2:
                    dve.wait_ge(ya_out[s], 16 * (m // 2))
                nc.vector.tensor_tensor_scan(hh[:, s], aa[:], ti[:], 0.0, ALU.mult, ALU.add).then_inc(h_ready, 1)
                dve.wait_ge(h_ready, m + 1)
                nc.vector.tensor_copy(pack[:, m, 27:28], hh[:, s, TP - 1:TP])
                nc.vector.tensor_copy(pack[:, m, 28:36], hh[:, s, TP + LS - 1:T:LS]).then_inc(packed, 1)
                dve.wait_ge(ag_moved, m + 1)
                dve.wait_ge(packed, m + 1)
                nc.vector.tensor_tensor(hh[:, s], hh[:, s], gl[:, s], ALU.mult).then_inc(ya_ready, 1)

            for m in range(DT):
                if m >= 2:
                    dve.wait_ge(ri_ready, 3 * (m - 1))
                conv(m)
                if m:
                    scan(m - 1)
            scan(DT - 1)
            nc.vector.tensor_copy(pack[:, :, 0:3], ext_p[:, :, TP:TP + 3]).then_inc(packed, 1)
            nc.vector.tensor_copy(pack[:, :, 3:27].rearrange("p m (b j) -> p m b j", b=NB),
                                  ext_s[:, :, :, LS:LS + 3]).then_inc(packed, 1)
            for half in range(2):
                dve.wait_ge(pack_turned, half + 1)
                nc.vector.tensor_copy(outrow[:, half * 512:(half + 1) * 512],
                                      g.bank[6 + half][0:36, :]).then_inc(rows_ready, 1)


def stage_sb_project(nc, g, xT, qT, kT, v_tok):
    with ExitStack() as ctx:
        sem = ctx.enter_context(stage_semaphores(nc))
        def sb(name, shape):
            return ctx.enter_context(nc.sbuf_tensor(name, shape, F32))

        w = sb("w_sb", [P, 3, DT, 512])
        bias = sb("kv_bias", [P, 2, 512])
        k_tok = sb("k_tok", [P, 2, 512])
        w_loaded = [sem(f"b_w{i}") for i in range(3)]
        bias_in = sem("b_bias_in")
        prod = sem("b_prod")
        kv_moved = sem("b_kv_moved")
        q_moved = sem("b_q_moved")
        k_turned = sem("b_k_turned")
        kT_moved = sem("b_kT_moved")
        k_out = [sem("b_k_out0"), sem("b_k_out1")]
        v_out = sem("b_v_out")
        block = ctx.enter_context(nc.Block())
        w_in_t = g.w_in[0].rearrange("(k p) n -> p k n", p=P)
        NBK = 6

        @block.sync
        def _(sp):
            for s, off in enumerate((O_SK, O_SV, O_SQ)):
                sp.dma_start(w[:, s], w_in_t[:, :, off:off + 512]).then_inc(w_loaded[s], 16)
                if s == 0:
                    sp.dma_start(bias[:].rearrange("p a n -> p (a n)"),
                                 g.b_in[0:1, O_SK:O_SK + 1024].broadcast_to([P, 1024])).then_inc(bias_in, 16)
            kp, vp = (t[0, 0].rearrange("(i p) h d -> i p (h d)", p=P) for t in (g.o_k_p, g.o_v_p))
            ks, vs = (t[0].rearrange("b t h d -> (b t) (h d)") for t in (g.o_k_s, g.o_v_s))
            for i in range(NT):
                sp.wait_ge(kv_moved, 2 * i + 1)
                sp.dma_start(kp[i] if i < NT - 1 else ks, k_tok[:, i % 2, :]).then_inc(k_out[i % 2], 16)
                sp.wait_ge(kv_moved, 2 * i + 2)
                sp.dma_start(vp[i] if i < NT - 1 else vs, v_tok[:, i, :]).then_inc(v_out, 16)
            sp.wait_ge(k_out[0], 16 * 5)
            sp.wait_ge(k_out[1], 16 * 4)
            sp.wait_ge(v_out, 16 * NT)

        @block.tensor
        def _(pe):
            def turn_k(i):
                pe.wait_ge(kv_moved, 2 * i + 1)
                if i >= 2:
                    pe.wait_ge(kT_moved, i - 1)
                for h in range(H):
                    last = nc.tensor.transpose(g.bank[6 + i % 2][:, h * P:(h + 1) * P],
                                               k_tok[:, i % 2, h * P:(h + 1) * P], g.ident[:])
                last.then_inc(k_turned, 1)

            n = 0
            for i in range(NT):
                for s in range(2):
                    pe.wait_ge(w_loaded[s], 16)
                    if n >= NBK:
                        pe.wait_ge(kv_moved, n - NBK + 1)
                    for k in range(DT):
                        last = nc.tensor.matmul(g.bank[n % NBK][:], xT[:, k, i * P:(i + 1) * P], w[:, s, k, :],
                                                start=(k == 0), stop=(k == DT - 1))
                    last.then_inc(prod, 1)
                    n += 1
                if i:
                    turn_k(i - 1)
            pe.wait_ge(w_loaded[2], 16)
            for h in range(H):
                for lo, hi in CHUNKS:
                    if n - NBK < 2 * NT:
                        pe.wait_ge(kv_moved, n - NBK + 1)
                    else:
                        pe.wait_ge(q_moved, n - NBK + 1 - 2 * NT)
                    for k in range(DT):
                        last = nc.tensor.matmul(g.bank[n % NBK][:, 0:hi - lo], w[:, 2, k, h * P:(h + 1) * P],
                                                xT[:, k, lo:hi], start=(k == 0), stop=(k == DT - 1))
                    last.then_inc(prod, 1)
                    n += 1
                if h == 0:
                    turn_k(NT - 1)

        @block.vector
        def _(dve):
            dve.wait_ge(bias_in, 16)
            for n in range(2 * NT):
                i, s = divmod(n, 2)
                dve.wait_ge(prod, n + 1)
                if s == 0 and i >= 2:
                    dve.wait_ge(k_turned, i - 1)
                    dve.wait_ge(k_out[i % 2], 16 * (i // 2))
                out = v_tok[:, i, :] if s else k_tok[:, i % 2, :]
                nc.vector.tensor_tensor(out, g.bank[n % NBK][:], bias[:, s, :], ALU.add).then_inc(kv_moved, 1)

        @block.scalar
        def _(act):
            def move_kT(i):
                act.wait_ge(k_turned, i + 1)
                nc.scalar.copy(kT[:, :, i * P:(i + 1) * P],
                               g.bank[6 + i % 2][:].rearrange("p (h t) -> p h t", h=H)).then_inc(kT_moved, 1)

            for i in range(NT - 1):
                move_kT(i)
            n = 2 * NT
            for h in range(H):
                for lo, hi in CHUNKS:
                    act.wait_ge(prod, n + 1)
                    nc.scalar.activation(qT[:, h, lo:hi], g.bank[n % NBK][:, 0:hi - lo], ACT.Identity,
                                         bias=g.qbias[:, h:h + 1], scale=SB_SCALE).then_inc(q_moved, 1)
                    n += 1
            move_kT(NT - 1)


def stage_sb_prompt(nc, g, qT, kT, v_tok):
    units = []
    for h in range(H):
        for c in range(2):
            blocks = list(range(4 * c + 3, -1, -1))
            for j in blocks:
                units.append((h, 2 * h + c, c, j, max(j * P - 512 * c, 0), j == blocks[0], j == 0))
    N = len(units)
    NZ, RING = 5, 4
    with ExitStack() as ctx:
        sem = ctx.enter_context(stage_semaphores(nc))
        def sb(name, shape):
            return ctx.enter_context(nc.sbuf_tensor(name, shape, F32))

        e = sb("softplus_work", [P, RING, 512])
        u = sb("softplus", [P, RING, 512])
        acc = sb("later_keys_sum", [P, 3, 512])
        w = sb("sb_weights", [P, RING, 512])
        z_ready = sem("p_z_ready")
        abs_ready = sem("p_abs_ready")
        exp_ready = sem("p_exp_ready")
        ln_ready = sem("p_ln_ready")
        u_step = sem("p_u_step")
        u_ready = sem("p_u_ready")
        s_ready = sem("p_s_ready")
        acc_ready = sem("p_acc_ready")
        w_ready = sem("p_w_ready")
        w_masked = sem("p_w_masked")
        pv_done = sem("p_pv_done")
        y_moved = sem("p_y_moved")
        block = ctx.enter_context(nc.Block())

        def diagonal(n):
            return units[n][3] >= 4 * units[n][2]

        def diagonals(n):
            return sum(diagonal(m) for m in range(n))

        def zb(n, lo=0):
            return g.bank[n % NZ][:, lo:512]

        @block.tensor
        def _(pe):
            def z(n):
                h, chain, c, j, off, first, last = units[n]
                if n >= NZ:
                    pe.wait_ge(w_ready, n - NZ + 1)
                nc.tensor.matmul(zb(n, off), kT[:, h, j * P:(j + 1) * P], qT[:, h, 512 * c + off:512 * c + 512],
                                 start=True, stop=True, skip_group_check=True).then_inc(z_ready, 1)

            def s(n):
                h, chain, c, j, off, first, last = units[n]
                pe.wait_ge(u_ready, n + 1)
                ins = nc.tensor.matmul(zb(n, off), g.tri_neg[:], u[:, n % RING, off:512], start=False, stop=True,
                                       skip_group_check=True)
                if not first:
                    pe.wait_ge(acc_ready, n)
                    off_before = units[n - 1][4]
                    ins = nc.tensor.matmul(zb(n, off_before), g.neg_ones[:], acc[:, (n - 1) % 3, off_before:512],
                                           start=False, stop=True, skip_group_check=True)
                ins.then_inc(s_ready, 1)

            def pv(n):
                h, chain, c, j, off, first, last = units[n]
                pe.wait_ge(w_ready, n + 1)
                if diagonal(n):
                    pe.wait_ge(w_masked, diagonals(n + 1))
                if first and chain >= 2:
                    pe.wait_ge(y_moved, chain - 1)
                nc.tensor.matmul(g.bank[6 + chain % 2][:, off:512], v_tok[:, j, h * P:(h + 1) * P],
                                 w[:, n % RING, off:512], start=first, stop=last,
                                 skip_group_check=True).then_inc(pv_done, 1)

            for n in range(N + 4):
                if n < N:
                    z(n)
                if 0 <= n - 2 < N:
                    s(n - 2)
                if n >= 4:
                    pv(n - 4)

        @block.vector
        def _(dve):
            def softplus(n):
                off = units[n][4]
                dve.wait_ge(ln_ready, n + 1)
                if n >= RING:
                    dve.wait_ge(s_ready, n - RING + 1)
                    dve.wait_ge(acc_ready, n - RING + 1)
                ins = nc.vector.scalar_tensor_tensor(out=u[:, n % RING, off:512], in0=zb(n, off), scalar=0.0,
                                                     in1=e[:, n % RING, off:512], op0=ALU.max, op1=ALU.add)
                if diagonal(n):
                    ins.then_inc(u_step, 1)
                    dve.wait_ge(u_step, diagonals(n + 1))
                    ins = nc.vector.tensor_tensor(u[:, n % RING, off:off + P], u[:, n % RING, off:off + P],
                                                  g.strict[:], ALU.mult)
                ins.then_inc(u_ready, 1)

            def mask_w(n):
                off = units[n][4]
                if diagonal(n):
                    dve.wait_ge(w_ready, n + 1)
                    part = w[:, n % RING, off:off + P]
                    nc.vector.scalar_tensor_tensor(out=part, in0=part, scalar=3e38, in1=g.strict[:],
                                                   op0=ALU.min, op1=ALU.mult).then_inc(w_masked, 1)

            def move_y(n):
                h, chain, c, j, off, first, last = units[n]
                if last:
                    dve.wait_ge(pv_done, n + 1)
                    nc.vector.tensor_copy(qT[:, h, 512 * c:512 * c + 512],
                                          g.bank[6 + chain % 2][:]).then_inc(y_moved, 1)

            for n in range(N + 5):
                if 0 <= n - 1 < N:
                    softplus(n - 1)
                if 0 <= n - 3 < N:
                    mask_w(n - 3)
                if n >= 5:
                    move_y(n - 5)

        @block.scalar
        def _(act):
            def log_part(n):
                off = units[n][4]
                part = e[:, n % RING, off:512]
                act.wait_ge(z_ready, n + 1)
                if n >= RING:
                    act.wait_ge(u_ready, n - RING + 1)
                nc.scalar.activation(part, zb(n, off), ACT.Abs).then_inc(abs_ready, 1)
                act.wait_ge(abs_ready, n + 1)
                nc.scalar.activation(part, part, ACT.Exp, scale=-1.0).then_inc(exp_ready, 1)
                act.wait_ge(exp_ready, n + 1)
                nc.scalar.activation(part, part, ACT.Ln, bias=1.0).then_inc(ln_ready, 1)

            def weights(n):
                off = units[n][4]
                act.wait_ge(s_ready, n + 1)
                if n >= RING:
                    act.wait_ge(pv_done, n - RING + 1)
                nc.scalar.activation(w[:, n % RING, off:512], zb(n, off), ACT.Exp).then_inc(w_ready, 1)

            nc.scalar.preload_act_table_set("natural_log_exp_and_others")
            for n in range(N + 2):
                if n < N:
                    log_part(n)
                if n >= 2:
                    weights(n - 2)

        @block.gpsimd
        def _(pool):
            for n in range(N):
                off, first = units[n][4], units[n][5]
                pool.wait_ge(u_ready, n + 1)
                if n >= 2:
                    pool.wait_ge(s_ready, n - 1)
                if first:
                    ins = pool.tensor_copy(acc[:, n % 3, off:512], u[:, n % RING, off:512])
                else:
                    before = units[n - 1][4]
                    pool.wait_ge(acc_ready, n)
                    ins = pool.tensor_tensor(acc[:, n % 3, before:512], acc[:, (n - 1) % 3, before:512],
                                             u[:, n % RING, before:512], ALU.add)
                    if off < before:
                        ins = pool.tensor_copy(acc[:, n % 3, off:before], u[:, n % RING, off:before])
                ins.then_inc(acc_ready, 1)


def stage_sb_sample(nc, g, qT, kT, v_tok):
    N = KB + 1
    HB = NB // 2
    KR = 4
    with ExitStack() as ctx:
        sem = ctx.enter_context(stage_semaphores(nc))
        def sb(name, shape):
            return ctx.enter_context(nc.sbuf_tensor(name, shape, F32))

        kc = sb("cached_k", [P, KR, HB, 512])
        vc = sb("cached_v", [P, 2, NB, 512])
        kcT = sb("cached_kT", [P, 2, HB, H * P])
        e = sb("s_softplus_work", [P, 2, 512])
        u = sb("s_softplus", [P, 2, 512])
        acc = sb("s_later_keys_sum", [P, 2, 512])
        w = sb("s_weights", [P, 2, 512])
        k_in = [sem(f"s_k_in{i}") for i in range(KR)]
        v_in = [sem("s_v_in0"), sem("s_v_in1")]
        turned = sem("s_turned")
        turn_moved = [sem("s_turn_moved_act"), sem("s_turn_moved_dve")]
        z_half = sem("s_z_half")
        z_ready = sem("s_z_ready")
        abs_ready = sem("s_abs_ready")
        exp_ready = sem("s_exp_ready")
        ln_ready = sem("s_ln_ready")
        u_step = sem("s_u_step")
        u_ready = sem("s_u_ready")
        s_ready = sem("s_s_ready")
        acc_ready = sem("s_acc_ready")
        w_ready = sem("s_w_ready")
        w_masked = sem("s_w_masked")
        pv_done = sem("s_pv_done")
        block = ctx.enter_context(nc.Block())
        kv = [t[0].rearrange("b (j p) h d -> j p b (h d)", p=P) for t in (g.cache_k, g.cache_v)]

        @block.sync
        def _(sp):
            def load_k(n):
                for half in range(2):
                    f = 2 * (n - 1) + half
                    if f >= KR:
                        sp.wait_ge(turned, HB * (f - KR + 1))
                    sp.dma_start(kc[:, f % KR],
                                 kv[0][KB - n][:, half * HB:(half + 1) * HB, :]).then_inc(k_in[f % KR], 16)

            load_k(1)
            load_k(2)
            for n in range(1, N):
                if n + 2 < N:
                    load_k(n + 2)
                if n >= 3:
                    sp.wait_ge(pv_done, n - 1)
                sp.dma_start(vc[:, n % 2], kv[1][KB - n]).then_inc(v_in[n % 2], 16)

        @block.tensor
        def _(pe):
            def z(n):
                bank = g.bank[n % 2]
                if n >= 2:
                    pe.wait_ge(w_ready, n - 1)
                if n == 0:
                    for h in range(H):
                        last = nc.tensor.matmul(bank[:, h * P:(h + 1) * P], kT[:, h, TP:T], qT[:, h, TP:T],
                                                start=(h == 0), stop=True, skip_group_check=True)
                    last.then_inc(z_ready, 1)
                    return
                for half in range(2):
                    f = 2 * (n - 1) + half
                    pe.wait_ge(k_in[f % KR], 16 * (f // KR + 1))
                    for r in range(HB):
                        t = HB * f + r
                        if t >= 4:
                            pe.wait_ge(turn_moved[t % 2], t // 2 - 1)
                        for h in range(H):
                            last = nc.tensor.transpose(g.bank[4 + t % 4][:, h * P:(h + 1) * P],
                                                       kc[:, f % KR, r, h * P:(h + 1) * P], g.ident[:])
                        last.then_inc(turned, 1)
                for half in range(2):
                    f = 2 * (n - 1) + half
                    pe.wait_ge(turn_moved[0], 2 * (f + 1))
                    pe.wait_ge(turn_moved[1], 2 * (f + 1))
                    for r in range(HB):
                        b = half * HB + r
                        for h in range(H):
                            col = h * P + b * LS
                            last = nc.tensor.matmul(bank[:, col:col + LS], kcT[:, half, r, h * P:(h + 1) * P],
                                                    qT[:, h, TP + b * LS:TP + (b + 1) * LS],
                                                    start=(b == 0 and h == 0), stop=True, skip_group_check=True)
                    last.then_inc(z_half, 1)
                    if half == 1:
                        pe.wait_ge(z_half, 2 * n)
                        nc.tensor.nop().then_inc(z_ready, 1)

            def s(n):
                pe.wait_ge(u_ready, n + 1)
                ins = nc.tensor.matmul(g.bank[n % 2][:], g.tri_neg[:], u[:, n % 2, :], start=False, stop=True,
                                       skip_group_check=True)
                if n:
                    pe.wait_ge(acc_ready, n)
                    ins = nc.tensor.matmul(g.bank[n % 2][:], g.neg_ones[:], acc[:, (n - 1) % 2, :], start=False,
                                           stop=True, skip_group_check=True)
                ins.then_inc(s_ready, 1)

            def pv(n):
                pe.wait_ge(w_ready, n + 1)
                out = g.bank[2]
                if n == 0:
                    pe.wait_ge(w_masked, 1)
                    for h in range(H):
                        last = nc.tensor.matmul(out[:, h * P:(h + 1) * P], v_tok[:, NT - 1, h * P:(h + 1) * P],
                                                w[:, 0, h * P:(h + 1) * P], start=(h == 0), stop=False,
                                                skip_group_check=True)
                else:
                    pe.wait_ge(v_in[n % 2], 16 * ((n + 1) // 2))
                    for h in range(H):
                        for b in range(NB):
                            col = h * P + b * LS
                            last = nc.tensor.matmul(out[:, col:col + LS], vc[:, n % 2, b, h * P:(h + 1) * P],
                                                    w[:, n % 2, col:col + LS], start=False, stop=(n == N - 1),
                                                    skip_group_check=True)
                last.then_inc(pv_done, 1)

            for n in range(N + 2):
                if n < N:
                    z(n)
                if 0 <= n - 1 < N:
                    s(n - 1)
                if n >= 2:
                    pv(n - 2)

        def move_turned(eng, copy, parity, n):
            for b in range(parity, NB, 2):
                t = NB * (n - 1) + b
                half, r = divmod(b, HB)
                eng.wait_ge(turned, t + 1)
                if n >= 2:
                    eng.wait_ge(z_half, 2 * (n - 2) + half + 1)
                copy(kcT[:, half, r, :], g.bank[4 + t % 4][:]).then_inc(turn_moved[parity], 1)

        @block.vector
        def _(dve):
            mask = g.strict_s[:].unsqueeze(1).broadcast_to([P, H, P])

            def softplus(n):
                dve.wait_ge(ln_ready, n + 1)
                if n >= 2:
                    dve.wait_ge(s_ready, n - 1)
                    dve.wait_ge(acc_ready, n - 1)
                ins = nc.vector.scalar_tensor_tensor(out=u[:, n % 2], in0=g.bank[n % 2][:], scalar=0.0,
                                                     in1=e[:, n % 2], op0=ALU.max, op1=ALU.add)
                if n == 0:
                    ins.then_inc(u_step, 1)
                    dve.wait_ge(u_step, 1)
                    part = u[:, 0].rearrange("p (h t) -> p h t", h=H)
                    ins = nc.vector.tensor_tensor(part, part, mask, ALU.mult)
                ins.then_inc(u_ready, 1)

            for n in range(N + 1):
                if 1 <= n < N:
                    move_turned(dve, nc.vector.tensor_copy, 1, n)
                if n < N:
                    softplus(n)
                if n == 1:
                    dve.wait_ge(w_ready, 1)
                    part = w[:, 0].rearrange("p (h t) -> p h t", h=H)
                    nc.vector.scalar_tensor_tensor(out=part, in0=part, scalar=3e38, in1=mask, op0=ALU.min,
                                                   op1=ALU.mult).then_inc(w_masked, 1)
            dve.wait_ge(pv_done, N)
            nc.vector.tensor_copy(qT[:, :, TP:T], g.bank[2][:].rearrange("p (h t) -> p h t", h=H))

        @block.scalar
        def _(act):
            nc.scalar.preload_act_table_set("natural_log_exp_and_others")
            for n in range(N + 1):
                if 1 <= n < N:
                    move_turned(act, nc.scalar.copy, 0, n)
                if n < N:
                    act.wait_ge(z_ready, n + 1)
                    if n >= 2:
                        act.wait_ge(u_ready, n - 1)
                    nc.scalar.activation(e[:, n % 2], g.bank[n % 2][:], ACT.Abs).then_inc(abs_ready, 1)
                    act.wait_ge(abs_ready, n + 1)
                    nc.scalar.activation(e[:, n % 2], e[:, n % 2], ACT.Exp, scale=-1.0).then_inc(exp_ready, 1)
                    act.wait_ge(exp_ready, n + 1)
                    nc.scalar.activation(e[:, n % 2], e[:, n % 2], ACT.Ln, bias=1.0).then_inc(ln_ready, 1)
                if n:
                    m = n - 1
                    act.wait_ge(s_ready, m + 1)
                    if m >= 2:
                        act.wait_ge(pv_done, m - 1)
                    nc.scalar.activation(w[:, m % 2], g.bank[m % 2][:], ACT.Exp).then_inc(w_ready, 1)

        @block.gpsimd
        def _(pool):
            for n in range(N):
                pool.wait_ge(u_ready, n + 1)
                if n >= 2:
                    pool.wait_ge(s_ready, n)
                if n == 0:
                    pool.tensor_copy(acc[:, 0], u[:, 0]).then_inc(acc_ready, 1)
                else:
                    pool.wait_ge(acc_ready, n)
                    pool.tensor_tensor(acc[:, n % 2], acc[:, (n - 1) % 2], u[:, n % 2],
                                       ALU.add).then_inc(acc_ready, 1)


def stage_ml_project(nc, g, xT, m):
    with ExitStack() as ctx:
        sem = ctx.enter_context(stage_semaphores(nc))
        def sb(name, shape):
            return ctx.enter_context(nc.sbuf_tensor(name, shape, F32))

        w = sb("w_ml", [P, 2, DT, 512])
        w_gates = sb("w_ml_gates", [P, DT, 2 * H])
        bias = sb("ml_bias", [P, 2, 512])
        gate_bias = sb("ml_gate_bias", [H, 2])
        w_loaded = [sem(f"m_w{i}") for i in range(3)]
        gates_in = sem("m_gates_in")
        bias_in = sem("m_bias_in")
        zeroed = sem("m_zeroed")
        prod = sem("m_prod")
        tok_moved = sem("m_tok_moved")
        feat_moved = sem("m_feat_moved")
        k_turned = sem("m_k_turned")
        k_moved = sem("m_k_moved")
        block = ctx.enter_context(nc.Block())
        w_in_t = g.w_in[0].rearrange("(k p) n -> p k n", p=P)
        NBK = 6
        NTOK = 2 * NT

        @block.sync
        def _(sp):
            sp.dma_start(w_gates[:], w_in_t[:, :, O_MI:O_MI + 2 * H]).then_inc(gates_in, 16)
            sp.dma_start(gate_bias[:], g.b_in[0, O_MI:O_MI + 2 * H].rearrange("(a h) -> h a", h=H),
                         allow_slow_non_contiguous=True).then_inc(gates_in, 16)
            for s, off in enumerate((O_MV, O_MO, O_MQ)):
                if s == 2:
                    sp.wait_ge(prod, NTOK - 1)
                sp.dma_start(w[:, s % 2], w_in_t[:, :, off:off + 512]).then_inc(w_loaded[s], 16)
                if s == 0:
                    sp.dma_start(bias[:].rearrange("p a n -> p (a n)"),
                                 g.b_in[0:1, O_MV:O_MV + 1024].broadcast_to([P, 1024])).then_inc(bias_in, 16)

        @block.gpsimd
        def _(pool):
            pool.memset(m.qz[:], 0.0).then_inc(zeroed, 1)
            pool.memset(m.v_aug[:, :, :, HD:HD + 1], 1.0)

        @block.tensor
        def _(pe):
            n = 0

            def bank_free(n):
                last = n - NBK
                if 0 <= last < NTOK:
                    pe.wait_ge(tok_moved, last + 1)
                elif last >= NTOK:
                    pe.wait_ge(feat_moved, last + 1 - NTOK)

            for i in range(NT):
                for s in range(2):
                    pe.wait_ge(w_loaded[s], 16)
                    bank_free(n)
                    for k in range(DT):
                        last = nc.tensor.matmul(g.bank[n % NBK][:], xT[:, k, i * P:(i + 1) * P], w[:, s, k, :],
                                                start=(k == 0), stop=(k == DT - 1))
                    last.then_inc(prod, 1)
                    n += 1
            pe.wait_ge(w_loaded[2], 16)
            for tile in (2, 3, 0, 1):
                for lo, hi in CHUNKS:
                    bank_free(n)
                    for k in range(DT):
                        last = nc.tensor.matmul(g.bank[n % NBK][:, 0:hi - lo], w[:, 0, k, tile * P:(tile + 1) * P],
                                                xT[:, k, lo:hi], start=(k == 0), stop=(k == DT - 1))
                    last.then_inc(prod, 1)
                    n += 1
            pe.wait_ge(gates_in, 32)
            for a in range(2):
                for lo, hi in CHUNKS:
                    bank_free(n)
                    for k in range(DT):
                        last = nc.tensor.matmul(g.bank[n % NBK][0:H, 0:hi - lo], w_gates[:, k, a * H:(a + 1) * H],
                                                xT[:, k, lo:hi], start=(k == 0), stop=(k == DT - 1))
                    last.then_inc(prod, 1)
                    n += 1
            pe.wait_ge(feat_moved, 6)
            for i in range(NT):
                if i >= 4:
                    pe.wait_ge(k_moved, i // 2 - 1)
                off = (i % 2) * 256
                for pair in range(2):
                    last = nc.tensor.transpose(g.bank[6 + i // 2 % 2][:, off + pair * P:off + (pair + 1) * P],
                                               m.kT[:, pair, i * P:(i + 1) * P], g.ident[:])
                if i % 2 or i == NT - 1:
                    last.then_inc(k_turned, 1)

        @block.vector
        def _(dve):
            dve.wait_ge(bias_in, 16)
            for n in range(NTOK):
                i, s = divmod(n, 2)
                dve.wait_ge(prod, n + 1)
                if s == 0:
                    nc.vector.tensor_tensor(m.v_aug[:, i, :, 0:HD],
                                            g.bank[n % NBK][:].rearrange("p (h e) -> p h e", h=H),
                                            bias[:, 0, :].rearrange("p (h e) -> p h e", h=H),
                                            ALU.add).then_inc(tok_moved, 1)
                else:
                    nc.vector.tensor_tensor(m.o_gate[:, i, :], g.bank[n % NBK][:], bias[:, 1, :],
                                            ALU.add).then_inc(tok_moved, 1)
            for t in range(5):
                dve.wait_ge(k_turned, t + 1)
                tiles = 2 if t < 4 else 1
                nc.vector.tensor_copy(m.k_tok[:, 2 * t:2 * t + tiles, :],
                                      g.bank[6 + t % 2][:, 0:tiles * 256].rearrange("p (i d) -> p i d", i=tiles)
                                      ).then_inc(k_moved, 1)

        @block.scalar
        def _(act):
            n = NTOK
            act.wait_ge(zeroed, 1)
            for tile in (2, 3, 0, 1):
                for lo, hi in CHUNKS:
                    act.wait_ge(prod, n + 1)
                    ps = g.bank[n % NBK][:, 0:hi - lo]
                    if tile >= 2:
                        last = nc.scalar.activation(m.kT[:, tile - 2, lo:hi], ps, ACT.Identity,
                                                    bias=g.mkbias[:, tile - 2:tile - 1], scale=ML_SCALE)
                    else:
                        col = V_BIN + O_MQ // P + tile
                        for half in range(2):
                            r = slice(64 * half, 64 * half + 64)
                            last = nc.scalar.activation(m.qz[r, 2 * tile + half, lo:hi], ps[r, :], ACT.Identity,
                                                        bias=g.vec[r, col:col + 1])
                    last.then_inc(feat_moved, 1)
                    n += 1
            for a, row in enumerate((m.ig, m.fg)):
                for lo, hi in CHUNKS:
                    act.wait_ge(prod, n + 1)
                    nc.scalar.activation(row[:, lo:hi], g.bank[n % NBK][0:H, 0:hi - lo], ACT.Identity,
                                         bias=gate_bias[:, a:a + 1]).then_inc(feat_moved, 1)
                    n += 1


def stage_ml_gates(nc, g, m):
    NC = 16
    with ExitStack() as ctx:
        sem = ctx.enter_context(stage_semaphores(nc))
        def sb(name, shape):
            return ctx.enter_context(nc.sbuf_tensor(name, shape, F32))

        keep = sb("keep_row", [H, T])
        lf2, ig2, b, mm = (sb(n, [H, T]) for n in ("lf_restart", "ig_restart", "b_row", "m_row"))
        m_prev = sb("m_prev", [H, NC])
        w_end = sb("w_end", [H, NC])
        tmp = sb("start_tmp", [H, NB])
        step = sem("g_step")
        keep_ready = sem("g_keep_ready")
        m0_in = sem("g_m0_in")
        f_abs = sem("g_f_abs")
        f_ln = sem("g_f_ln")
        exps = sem("g_exps")
        turned = sem("g_turned")
        spread = sem("g_spread")
        m_out = sem("g_m_out")
        m_ready = sem("g_m_ready")
        rows_ready = sem("g_rows_ready")
        rows_exp = sem("g_rows_exp")
        sig = sem("g_sig")
        norm_in = sem("g_norm_in")
        block = ctx.enter_context(nc.Block())

        def parts(row):
            return (row[:, 0:TP].rearrange("h (c t) -> h c t", c=8),
                    row[:, TP:T].rearrange("h (c t) -> h c t", c=NB))

        @block.sync
        def _(sp):
            sp.dma_start(m_prev[:, 8:16], g.state_m[0].rearrange("b h -> h b"),
                         allow_slow_non_contiguous=True).then_inc(m0_in, 16)
            sp.dma_start(m.norm_g[:], g.ml_norm_g.broadcast_to([P, 512])).then_inc(norm_in, 16)
            sp.wait_ge(m_ready, 1)
            sp.dma_start(g.o_m_p[0].rearrange("b h -> h b"), mm[:, TP - 1:TP],
                         allow_slow_non_contiguous=True).then_inc(m_out, 16)
            sp.dma_start(g.o_m_s[0].rearrange("b h -> h b"), mm[:, TP + LS - 1:T:LS],
                         allow_slow_non_contiguous=True).then_inc(m_out, 16)
            sp.wait_ge(m_out, 32)

        @block.gpsimd
        def _(pool):
            pool.memset(keep[:], 1.0).then_inc(keep_ready, 1)
            pool.wait_ge(keep_ready, 1)
            pool.memset(keep[:, 0:TP:P], 0.0)
            pool.memset(keep[:, TP:T:LS], 0.0).then_inc(keep_ready, 1)
            pool.wait_ge(norm_in, 16)
            for i in range(NT):
                pool.wait_ge(sig, i + 1)
                pool.tensor_tensor(m.o_gate[:, i, :], m.o_gate[:, i, :], m.norm_g[:], ALU.mult)

        @block.scalar
        def _(act):
            act.wait_ge(step, 1)
            nc.scalar.activation(b[:], m.fg[:], ACT.Abs).then_inc(f_abs, 1)
            act.wait_ge(f_abs, 1)
            nc.scalar.activation(b[:], b[:], ACT.Exp, scale=-1.0).then_inc(f_abs, 1)
            act.wait_ge(f_abs, 2)
            nc.scalar.activation(b[:], b[:], ACT.Ln, bias=1.0).then_inc(f_ln, 1)
            for i in range(NT):
                nc.scalar.activation(m.o_gate[:, i, :], m.o_gate[:, i, :], ACT.Sigmoid).then_inc(sig, 1)
            act.wait_ge(rows_ready, 1)
            nc.scalar.activation(lf2[:], lf2[:], ACT.Exp)
            nc.scalar.activation(ig2[:], ig2[:], ACT.Exp)
            nc.scalar.activation(m_prev[:], m_prev[:], ACT.Exp)
            nc.scalar.activation(m.fg[:], mm[:], ACT.Exp, scale=-1.0).then_inc(rows_exp, 1)

        @block.tensor
        def _(pe):
            pe.wait_ge(rows_exp, 1)
            for q, row in enumerate((m.ig, lf2, m.fg, ig2)):
                for i in range(NT):
                    col = (q * NT + i) * H
                    last = nc.tensor.transpose(g.bank[0][:, col:col + H], row[:, i * P:(i + 1) * P],
                                               g.ident[0:H, 0:H])
            last.then_inc(turned, 1)
            for h in range(H):
                last = nc.tensor.matmul(g.bank[1][:, h * NC:(h + 1) * NC], g.sel[:, h, :], m_prev[:],
                                        start=True, stop=True)
            last.then_inc(turned, 1)

        @block.vector
        def _(dve):
            count = [0]

            def link(ins):
                count[0] += 1
                ins.then_inc(step, 1)
                dve.wait_ge(step, count[0])

            link(nc.vector.memset(m_prev[:, 0:1], 0.0))
            dve.wait_ge(f_ln, 1)
            link(nc.vector.scalar_tensor_tensor(out=m.fg[:], in0=m.fg[:], scalar=0.0, in1=b[:], op0=ALU.min,
                                                op1=ALU.subtract))
            dve.wait_ge(keep_ready, 2)
            link(nc.vector.tensor_tensor_scan(b[:], keep[:], m.fg[:], 0.0, ALU.mult, ALU.add))
            link(nc.vector.tensor_copy(lf2[:], m.fg[:]))
            link(nc.vector.tensor_copy(ig2[:], m.ig[:]))
            dve.wait_ge(m0_in, 16)
            link(nc.vector.tensor_tensor(tmp[:], m.fg[:, TP:T:LS], m_prev[:, 8:16], ALU.add))
            link(nc.vector.tensor_tensor(ig2[:, TP:T:LS], tmp[:], m.ig[:, TP:T:LS], ALU.max))
            link(nc.vector.memset(lf2[:, TP:T:LS], NEG))
            link(nc.vector.tensor_tensor_scan(mm[:], lf2[:], ig2[:], 0.0, ALU.add, ALU.max))
            nc.vector.tensor_copy(m_prev[:, 1:8], mm[:, P - 1:TP - P:P]).then_inc(m_ready, 1)
            link(nc.vector.tensor_tensor(m.ig[:], m.ig[:], b[:], ALU.subtract))
            link(nc.vector.tensor_tensor(m.w[:], b[:], mm[:], ALU.subtract))
            link(nc.vector.tensor_copy(w_end[:, 0:8], m.w[:, P - 1:TP:P]))
            link(nc.vector.tensor_copy(w_end[:, 8:16], m.w[:, TP + LS - 1:T:LS]))
            for n, (o, a, c) in enumerate(zip(parts(lf2), parts(m.w), (m_prev[:, 0:8], m_prev[:, 8:16]))):
                nc.vector.tensor_tensor(o, a, c.unsqueeze(2).broadcast_to(list(a.shape)), ALU.add)
            for o, a, c in zip(parts(ig2), parts(m.ig), (w_end[:, 0:8], w_end[:, 8:16])):
                link(nc.vector.tensor_tensor(o, a, c.unsqueeze(2).broadcast_to(list(a.shape)), ALU.add))
            nc.vector.tensor_tensor(m_prev[:], m_prev[:], w_end[:], ALU.add).then_inc(rows_ready, 1)
            dve.wait_ge(turned, 2)
            nc.vector.tensor_copy(m.cols[:].rearrange("p q i h -> p (q i h)"), g.bank[0][:, 0:4 * NT * H])
            nc.vector.tensor_copy(m.s_old[:].rearrange("p h c -> p (h c)"), g.bank[1][:, 0:H * NC])


def stage_mlstm(nc, g, m, ycT):
    U, S_IN, E_M, G_W = range(4)
    A = HD + 1
    with ExitStack() as ctx:
        sem = ctx.enter_context(stage_semaphores(nc))
        def sb(name, shape):
            return ctx.enter_context(nc.sbuf_tensor(name, shape, F32))

        c_state = sb("c_state", [P, 2, A])
        cs = sb("c_sample", [P, NB, 2, A])
        qs = sb("q_by_request", [P, H, NB, P])
        dexp = sb("pair_weights", [P, H, P])
        wqk = sb("wqk", [P, H, P])
        kg = sb("weighted_k", [P, 2, 256])
        kgb = sb("weighted_k_by_request", [P, NB, 256])
        inter = sb("inter", [P, H, A])
        num = sb("num", [P, H, A])
        den = sb("den", [P, 3, H])
        hc = sb("hc", [P, NT, 512])
        stats = sb("hc_stats", [P, NT, H, 6])
        mv = sb("hc_mean_var", [P, NT, H, 2])
        rstd = sb("hc_rstd", [P, NT, H, 1])
        seg = sb("request_mask", [P, NB])
        c_in = sem("r_c_in")
        filled = sem("r_filled")
        qs_ready = sem("r_qs_ready")
        c_zero = sem("r_c_zero")
        w_bank = sem("r_w_bank")
        s_bank = sem("r_s_bank")
        dexp_ready = sem("r_dexp_ready")
        wqk_ready = sem("r_wqk_ready")
        kg_ready = sem("r_kg_ready")
        inter_prod = sem("r_inter_prod")
        inter_ready = sem("r_inter_ready")
        intra_prod = sem("r_intra_prod")
        num_ready = sem("r_num_ready")
        c_prod = sem("r_c_prod")
        c_ready = sem("r_c_ready")
        step = sem("r_step")
        var_ready = sem("r_var_ready")
        std_ready = sem("r_std_ready")
        yc_ready = sem("r_yc_ready")
        yc_turned = sem("r_yc_turned")
        yc_moved = sem("r_yc_moved")
        states_out = sem("r_states_out")
        block = ctx.enter_context(nc.Block())

        @block.sync
        def _(sp):
            for two in range(2):
                r = slice(64 * two, 64 * two + 64)
                for pair in range(2):
                    sp.dma_start(cs[r, :, pair, 0:HD], g.state_c[0, :, 2 * pair + two].rearrange("b d e -> d b e")
                                 ).then_inc(c_in, 16)
                    sp.dma_start(cs[r, :, pair, HD], g.state_n[0, :, 2 * pair + two].rearrange("b d -> d b"),
                                 allow_slow_non_contiguous=True).then_inc(c_in, 16)
            sp.wait_ge(c_ready, 8)
            for two in range(2):
                r = slice(64 * two, 64 * two + 64)
                sp.dma_start(g.o_c_p[0, 0, two::2].rearrange("q d e -> d q e"), c_state[r, :, 0:HD]
                             ).then_inc(states_out, 16)
                sp.dma_start(g.o_n_p[0, 0, two::2].rearrange("q d -> d q"), c_state[r, :, HD],
                             allow_slow_non_contiguous=True).then_inc(states_out, 16)
            sp.wait_ge(c_ready, 8 + NB)
            for two in range(2):
                r = slice(64 * two, 64 * two + 64)
                for pair in range(2):
                    sp.dma_start(g.o_c_s[0, :, 2 * pair + two].rearrange("b d e -> d b e"), cs[r, :, pair, 0:HD]
                                 ).then_inc(states_out, 16)
                    sp.dma_start(g.o_n_s[0, :, 2 * pair + two].rearrange("b d -> d b"), cs[r, :, pair, HD],
                                 allow_slow_non_contiguous=True).then_inc(states_out, 16)
            sp.wait_ge(states_out, 16 * 12)

        @block.gpsimd
        def _(pool):
            pool.memset(c_state[:], 0.0).then_inc(c_zero, 1)
            pool.memset(seg[:], 1.0).then_inc(filled, 1)
            pool.memset(qs[:], 0.0).then_inc(filled, 1)
            pool.wait_ge(filled, 2)
            pool.affine_select(out=seg[:], in_=seg[:], compare_op=ALU.is_ge, fill=0.0, base=0,
                               pattern=[[-LS, NB]], channel_multiplier=1).then_inc(filled, 1)
            pool.wait_ge(filled, 3)
            pool.affine_select(out=seg[:], in_=seg[:], compare_op=ALU.is_ge, fill=0.0, base=LS - 1,
                               pattern=[[LS, NB]], channel_multiplier=-1).then_inc(filled, 1)
            for b in range(NB):
                last = pool.tensor_copy(qs[:, :, b, b * LS:(b + 1) * LS], m.qz[:, :, TP + b * LS:TP + (b + 1) * LS])
            last.then_inc(qs_ready, 1)
            for i in range(NT):
                if i >= 2:
                    pool.wait_ge(c_prod, i - 1)
                pool.tensor_tensor(kg[:, i % 2].rearrange("p (h d) -> p h d", h=H),
                                   m.k_tok[:, i, :].rearrange("p (h d) -> p h d", h=H),
                                   m.cols[:, G_W, i, :].unsqueeze(2).broadcast_to([P, H, QD]),
                                   ALU.mult).then_inc(kg_ready, 1)
            pool.wait_ge(kg_ready, NT)
            pool.wait_ge(filled, 4)
            for b in range(NB):
                last = pool.tensor_scalar(kgb[:, b], kg[:, (NT - 1) % 2], seg[:, b:b + 1], None, ALU.mult)
            last.then_inc(kg_ready, 1)

        @block.tensor
        def _(pe):
            def scores(i):
                cols = slice(i * P, (i + 1) * P)
                mask = g.causal_s if i == NT - 1 else g.causal
                if i:
                    pe.wait_ge(dexp_ready, i)
                for h in range(H):
                    out = g.bank[0][:, h * P:(h + 1) * P]
                    nc.tensor.matmul(out, g.sel[:, h, :], m.w[:, cols], start=True, stop=False)
                    last = nc.tensor.matmul(out, g.ident[:], mask[:], start=False, stop=True)
                last.then_inc(w_bank, 1)
                if i:
                    pe.wait_ge(wqk_ready, i)
                for h in range(H):
                    last = nc.tensor.matmul(g.bank[1][:, h * P:(h + 1) * P], m.kT[:, h // 2, cols],
                                            m.qz[:, h, cols], start=True, stop=True)
                last.then_inc(s_bank, 1)

            scores(0)
            for i in range(NT):
                cols = slice(i * P, (i + 1) * P)
                if i:
                    pe.wait_ge(inter_ready, i)
                    if i < NT - 1:
                        pe.wait_ge(c_ready, i)
                    else:
                        pe.wait_ge(c_in, 16 * 8)
                        pe.wait_ge(qs_ready, 1)
                else:
                    pe.wait_ge(c_zero, 1)
                for h in range(H):
                    out = g.bank[2 + h // 2][:, (h % 2) * A:(h % 2 + 1) * A]
                    if i < NT - 1:
                        last = nc.tensor.matmul(out, m.qz[:, h, cols], c_state[:, h // 2, :], start=True, stop=True)
                    else:
                        for b in range(NB):
                            last = nc.tensor.matmul(out, qs[:, h, b, :], cs[:, b, h // 2, :],
                                                    start=(b == 0), stop=(b == NB - 1))
                last.then_inc(inter_prod, 1)
                if i < NT - 1:
                    pe.wait_ge(kg_ready, i + 1)
                    if i:
                        pe.wait_ge(c_ready, i)
                    for h in range(H):
                        last = nc.tensor.matmul(g.bank[6 + h // 2][:, (h % 2) * A:(h % 2 + 1) * A],
                                                kg[:, i % 2, (h // 2) * P:(h // 2 + 1) * P], m.v_aug[:, i, h, :],
                                                start=True, stop=True)
                    last.then_inc(c_prod, 1)
                if i + 1 < NT:
                    scores(i + 1)
                pe.wait_ge(wqk_ready, i + 1)
                if i:
                    pe.wait_ge(num_ready, i)
                for h in range(H):
                    last = nc.tensor.matmul(g.bank[4 + h // 2][:, (h % 2) * A:(h % 2 + 1) * A], wqk[:, h, :],
                                            m.v_aug[:, i, h, :], start=True, stop=True)
                last.then_inc(intra_prod, 1)
            pe.wait_ge(kg_ready, NT + 1)
            pe.wait_ge(inter_ready, NT)
            for b in range(NB):
                if b == 0:
                    pe.wait_ge(c_ready, 8)
                if b == 1:
                    pe.wait_ge(dexp_ready, NT)
                if b >= 2:
                    pe.wait_ge(c_ready, 8 + b - 1)
                for h in range(H):
                    last = nc.tensor.matmul(g.bank[(6, 0)[b % 2] + h // 2][:, (h % 2) * A:(h % 2 + 1) * A],
                                            kgb[:, b, (h // 2) * P:(h // 2 + 1) * P], m.v_aug[:, NT - 1, h, :],
                                            start=True, stop=True)
                last.then_inc(c_prod, 1)
            for i in range(NT):
                pe.wait_ge(yc_ready, i + 1)
                if i >= 2:
                    pe.wait_ge(yc_moved, i - 1)
                for h in range(H):
                    last = nc.tensor.transpose(g.bank[2 + i % 2][:, h * P:(h + 1) * P],
                                               hc[:, i, h * P:(h + 1) * P], g.ident[:])
                last.then_inc(yc_turned, 1)

        @block.scalar
        def _(act):
            for i in range(NT):
                act.wait_ge(w_bank, i + 1)
                if i:
                    act.wait_ge(wqk_ready, i)
                for h in range(H):
                    last = nc.scalar.activation(dexp[:, h, :], g.bank[0][:, h * P:(h + 1) * P], ACT.Exp,
                                                bias=m.cols[:, U, i, h:h + 1])
                last.then_inc(dexp_ready, 1)
                act.wait_ge(inter_prod, i + 1)
                if i:
                    act.wait_ge(num_ready, i)
                for h in range(H):
                    last = nc.scalar.activation(inter[:, h, :], g.bank[2 + h // 2][:, (h % 2) * A:(h % 2 + 1) * A],
                                                ACT.Copy, scale=m.cols[:, S_IN, i, h:h + 1])
                last.then_inc(inter_ready, 1)
            act.wait_ge(var_ready, 1)
            nc.scalar.activation(rstd[:], mv[:, :, :, 1:2], ACT.Sqrt).then_inc(std_ready, 1)
            for i in range(NT):
                act.wait_ge(yc_turned, i + 1)
                nc.scalar.copy(ycT[:, :, i * P:(i + 1) * P],
                               g.bank[2 + i % 2][:].rearrange("p (h t) -> p h t", h=H)).then_inc(yc_moved, 1)

        @block.vector
        def _(dve):
            count = [0]

            def link(ins):
                count[0] += 1
                ins.then_inc(step, 1)
                dve.wait_ge(step, count[0])

            def new_state(state, c, bank0):
                for h in range(H):
                    r = slice(64 * (h % 2), 64 * (h % 2) + 64)
                    last = nc.vector.scalar_tensor_tensor(
                        out=state[r, h // 2, :], in0=state[r, h // 2, :], scalar=m.s_old[r, h, c:c + 1],
                        in1=g.bank[bank0 + h // 2][r, (h % 2) * A:(h % 2 + 1) * A], op0=ALU.mult, op1=ALU.add)
                last.then_inc(c_ready, 1)

            for i in range(NT):
                dve.wait_ge(dexp_ready, i + 1)
                dve.wait_ge(s_bank, i + 1)
                if i:
                    dve.wait_ge(intra_prod, i)
                nc.vector.tensor_tensor(wqk[:].rearrange("p h t -> p (h t)"), dexp[:].rearrange("p h t -> p (h t)"),
                                        g.bank[1][:], ALU.mult).then_inc(wqk_ready, 1)
                if i < NT - 1:
                    dve.wait_ge(c_prod, i + 1)
                    if i:
                        dve.wait_ge(c_ready, i)
                    new_state(c_state, i, 6)
                dve.wait_ge(inter_ready, i + 1)
                dve.wait_ge(intra_prod, i + 1)
                for pair in range(2):
                    last = nc.vector.tensor_tensor(num[:, 2 * pair:2 * pair + 2, :].rearrange("p h a -> p (h a)"),
                                                   inter[:, 2 * pair:2 * pair + 2, :].rearrange("p h a -> p (h a)"),
                                                   g.bank[4 + pair][:, 0:2 * A], ALU.add)
                last.then_inc(num_ready, 1)
                dve.wait_ge(num_ready, i + 1)
                link(nc.vector.tensor_scalar(den[:, 0], num[:, :, HD], -1.0, None, ALU.mult))
                link(nc.vector.tensor_tensor(den[:, 1], den[:, 0], num[:, :, HD], ALU.max))
                link(nc.vector.tensor_tensor(den[:, 0], den[:, 1], m.cols[:, E_M, i, :], ALU.max))
                link(nc.vector.reciprocal(den[:, 2], den[:, 0]))
                link(nc.vector.tensor_tensor(hc[:, i, :].rearrange("p (h e) -> p h e", h=H), num[:, :, 0:HD],
                                             den[:, 2].unsqueeze(2).broadcast_to([P, H, HD]), ALU.mult))
                for h in range(H):
                    last = nc.vector.bn_stats(stats[:, i, h, :], hc[:, i, h * P:(h + 1) * P])
                link(last)
                for h in range(H):
                    last = nc.vector.bn_aggr(mv[:, i, h, :], stats[:, i, h, :])
                if i == NT - 1:
                    link(last)
            for b in range(NB):
                dve.wait_ge(c_prod, 8 + b + 1)
                new_state(cs[:, b], 8 + b, (6, 0)[b % 2])
            nc.vector.tensor_scalar(mv[:, :, :, 1:2], mv[:, :, :, 1:2], LN_EPS, None, ALU.add).then_inc(var_ready, 1)
            dve.wait_ge(std_ready, 1)
            link(nc.vector.reciprocal(rstd[:], rstd[:]))
            for i in range(NT):
                for h in range(H):
                    part = hc[:, i, h * P:(h + 1) * P]
                    last = nc.vector.tensor_scalar(part, part, mv[:, i, h, 0:1], rstd[:, i, h, :], ALU.subtract,
                                                   ALU.mult)
                link(last)
                nc.vector.tensor_tensor(hc[:, i, :], hc[:, i, :], m.o_gate[:, i, :], ALU.mult).then_inc(yc_ready, 1)


def stage_mix(nc, g, xT, ybT, ycT, mixT):
    units = [(m, r, c) for m in range(DT) for r in range(3) for c in range(len(CHUNKS))]
    NSET, RING = 4, 4
    with ExitStack() as ctx:
        sem = ctx.enter_context(stage_semaphores(nc))
        def sb(name, shape):
            return ctx.enter_context(nc.sbuf_tensor(name, shape, F32))

        yaT = sb("yaT", [P, DT, T])
        wg = sb("w_gates", [P, 2, 3, DT, P])
        wp = sb("w_proj", [P, 2, 2 * DT, P])
        sig = sb("gate_sigmoid", [P, RING, 512])
        ya_in = sem("x_ya_in")
        w_in = [sem("x_w_in0"), sem("x_w_in1")]
        prod = sem("x_prod")
        sig_ready = sem("x_sig_ready")
        mul_ready = sem("x_mul_ready")
        add_ready = sem("x_add_ready")
        block = ctx.enter_context(nc.Block())
        PER = 3 * len(CHUNKS)
        SRC = ((yaT, 0, DT), (ybT, DT, H), (ycT, DT + H, H))

        def adds(n):
            return sum(r > 0 for _, r, _ in units[:n])

        @block.sync
        def _(sp):
            w_in_t = g.w_in[0].rearrange("(k p) n -> p k n", p=P)
            for m in range(DT):
                s, cols = m % 2, slice(m * P, (m + 1) * P)
                if m >= 2:
                    sp.wait_ge(prod, PER * (m - 1))
                for r in range(3):
                    sp.dma_start(wg[:, s, r], w_in_t[:, :, O_MG + r * D + m * P:O_MG + r * D + (m + 1) * P]
                                 ).then_inc(w_in[s], 16)
                for w, lo, k in ((g.w_pa, 0, DT), (g.w_pb, DT, H), (g.w_pc, DT + H, H)):
                    sp.dma_start(wp[:, s, lo:lo + k, :], w[0].rearrange("(k p) n -> p k n", p=P)[:, :, cols]
                                 ).then_inc(w_in[s], 16)
                if m == 0:
                    sp.dma_start(yaT[:], g.yaT_d.rearrange("k p t -> p k t")).then_inc(ya_in, 16)

        @block.tensor
        def _(pe):
            for n, (m, r, c) in enumerate(units):
                lo, hi = CHUNKS[c]
                if n % PER == 0:
                    pe.wait_ge(w_in[m % 2], 16 * 6 * (m // 2 + 1))
                if n >= NSET:
                    pe.wait_ge(mul_ready, n - NSET + 1)
                gate, proj = g.bank[2 * (n % NSET)][:, 0:hi - lo], g.bank[2 * (n % NSET) + 1][:, 0:hi - lo]
                for k in range(DT):
                    nc.tensor.matmul(gate, wg[:, m % 2, r, k, :], xT[:, k, lo:hi], start=(k == 0),
                                     stop=(k == DT - 1))
                if n == 0:
                    pe.wait_ge(ya_in, 16)
                src, off, kn = SRC[r]
                for k in range(kn):
                    last = nc.tensor.matmul(proj, wp[:, m % 2, off + k, :], src[:, k, lo:hi], start=(k == 0),
                                            stop=(k == kn - 1))
                last.then_inc(prod, 1)

        @block.scalar
        def _(act):
            for n, (m, r, c) in enumerate(units):
                lo, hi = CHUNKS[c]
                act.wait_ge(prod, n + 1)
                if n >= RING:
                    act.wait_ge(mul_ready, n - RING + 1)
                    if adds(n - RING + 1):
                        act.wait_ge(add_ready, adds(n - RING + 1))
                nc.scalar.activation(sig[:, n % RING, 0:hi - lo], g.bank[2 * (n % NSET)][:, 0:hi - lo], ACT.Sigmoid,
                                     bias=g.vec[:, V_BMG + r * DT + m:V_BMG + r * DT + m + 1]).then_inc(sig_ready, 1)

        @block.vector
        def _(dve):
            for n, (m, r, c) in enumerate(units):
                lo, hi = CHUNKS[c]
                dve.wait_ge(sig_ready, n + 1)
                part = sig[:, n % RING, 0:hi - lo]
                nc.vector.tensor_tensor(mixT[:, m, lo:hi] if r == 0 else part, part,
                                        g.bank[2 * (n % NSET) + 1][:, 0:hi - lo], ALU.mult).then_inc(mul_ready, 1)

        @block.gpsimd
        def _(pool):
            for n, (m, r, c) in enumerate(units):
                lo, hi = CHUNKS[c]
                if r:
                    pool.wait_ge(mul_ready, n + 1)
                    if adds(n):
                        pool.wait_ge(add_ready, adds(n))
                    pool.tensor_tensor(mixT[:, m, lo:hi], mixT[:, m, lo:hi], sig[:, n % RING, 0:hi - lo],
                                       ALU.add).then_inc(add_ready, 1)


def stage_out(nc, g, mixT, x1T):
    R = 3
    with ExitStack() as ctx:
        sem = ctx.enter_context(stage_semaphores(nc))
        def sb(name, shape):
            return ctx.enter_context(nc.sbuf_tensor(name, shape, F32))

        w = sb("w_out_sb", [P, DT, D])
        x = sb("x_residual", [P, R, D])
        norm = sb("ln1_scale_shift", [P, 2, D])
        zero = sb("zero_row", [1, D])
        stats = sb("ln1_stats", [P, R, 2, 6])
        mv = sb("ln1_mean_var", [P, R, 2])
        w_in = [sem("o_w_in0"), sem("o_w_in1")]
        x_in = [sem(f"o_x_in{i}") for i in range(R)]
        norm_in = sem("o_norm_in")
        prod = sem("o_prod")
        sum_ready = sem("o_sum_ready")
        stat_ready = sem("o_stat_ready")
        var_ready = sem("o_var_ready")
        std_ready = sem("o_std_ready")
        rstd_ready = sem("o_rstd_ready")
        hat_ready = sem("o_hat_ready")
        scaled = sem("o_scaled")
        x1_ready = sem("o_x1_ready")
        x1_out = [sem(f"o_x1_out{i}") for i in range(R)]
        turned = sem("o_turned")
        moved = sem("o_moved")
        zero_ready = sem("o_zero_ready")
        zero_out = sem("o_zero_out")
        block = ctx.enter_context(nc.Block())

        @block.sync
        def _(sp):
            wv = g.w_out[0].rearrange("(k p) n -> p k n", p=P)
            xp = g.x_prompt[0].rearrange("(i p) d -> i p d", p=P)
            for half in range(2):
                sp.dma_start(w[:, :, half * 512:(half + 1) * 512], wv[:, :, half * 512:(half + 1) * 512]
                             ).then_inc(w_in[half], 16)
            for i in range(NT):
                if i >= R:
                    sp.wait_ge(x1_out[i % R], 16 * (i // R))
                    sp.wait_ge(turned, 2 * (i - R + 1))
                src = xp[i] if i < NT - 1 else g.x_sample.rearrange("b t d -> (b t) d")
                sp.dma_start(x[:, i % R, :], src).then_inc(x_in[i % R], 16)
                if i == 0:
                    for a, v in enumerate((g.ln1_g, g.ln1_b)):
                        sp.dma_start(norm[:, a, :], v.broadcast_to([P, D])).then_inc(norm_in, 16)

        @block.tensor
        def _(pe):
            def turn(i):
                pe.wait_ge(x1_ready, i + 1)
                for half in range(2):
                    n = 2 * i + half
                    if n >= 4:
                        pe.wait_ge(moved, n - 3)
                    for k in range(4):
                        last = nc.tensor.transpose(g.bank[4 + n % 4][:, k * P:(k + 1) * P],
                                                   x[:, i % R, (4 * half + k) * P:(4 * half + k + 1) * P], g.ident[:])
                    last.then_inc(turned, 1)

            for i in range(NT + 2):
                if i < NT:
                    for half in range(2):
                        n = 2 * i + half
                        pe.wait_ge(w_in[half], 16)
                        if n >= 4:
                            pe.wait_ge(sum_ready, n - 3)
                        for k in range(DT):
                            last = nc.tensor.matmul(g.bank[n % 4][:], mixT[:, k, i * P:(i + 1) * P],
                                                    w[:, k, half * 512:(half + 1) * 512], start=(k == 0),
                                                    stop=(k == DT - 1))
                        last.then_inc(prod, 1)
                if i >= 2:
                    turn(i - 2)

        @block.vector
        def _(dve):
            for i in range(NT):
                s = i % R
                dve.wait_ge(x_in[s], 16 * (i // R + 1))
                for half in range(2):
                    n = 2 * i + half
                    part = x[:, s, half * 512:(half + 1) * 512]
                    dve.wait_ge(prod, n + 1)
                    nc.vector.scalar_tensor_tensor(out=part, in0=part, scalar=ALPHA, in1=g.bank[n % 4][:],
                                                   op0=ALU.mult, op1=ALU.add).then_inc(sum_ready, 1)
                for half in range(2):
                    dve.wait_ge(sum_ready, 2 * i + half + 1)
                    nc.vector.bn_stats(stats[:, s, half, :], x[:, s, half * 512:(half + 1) * 512]
                                       ).then_inc(stat_ready, 1)
                dve.wait_ge(stat_ready, 2 * i + 2)
                nc.vector.bn_aggr(mv[:, s, :], stats[:, s].rearrange("p a b -> p (a b)")).then_inc(var_ready, 1)
                dve.wait_ge(std_ready, i + 1)
                nc.vector.reciprocal(mv[:, s, 1:2], mv[:, s, 1:2]).then_inc(rstd_ready, 1)
                dve.wait_ge(rstd_ready, i + 1)
                nc.vector.tensor_scalar(x[:, s, :], x[:, s, :], mv[:, s, 0:1], mv[:, s, 1:2], ALU.subtract,
                                        ALU.mult).then_inc(hat_ready, 1)

        @block.scalar
        def _(act):
            def move(i):
                for half in range(2):
                    n = 2 * i + half
                    act.wait_ge(turned, n + 1)
                    nc.scalar.copy(x1T[:, 4 * half:4 * half + 4, i * P:(i + 1) * P],
                                   g.bank[4 + n % 4][:].rearrange("p (k t) -> p k t", k=4)).then_inc(moved, 1)

            for i in range(NT + 1):
                if i < NT:
                    act.wait_ge(var_ready, i + 1)
                    nc.scalar.activation(mv[:, i % R, 1:2], mv[:, i % R, 1:2], ACT.Sqrt,
                                         bias=g.eps[:]).then_inc(std_ready, 1)
                if i >= 1:
                    act.wait_ge(x1_ready, i)
                    act.dma_start(g.x1_d[(i - 1) * P:i * P, :], x[:, (i - 1) % R, :]).then_inc(x1_out[(i - 1) % R], 16)
                if i >= 2:
                    move(i - 2)
            move(NT - 1)
            act.wait_ge(zero_ready, 1)
            act.dma_start(g.x1_d[T:T + 1, :], zero[:]).then_inc(zero_out, 16)
            for s in x1_out:
                act.wait_ge(s, 16 * (NT // R))
            act.wait_ge(zero_out, 16)

        @block.gpsimd
        def _(pool):
            pool.memset(zero[:], 0.0).then_inc(zero_ready, 1)
            pool.wait_ge(norm_in, 32)
            for i in range(NT):
                pool.wait_ge(hat_ready, i + 1)
                pool.tensor_tensor(x[:, i % R, :], x[:, i % R, :], norm[:, 0, :], ALU.mult).then_inc(scaled, 1)
                pool.wait_ge(scaled, i + 1)
                pool.tensor_tensor(x[:, i % R, :], x[:, i % R, :], norm[:, 1, :], ALU.add).then_inc(x1_ready, 1)


def stage_route(nc, g, x1T):
    R = 3
    with ExitStack() as ctx:
        sem = ctx.enter_context(stage_semaphores(nc))
        def sb(name, shape, dt=F32):
            return ctx.enter_context(nc.sbuf_tensor(name, shape, dt))

        rw = sb("router_w_sb", [P, DT, NE])
        rb = sb("router_bias", [P, NE])
        lg = sb("logits", [P, NT, NE])
        top = sb("top8", [P, NT, 8])
        top_i = sb("top8_index", [P, NT, 8], U32)
        top_f = sb("top8_index_f", [P, NT, TOPK])
        eid = sb("expert_ids", [P, NE])
        one_hot = sb("one_hot", [P, NT, TOPK, NE])
        picked = sb("picked", [P, NT, NE])
        rank = sb("rank", [P, NT, NE])
        before = sb("picked_before_tile", [P, NT + 1, NE])
        blocks = sb("blocks", [P, 4, NE])
        gsum = sb("gate_sum", [P, NT, 1])
        dest_f = sb("dest_f", [P, NT * TOPK])
        bid = sb("block_ids", [P, NBLK])
        cmp = sb("block_compare", [P, NBLK, NE])
        ctl_f = sb("control_f", [P, 1 + NBLK])
        code = sb("pick_codes", [P, NT, TOPK], I32)
        dest = sb("pick_slots", [P, NT * TOPK], I32)
        fill = sb("unused_slots", [P, (NSLOT + 2 * SLOTS) // 64], I32)
        wg = sb("ple_gate_w_sb", [P, DT, D])
        wp = sb("ple_w_sb", [P, 2, D])
        bg = sb("ple_gate_bias", [P, D])
        p_tok = sb("p_tokens", [P, NT, PLE])
        pT = sb("pT", [P, 2, T])
        x1 = sb("x1_rows", [P, R, D])
        t = sb("ple_work", [P, 3, 512])
        rw_in = sem("t_rw_in")
        w_in = sem("t_w_in")
        p_in = sem("t_p_in")
        x1_in = [sem(f"t_x1_in{i}") for i in range(R)]
        ids_ready = sem("t_ids_ready")
        fill_out = sem("t_fill_out")
        logit_prod = sem("t_logit_prod")
        step = sem("t_step")
        picked_ready = sem("t_picked_ready")
        rank_prod = sem("t_rank_prod")
        diff_ready = sem("t_diff_ready")
        gate_exp = sem("t_gate_exp")
        dest_ready = sem("t_dest_ready")
        scattered = sem("t_scattered")
        p_turned = sem("t_p_turned")
        p_moved = sem("t_p_moved")
        prod = sem("t_prod")
        biased = sem("t_biased")
        sig_ready = sem("t_sig_ready")
        mul_ready = sem("t_mul_ready")
        res_ready = sem("t_res_ready")
        res_out = [sem(f"t_res_out{i}") for i in range(R)]
        block = ctx.enter_context(nc.Block())
        units = [(i, half) for i in range(NT) for half in range(2)]

        @block.sync
        def _(sp):
            sp.dma_start(rw[:], g.router_w[0].rearrange("(k p) e -> p k e", p=P)).then_inc(rw_in, 16)
            sp.dma_start(rb[:], g.router_b.broadcast_to([P, NE])).then_inc(rw_in, 16)
            sp.dma_start(p_tok[:, 0:NT - 1, :], g.p_prompt[0, 0].rearrange("(i p) d -> p i d", p=P)
                         ).then_inc(p_in, 16)
            sp.dma_start(p_tok[:, NT - 1, :], g.p_sample[0].rearrange("b t d -> (b t) d")).then_inc(p_in, 16)
            sp.dma_start(wg[:], g.ple_gate_w[0].rearrange("(k p) n -> p k n", p=P)).then_inc(w_in, 16)
            sp.dma_start(wp[:], g.ple_w[0].rearrange("(k p) n -> p k n", p=P)).then_inc(w_in, 16)
            sp.dma_start(bg[:], g.ple_gate_b.broadcast_to([P, D])).then_inc(w_in, 16)
            sp.wait_ge(ids_ready, 1)
            sp.dma_start(g.table_d.rearrange("(p c) o -> p (c o)", p=64), fill[0:64, :]).then_inc(fill_out, 16)
            for i in range(NT):
                if i >= R:
                    sp.wait_ge(res_out[i % R], 16 * (i // R))
                sp.dma_start(x1[:, i % R, :], g.x1_d[i * P:(i + 1) * P, :]).then_inc(x1_in[i % R], 16)

        @block.gpsimd
        def _(pool):
            pool.memset(fill[:], T * TOPK).then_inc(ids_ready, 1)
            pool.iota(code[:], pattern=[[P * TOPK, NT], [1, TOPK]], base=0, channel_multiplier=TOPK)
            pool.iota(eid[:], pattern=[[1, NE]], base=0, channel_multiplier=0, allow_small_or_imprecise_dtypes=True)
            pool.iota(bid[:], pattern=[[1, NBLK]], base=0, channel_multiplier=0,
                      allow_small_or_imprecise_dtypes=True).then_inc(ids_ready, 1)
            pool.wait_ge(fill_out, 16)
            pool.wait_ge(ids_ready, 2)
            pool.wait_ge(dest_ready, 1)
            for i in range(NT):
                for k in range(TOPK):
                    c = i * TOPK + k
                    pool.indirect_dma_start(
                        out=g.table_d, out_offset=bass.IndirectOffsetOnAxis(ap=dest[:, c:c + 1], axis=0),
                        in_=code[:, i, k:k + 1], in_offset=None).then_inc(scattered, 16)
            pool.wait_ge(scattered, 16 * NT * TOPK)

        @block.tensor
        def _(pe):
            pe.wait_ge(rw_in, 32)
            for i in range(NT):
                for k in range(DT):
                    last = nc.tensor.matmul(g.bank[0][:, i * NE:(i + 1) * NE], x1T[:, k, i * P:(i + 1) * P],
                                            rw[:, k, :], start=(k == 0), stop=(k == DT - 1))
            last.then_inc(logit_prod, 1)
            pe.wait_ge(p_in, 32)
            for i in range(NT):
                if i >= 4:
                    pe.wait_ge(p_moved, i // 2 - 1)
                for k in range(2):
                    last = nc.tensor.transpose(g.bank[6 + i // 2 % 2][:, (k * 2 + i % 2) * P:(k * 2 + i % 2 + 1) * P],
                                               p_tok[:, i, k * P:(k + 1) * P], g.ident[:])
                if i % 2 or i == NT - 1:
                    last.then_inc(p_turned, 1)
            pe.wait_ge(w_in, 48)
            pe.wait_ge(p_moved, 5)
            for n, (i, half) in enumerate(units):
                if n == 6:
                    pe.wait_ge(picked_ready, 1)
                    nc.tensor.matmul(g.bank[0][:, 0:NT * NE], g.tri_before[:], picked[:].rearrange("p i e -> p (i e)"),
                                     start=True, stop=True).then_inc(rank_prod, 1)
                    nc.tensor.matmul(g.bank[1][:, 0:NT * NE], g.ones[:], picked[:].rearrange("p i e -> p (i e)"),
                                     start=True, stop=True).then_inc(rank_prod, 1)
                if n >= 3:
                    pe.wait_ge(mul_ready, n - 2)
                gate, proj = g.bank[2 + 2 * (n % 3)], g.bank[3 + 2 * (n % 3)]
                cols = slice(half * 512, (half + 1) * 512)
                for k in range(DT):
                    nc.tensor.matmul(gate[:], x1T[:, k, i * P:(i + 1) * P], wg[:, k, cols], start=(k == 0),
                                     stop=(k == DT - 1))
                for k in range(2):
                    last = nc.tensor.matmul(proj[:], pT[:, k, i * P:(i + 1) * P], wp[:, k, cols], start=(k == 0),
                                            stop=(k == 1))
                last.then_inc(prod, 1)

        @block.scalar
        def _(act):
            for c in range(5):
                n = min(2, NT - 2 * c)
                act.wait_ge(p_turned, c + 1)
                nc.scalar.copy(pT[:, :, 2 * c * P:(2 * c + n) * P],
                               g.bank[6 + c % 2][:].rearrange("p (k t) -> p k t", k=2)[:, :, 0:n * P]
                               ).then_inc(p_moved, 1)
            act.wait_ge(diff_ready, 1)
            nc.scalar.activation(g.gates[:], g.gates[:], ACT.Exp).then_inc(gate_exp, 1)
            for n, (i, half) in enumerate(units):
                act.wait_ge(biased, n + 1)
                nc.scalar.activation(t[:, n % 3, :], t[:, n % 3, :], ACT.Sigmoid).then_inc(sig_ready, 1)
                if half:
                    act.wait_ge(res_ready, n + 1)
                    act.dma_start(g.residual_d[i], x1[:, i % R, :]).then_inc(res_out[i % R], 16)
            for s in res_out:
                act.wait_ge(s, 16 * (NT // R))

        @block.vector
        def _(dve):
            count = [0]

            def link(ins):
                count[0] += 1
                ins.then_inc(step, 1)
                dve.wait_ge(step, count[0])

            def add_bias(n):
                half = n % 2
                if n == 0:
                    dve.wait_ge(w_in, 48)
                dve.wait_ge(prod, n + 1)
                nc.vector.tensor_tensor(t[:, n % 3, :], g.bank[2 + 2 * (n % 3)][:],
                                        bg[:, half * 512:(half + 1) * 512], ALU.add).then_inc(biased, 1)

            def add_residual(n):
                i, half = units[n]
                dve.wait_ge(sig_ready, n + 1)
                nc.vector.tensor_tensor(t[:, n % 3, :], t[:, n % 3, :], g.bank[3 + 2 * (n % 3)][:],
                                        ALU.mult).then_inc(mul_ready, 1)
                dve.wait_ge(mul_ready, n + 1)
                dve.wait_ge(x1_in[i % R], 16 * (i // R + 1))
                part = x1[:, i % R, half * 512:(half + 1) * 512]
                nc.vector.scalar_tensor_tensor(out=part, in0=part, scalar=ALPHA, in1=t[:, n % 3, :], op0=ALU.mult,
                                               op1=ALU.add).then_inc(res_ready, 1)

            def pick():
                dve.wait_ge(logit_prod, 1)
                link(nc.vector.tensor_tensor(lg[:], g.bank[0][:, 0:NT * NE].rearrange("p (i e) -> p i e", i=NT),
                                             rb[:].unsqueeze(1).broadcast_to([P, NT, NE]), ALU.add))
                for i in range(NT):
                    last = nc.vector.max(top[:, i, :], lg[:, i, :])
                link(last)
                for i in range(NT):
                    last = nc.vector.max_index(top_i[:, i, :], top[:, i, :], lg[:, i, :])
                link(last)
                link(nc.vector.tensor_copy(top_f[:], top_i[:, :, 0:TOPK]))
                nc.vector.tensor_tensor(g.gates[:].rearrange("p (i k) -> p i k", k=TOPK), top[:, :, 0:TOPK],
                                        top[:, :, 0:1].broadcast_to([P, NT, TOPK]),
                                        ALU.subtract).then_inc(diff_ready, 1)
                dve.wait_ge(ids_ready, 2)
                flat = one_hot[:].rearrange("p i k e -> p (i k) e")
                link(nc.vector.tensor_tensor(flat, eid[:].unsqueeze(1).broadcast_to([P, NT * TOPK, NE]),
                                             top_f[:].rearrange("p i k -> p (i k)").unsqueeze(2).broadcast_to(
                                                 [P, NT * TOPK, NE]), ALU.is_equal))
                link(nc.vector.tensor_tensor(picked[:], one_hot[:, :, 0, :], one_hot[:, :, 1, :], ALU.add))
                link(nc.vector.tensor_tensor(picked[:], picked[:], one_hot[:, :, 2, :], ALU.add))
                nc.vector.tensor_tensor(picked[:], picked[:], one_hot[:, :, 3, :], ALU.add).then_inc(picked_ready, 1)
                dve.wait_ge(gate_exp, 1)
                gv = g.gates[:].rearrange("p (i k) -> p i k", k=TOPK)
                link(nc.vector.tensor_reduce(gsum[:], gv, AX_X, ALU.add))
                link(nc.vector.reciprocal(gsum[:], gsum[:]))
                nc.vector.tensor_tensor(gv, gv, gsum[:].broadcast_to([P, NT, TOPK]), ALU.mult)

            def place():
                dve.wait_ge(rank_prod, 2)
                link(nc.vector.memset(before[:, 0, :], 0.0))
                for i in range(NT):
                    link(nc.vector.tensor_tensor(before[:, i + 1, :], before[:, i, :],
                                                 g.bank[1][:, i * NE:(i + 1) * NE], ALU.add))
                link(nc.vector.tensor_tensor(rank[:], before[:, 0:NT, :],
                                             g.bank[0][:, 0:NT * NE].rearrange("p (i e) -> p i e", i=NT), ALU.add))
                nblk, upto, base, one = (blocks[:, a, :] for a in range(4))
                count_e = before[:, NT, :]
                link(nc.vector.memset(one, 1.0))
                link(nc.vector.tensor_scalar(nblk, count_e, 0.0, None, ALU.is_gt))
                for j in range(1, T // SLOTS):
                    link(nc.vector.scalar_tensor_tensor(out=nblk, in0=count_e, scalar=float(j * SLOTS), in1=nblk,
                                                        op0=ALU.is_gt, op1=ALU.add))
                link(nc.vector.tensor_tensor_scan(upto, one, nblk, 0.0, ALU.mult, ALU.add))
                link(nc.vector.tensor_tensor(base, upto, nblk, ALU.subtract))
                link(nc.vector.tensor_scalar(base, base, float(SLOTS), None, ALU.mult))
                link(nc.vector.tensor_tensor(rank[:], rank[:], base.unsqueeze(1).broadcast_to([P, NT, NE]), ALU.add))
                for k in range(TOPK):
                    last = nc.vector.tensor_tensor(one_hot[:, :, k, :], one_hot[:, :, k, :], rank[:], ALU.mult)
                link(last)
                link(nc.vector.tensor_reduce(dest_f[:], one_hot[:].rearrange("p i k e -> p (i k) e"), AX_X, ALU.add))
                nc.vector.tensor_copy(dest[:], dest_f[:]).then_inc(dest_ready, 1)
                link(nc.vector.tensor_tensor(cmp[:], upto.unsqueeze(1).broadcast_to([P, NBLK, NE]),
                                             bid[:].unsqueeze(2).broadcast_to([P, NBLK, NE]), ALU.is_le))
                link(nc.vector.tensor_reduce(ctl_f[:, 1:], cmp[:], AX_X, ALU.add))
                link(nc.vector.tensor_scalar(ctl_f[:, 1:], ctl_f[:, 1:], float(NE - 1), None, ALU.min))
                link(nc.vector.tensor_scalar(bid[:, 0::2], bid[:, 0::2], upto[:, NE - 1:NE], None, ALU.is_lt))
                link(nc.vector.tensor_reduce(ctl_f[:, 0:1], bid[:, 0::2], AX_X, ALU.add))
                link(nc.vector.tensor_copy(g.ctl[:], ctl_f[:]))

            pick()
            for n in range(len(units) + 1):
                if n < len(units):
                    add_bias(n)
                if n == 7:
                    place()
                if n:
                    add_residual(n - 1)


def stage_experts(nc, g):
    S0, S1 = P, SLOTS - P
    ROWS = ((0, S0), (S0, S1))
    HF = FF // 2
    with ExitStack() as ctx:
        sem = ctx.enter_context(stage_semaphores(nc))
        def sb(name, shape, dt=F32):
            return ctx.enter_context(nc.sbuf_tensor(name, shape, dt))

        w1 = sb("expert_w1", [P, 2, DT, 2, HF])
        w2 = sb("expert_w2", [P, FT, D])
        w1_lo = sb("expert_w1_low", [P, 2, DT, 2, HF], F32R)
        w2_lo = sb("expert_w2_low", [P, FT, D], F32R)
        w1_hi = sb("expert_w1_high", [P, 2, DT, 2, HF], F32R)
        w2_hi = sb("expert_w2_high", [P, FT, D], F32R)
        b2 = sb("expert_b2", [P, 2, D])
        b1_rows = sb("expert_b1_rows", [P, 2, P])
        b1T = sb("expert_b1T", [P, NE, DT])
        b1 = sb("expert_b1", [P, 2, DT])
        code = sb("slot_codes", [P, 2], I32)
        out_code = sb("slot_codes_out", [P, 2, 2], I32)
        idx = sb("slot_tokens", [P, 2], I32)
        xg = sb("slot_rows", [P, 2, D])
        xT_hi = sb("slot_rowsT_high", [P, 2, DT, SLOTS], F32R)
        xT_lo = sb("slot_rowsT_low", [P, 2, DT, SLOTS], F32R)
        gt = sb("gate_part", [P, 2, SLOTS])
        up = sb("up_part", [P, 2, SLOTS])
        sg = sb("gate_sigmoid_e", [P, 2, SLOTS])
        act_t = sb("expert_act", [P, 2, SLOTS])
        act_hi = sb("expert_act_high", [P, FT, SLOTS], F32R)
        act_lo = sb("expert_act_low", [P, FT, SLOTS], F32R)
        y = sb("expert_y", [P, 2, D])
        b1_in = sem("e_b1_in")
        idx_ready = sem("e_idx_ready")
        codes_kept = sem("e_codes_kept")
        b1_turned = sem("e_b1_turned")
        b1_moved = sem("e_b1_moved")
        b1_picked = sem("e_b1_picked")
        idx_in, xg_in, y_out = (sem(f"e_{n}") for n in ("idx_in", "xg_in", "y_out"))
        w1_in = [sem(f"e_w1_in{pair}") for pair in range(2)]
        w2_in = sem("e_w2_in")
        t_ready = sem("e_t_ready")
        t_high = sem("e_t_high")
        t_moved = sem("e_t_moved")
        w1_high = sem("e_w1_high")
        w1_split = sem("e_w1_split")
        w1_last_split = sem("e_w1_last_split")
        w1_all_split = sem("e_w1_all_split")
        w2_high = sem("e_w2_high")
        w2_split = sem("e_w2_split")
        h_ready = sem("e_h_ready")
        h_free = sem("e_h_free")
        clipped = sem("e_clipped")
        up_step = sem("e_up_step")
        sig_ready = sem("e_sig_ready")
        glu_step = sem("e_glu_step")
        act_ready = sem("e_act_ready")
        act_high = sem("e_act_high")
        act_split = sem("e_act_split")
        y_ready = sem("e_y_ready")
        y_free = sem("e_y_free")
        y_left = sem("e_y_left")
        waits_passed = sem("e_waits_passed")
        block = ctx.enter_context(nc.Block())

        def turns(eng):
            return eng.value_load(g.ctl[0:1, 0:1], min_val=1, max_val=MAXBLK // 2)

        def expert_of(eng, n):
            return eng.value_load(g.ctl[0:1, bass.ds(n + 1, 1)], min_val=0, max_val=NE - 1)

        def w1_chunk(tile, f):
            return tile[:, f // 2, :, :, f % 2 * P:(f % 2 + 1) * P]

        @block.sync
        def _(sp):
            def load_w1(e, pair):
                src = g.exp_w1[0][bass.ds(e, 1)].rearrange("o (k p) n -> p (o k) n", p=P)
                for part in range(2):
                    lo = part * FF + pair * HF
                    sp.dma_start(w1[:, pair, :, part, :], src[:, :, lo:lo + HF]).then_inc(w1_in[pair], 16)

            def load_w2(e):
                sp.dma_start(w2[:], g.exp_w2[0][bass.ds(e, 1)].rearrange("o (k p) n -> p (o k) n", p=P)
                             ).then_inc(w2_in, 16)

            def load_b2(e, par):
                sp.dma_start(b2[:, par, :], g.exp_b2[0][bass.ds(e, 1)].broadcast_to([P, D])).then_inc(w2_in, 16)

            for half in range(2):
                sp.dma_start(b1_rows[:, half, :], g.exp_b1[0].rearrange("e (f p) -> (e f) p", p=P)
                             [half * P:(half + 1) * P, :]).then_inc(b1_in, 16)
            e = expert_of(sp, 0)
            load_w1(e, 0)
            load_w1(e, 1)
            load_w2(e)
            load_b2(e, 0)
            e = expert_of(sp, 1)
            sp.wait_ge(w1_split, 2)
            load_w1(e, 0)
            sp.wait_ge(w1_all_split, 1)
            load_w1(e, 1)
            with sp.Fori(0, turns(sp), 1) as it:
                for par in range(2):
                    n = 2 * it + par
                    e = expert_of(sp, n + 1)
                    sp.wait_ge(w2_split, 4 * n + 4)
                    load_w2(e)
                    sp.wait_ge(y_free, 4 * n + 4)
                    load_b2(e, 1 - par)
                    e = expert_of(sp, n + 2)
                    sp.wait_ge(w1_split, 3 * n + 5)
                    load_w1(e, 0)
                    sp.wait_ge(w1_all_split, n + 2)
                    load_w1(e, 1)

        @block.gpsimd
        def _(pool):
            def wait(semaphore, value):
                pool.wait_ge(semaphore, value)
                pool.nop().then_inc(waits_passed, 1)

            def gather(n):
                for r, (lo, rows) in enumerate(ROWS):
                    pool.dma_start(code[0:rows, r:r + 1],
                                   g.table_d[bass.ds(n * SLOTS + lo, rows)]).then_inc(idx_in, 16)
                wait(idx_in, 32 * n + 32)
                for r, (lo, rows) in enumerate(ROWS):
                    pool.tensor_scalar(idx[0:rows, r:r + 1], code[0:rows, r:r + 1], -1.5, 0.25, ALU.add,
                                       ALU.mult).then_inc(idx_ready, 1)
                wait(idx_ready, 2 * n + 2)
                for r, (lo, rows) in enumerate(ROWS):
                    pool.indirect_dma_start(
                        out=xg[0:rows, r, :], out_offset=None, in_=g.x1_d,
                        in_offset=bass.IndirectOffsetOnAxis(ap=idx[0:rows, r:r + 1], axis=0)
                    ).then_inc(xg_in, 16)

            def keep_codes(n, par):
                for r, (lo, rows) in enumerate(ROWS):
                    pool.tensor_copy(out_code[0:rows, par, r:r + 1], code[0:rows, r:r + 1]).then_inc(codes_kept, 1)
                wait(codes_kept, 2 * n + 2)

            def w1_last_low_part(m):
                wait(w1_high, 4 * m + FT)
                pool.tensor_tensor(w1_chunk(w1_lo, FT - 1), w1_chunk(w1, FT - 1),
                                   w1_chunk(w1_hi, FT - 1).bitcast(F32), ALU.subtract).then_inc(w1_last_split, 1)
                wait(w1_last_split, m + 1)
                wait(w1_split, 3 * m + 3)
                pool.nop().then_inc(w1_all_split, 1)

            pool.nop().then_inc(y_left, 1)
            gather(0)
            pool.wait_ge(t_ready, 4)
            keep_codes(0, 0)
            gather(1)
            w1_last_low_part(0)
            with pool.Fori(0, turns(pool), 1) as it:
                for par in range(2):
                    n = 2 * it + par
                    wait(t_ready, 4 * n + 8)
                    keep_codes(n + 1, 1 - par)
                    gather(n + 2)
                    w1_last_low_part(n + 1)
                    wait(y_free, 4 * n + 8)
                    for r, (lo, rows) in enumerate(ROWS):
                        pool.indirect_dma_start(
                            out=g.y_d, out_offset=bass.IndirectOffsetOnAxis(ap=out_code[0:rows, par, r:r + 1], axis=0),
                            in_=y[0:rows, r, :], in_offset=None, bounds_check=T * TOPK - 1, oob_is_err=False
                        ).then_inc(y_out, 16)
                    wait(y_out, 32 * n + 32)
                    pool.nop().then_inc(y_left, 1)
            last = turns(pool)
            wait(xg_in, 64 * last + 64)
            for pair in range(2):
                wait(w1_in[pair], 64 * last + 64)
            wait(w2_in, 64 * last + 32)

        @block.tensor
        def _(pe):
            def turn_rows(m, q):
                pe.wait_ge(xg_in, 32 * m + 32)
                pe.wait_ge(t_moved, 4 * m + q + 1)
                for k in range(2):
                    for r, (lo, rows) in enumerate(ROWS):
                        f = 2 * q + k
                        last = nc.tensor.transpose(
                            g.bank[q % 2][:, k * SLOTS + lo:k * SLOTS + lo + rows],
                            xg[0:rows, r, f * P:(f + 1) * P], g.ident[0:rows, 0:rows])
                last.then_inc(t_ready, 1)

            for s, credits in ((t_moved, 2), (h_free, 2), (y_free, 4)):
                nc.tensor.nop().then_inc(s, credits)
            pe.wait_ge(b1_in, 32)
            for half in range(2):
                last = nc.tensor.transpose(g.bank[2][:, half * P:(half + 1) * P], b1_rows[:, half, :], g.ident[:])
            last.then_inc(b1_turned, 1)
            pe.wait_ge(b1_moved, 1)
            for q in range(4):
                turn_rows(0, q)
            with pe.Fori(0, turns(pe), 1) as it:
                for par in range(2):
                    n4 = 8 * it + 4 * par
                    for f in range(FT):
                        if f < FT - 1:
                            pe.wait_ge(w1_split, 3 * (2 * it + par) + f + 1)
                        else:
                            pe.wait_ge(w1_last_split, 2 * it + par + 1)
                        pe.wait_ge(h_free, n4 + f + 1)
                        for part in range(2):
                            out = g.bank[2 + f % 2][:, part * SLOTS:(part + 1) * SLOTS]
                            for k in range(DT):
                                if f == 0 and part == 0 and k % 2 == 0:
                                    pe.wait_ge(t_moved, n4 + k // 2 + 3)
                                hi, lo = (w1_chunk(tile, f)[:, k, part, :] for tile in (w1_hi, w1_lo))
                                nc.tensor.matmul(out, hi, xT_hi[:, par, k, :], start=(k == 0), stop=False)
                                nc.tensor.matmul(out, hi, xT_lo[:, par, k, :], start=False, stop=False)
                                last = nc.tensor.matmul(out, lo, xT_hi[:, par, k, :], start=False, stop=(k == DT - 1))
                        last.then_inc(h_ready, 1)
                        turn_rows(2 * it + par + 1, f)
                    outs = [(lo, rows, half) for lo, rows in ROWS for half in range(2)]
                    for f in range(FT):
                        pe.wait_ge(w2_split, n4 + f + 1)
                        pe.wait_ge(act_split, n4 + f + 1)
                        for u, (lo, rows, half) in enumerate(outs):
                            if f == 0:
                                pe.wait_ge(y_free, n4 + u + 1)
                            out, cols = g.bank[4 + u][0:rows, :], slice(half * 512, (half + 1) * 512)
                            a_hi, a_lo = act_hi[:, f, lo:lo + rows], act_lo[:, f, lo:lo + rows]
                            nc.tensor.matmul(out, a_hi, w2_hi[:, f, cols], start=(f == 0), stop=False)
                            nc.tensor.matmul(out, a_hi, w2_lo[:, f, cols], start=False, stop=False)
                            last = nc.tensor.matmul(out, a_lo, w2_hi[:, f, cols], start=False, stop=(f == FT - 1))
                            if f == FT - 1:
                                last.then_inc(y_ready, 1)

        @block.scalar
        def _(act):
            def w1_high_part(f, m):
                act.wait_ge(w1_in[f // 2], 32 * m + 32)
                nc.scalar.copy(w1_chunk(w1_hi, f), w1_chunk(w1, f)).then_inc(w1_high, 1)

            def rows_high_part(par, m, q):
                act.wait_ge(t_ready, 4 * m + q + 1)
                nc.scalar.copy(xT_hi[:, par, 2 * q:2 * q + 2, :].rearrange("p k s -> p (k s)"),
                               g.bank[q % 2][:, 0:2 * SLOTS]).then_inc(t_high, 1)

            for f in range(FT):
                w1_high_part(f, 0)
            for q in range(4):
                rows_high_part(0, 0, q)
            with act.Fori(0, turns(act), 1) as it:
                for par in range(2):
                    n4 = 8 * it + 4 * par
                    for f in range(FT):
                        act.wait_ge(h_ready, n4 + f + 1)
                        act.wait_ge(clipped, n4 + f + 1)
                        nc.scalar.activation(sg[:, f % 2, :], gt[:, f % 2, :], ACT.Sigmoid,
                                             scale=1.702).then_inc(sig_ready, 1)
                        act.wait_ge(w2_in, 32 * (2 * it + par) + 32)
                        nc.scalar.copy(w2_hi[:, f, :], w2[:, f, :]).then_inc(w2_high, 1)
                        act.wait_ge(act_ready, n4 + f + 1)
                        nc.scalar.copy(act_hi[:, f, :], act_t[:, f % 2, :]).then_inc(act_high, 1)
                        rows_high_part(1 - par, 2 * it + par + 1, f)
                        w1_high_part(f, 2 * it + par + 1)

        @block.vector
        def _(dve):
            def w1_low_part(f, m4):
                dve.wait_ge(w1_high, m4 + f + 1)
                nc.vector.tensor_tensor(w1_chunk(w1_lo, f), w1_chunk(w1, f), w1_chunk(w1_hi, f).bitcast(F32),
                                        ALU.subtract).then_inc(w1_split, 1)

            def rows_low_part(par, m, q):
                dve.wait_ge(t_high, 4 * m + q + 1)
                hi, lo = (t[:, par, 2 * q:2 * q + 2, :].rearrange("p k s -> p (k s)") for t in (xT_hi, xT_lo))
                nc.vector.tensor_tensor(lo, g.bank[q % 2][:, 0:2 * SLOTS], hi.bitcast(F32),
                                        ALU.subtract).then_inc(t_moved, 1)

            dve.wait_ge(b1_turned, 1)
            nc.vector.tensor_copy(b1T[:].rearrange("p e f -> p (e f)"), g.bank[2][:, 0:2 * P]).then_inc(b1_moved, 1)
            dve.wait_ge(b1_moved, 1)
            for f in range(FT - 1):
                w1_low_part(f, 0)
            for q in range(4):
                rows_low_part(0, 0, q)
            with dve.Fori(0, turns(dve), 1) as it:
                for par in range(2):
                    n4 = 8 * it + 4 * par
                    e = expert_of(dve, 2 * it + par)
                    nc.vector.tensor_copy(b1[:, par, :], b1T[:, bass.ds(e, 1), :].rearrange("p o f -> p (o f)")
                                          ).then_inc(b1_picked, 1)
                    dve.wait_ge(b1_picked, 2 * it + par + 1)
                    for f in range(FT):
                        s = f % 2
                        dve.wait_ge(h_ready, n4 + f + 1)
                        nc.vector.tensor_scalar(gt[:, s, :], g.bank[2 + s][:, 0:SLOTS], b1[:, par, f:f + 1], 7.0,
                                                ALU.add, ALU.min).then_inc(clipped, 1)
                        nc.vector.tensor_scalar(up[:, s, :], g.bank[2 + s][:, SLOTS:2 * SLOTS],
                                                b1[:, par, FT + f:FT + f + 1], 7.0, ALU.add, ALU.min
                                                ).then_inc(h_free, 1)
                        dve.wait_ge(h_free, n4 + f + 3)
                        nc.vector.tensor_scalar(up[:, s, :], up[:, s, :], -7.0, 1.0, ALU.max, ALU.add
                                                ).then_inc(up_step, 1)
                        dve.wait_ge(up_step, n4 + f + 1)
                        nc.vector.tensor_tensor(up[:, s, :], up[:, s, :], gt[:, s, :], ALU.mult).then_inc(glu_step, 1)
                        dve.wait_ge(glu_step, n4 + f + 1)
                        dve.wait_ge(sig_ready, n4 + f + 1)
                        nc.vector.tensor_tensor(act_t[:, s, :], up[:, s, :], sg[:, s, :],
                                                ALU.mult).then_inc(act_ready, 1)
                        dve.wait_ge(w2_high, n4 + f + 1)
                        nc.vector.tensor_tensor(w2_lo[:, f, :], w2[:, f, :],
                                                w2_hi[:, f, :].bitcast(F32), ALU.subtract).then_inc(w2_split, 1)
                        dve.wait_ge(act_high, n4 + f + 1)
                        nc.vector.tensor_tensor(act_lo[:, f, :], act_t[:, s, :], act_hi[:, f, :].bitcast(F32),
                                                ALU.subtract).then_inc(act_split, 1)
                        rows_low_part(1 - par, 2 * it + par + 1, f)
                    for f in range(FT - 1):
                        w1_low_part(f, n4 + 4)
                    dve.wait_ge(y_left, 2 * it + par + 1)
                    for u in range(4):
                        lo, rows = ROWS[u // 2]
                        half = u % 2
                        dve.wait_ge(y_ready, n4 + u + 1)
                        cols = slice(half * 512, (half + 1) * 512)
                        nc.vector.tensor_tensor(y[0:rows, u // 2, cols], g.bank[4 + u][0:rows, :],
                                                b2[0:rows, par, cols], ALU.add).then_inc(y_free, 1)


def stage_combine(nc, g):
    R = 3
    with ExitStack() as ctx:
        sem = ctx.enter_context(stage_semaphores(nc))
        def sb(name, shape):
            return ctx.enter_context(nc.sbuf_tensor(name, shape, F32))

        res = sb("residual", [P, R, D])
        rows = sb("expert_rows", [P, R, TOPK, D])
        norm = sb("ln2_scale_shift", [P, 2, D])
        stats = sb("ln2_stats", [P, R, 2, 6])
        mv = sb("ln2_mean_var", [P, R, 2])
        norm_in = sem("k_norm_in")
        res_in = [sem(f"k_res_in{i}") for i in range(R)]
        rows_in = [sem(f"k_rows_in{i}") for i in range(R)]
        added = sem("k_added")
        stat_ready = sem("k_stat_ready")
        var_ready = sem("k_var_ready")
        std_ready = sem("k_std_ready")
        rstd_ready = sem("k_rstd_ready")
        hat_ready = sem("k_hat_ready")
        scaled = sem("k_scaled")
        y_ready = sem("k_y_ready")
        y_out = [sem(f"k_y_out{i}") for i in range(R)]
        block = ctx.enter_context(nc.Block())

        @block.sync
        def _(sp):
            for i in range(NT):
                if i >= R:
                    sp.wait_ge(y_out[i % R], 16 * (i // R))
                sp.dma_start(res[:, i % R, :], g.residual_d[i]).then_inc(res_in[i % R], 16)
                sp.dma_start(rows[:, i % R], g.y_d[i * P * TOPK:(i + 1) * P * TOPK, :].rearrange(
                    "(p k) d -> p k d", k=TOPK)).then_inc(rows_in[i % R], 16)
                if i == 0:
                    for a, v in enumerate((g.ln2_g, g.ln2_b)):
                        sp.dma_start(norm[:, a, :], v.broadcast_to([P, D])).then_inc(norm_in, 16)

        @block.vector
        def _(dve):
            dve.wait_ge(norm_in, 32)
            for i in range(NT):
                s = i % R
                dve.wait_ge(res_in[s], 16 * (i // R + 1))
                dve.wait_ge(rows_in[s], 16 * (i // R + 1))
                for k in range(TOPK):
                    c = i * TOPK + k
                    nc.vector.scalar_tensor_tensor(out=res[:, s, :], in0=rows[:, s, k, :], scalar=g.gates[:, c:c + 1],
                                                   in1=res[:, s, :], op0=ALU.mult, op1=ALU.add).then_inc(added, 1)
                    dve.wait_ge(added, TOPK * i + k + 1)
                for half in range(2):
                    nc.vector.bn_stats(stats[:, s, half, :], res[:, s, half * 512:(half + 1) * 512]
                                       ).then_inc(stat_ready, 1)
                dve.wait_ge(stat_ready, 2 * i + 2)
                nc.vector.bn_aggr(mv[:, s, :], stats[:, s].rearrange("p a b -> p (a b)")).then_inc(var_ready, 1)
                dve.wait_ge(std_ready, i + 1)
                nc.vector.reciprocal(mv[:, s, 1:2], mv[:, s, 1:2]).then_inc(rstd_ready, 1)
                dve.wait_ge(rstd_ready, i + 1)
                nc.vector.tensor_scalar(res[:, s, :], res[:, s, :], mv[:, s, 0:1], mv[:, s, 1:2], ALU.subtract,
                                        ALU.mult).then_inc(hat_ready, 1)
                dve.wait_ge(hat_ready, i + 1)
                nc.vector.tensor_tensor(res[:, s, :], res[:, s, :], norm[:, 0, :], ALU.mult).then_inc(scaled, 1)
                dve.wait_ge(scaled, i + 1)
                nc.vector.tensor_tensor(res[:, s, :], res[:, s, :], norm[:, 1, :], ALU.add).then_inc(y_ready, 1)

        @block.scalar
        def _(act):
            yp = g.o_y_p[0].rearrange("(i p) d -> i p d", p=P)
            for i in range(NT):
                act.wait_ge(var_ready, i + 1)
                nc.scalar.activation(mv[:, i % R, 1:2], mv[:, i % R, 1:2], ACT.Sqrt,
                                     bias=g.eps[:]).then_inc(std_ready, 1)
                act.wait_ge(y_ready, i + 1)
                dst = yp[i] if i < NT - 1 else g.o_y_s.rearrange("b t d -> (b t) d")
                act.dma_start(dst, res[:, i % R, :]).then_inc(y_out[i % R], 16)
            for s in y_out:
                act.wait_ge(s, 16 * (NT // R))


def build_program(nc, i, o):
    g = Shared()
    (g.x_prompt, g.x_sample, g.cache_k, g.cache_v, g.state_conv, g.state_lru, g.state_c, g.state_n,
     g.state_m, g.p_prompt, g.p_sample, g.w_in, g.b_in, g.conv_w, g.conv_b, g.lru_wr, g.lru_br,
     g.lru_wi, g.lru_bi, g.lru_lambda, g.ml_norm_g, g.w_pa, g.w_pb, g.w_pc, g.w_out, g.ln1_g, g.ln1_b,
     g.router_w, g.router_b, g.exp_w1, g.exp_b1, g.exp_w2, g.exp_b2, g.ple_w, g.ple_gate_w,
     g.ple_gate_b, g.ln2_g, g.ln2_b) = i
    (g.o_y_p, g.o_y_s, g.o_k_p, g.o_v_p, g.o_conv_p, g.o_lru_p, g.o_c_p, g.o_n_p, g.o_m_p, g.o_k_s,
     g.o_v_s, g.o_conv_s, g.o_lru_s, g.o_c_s, g.o_n_s, g.o_m_s) = o
    g.yaT_d = nc.dram_tensor("yaT_scratch", (DT, P, T), F32).ap()
    g.x1_d = nc.dram_tensor("x1_scratch", (T + 1, D), F32).ap()
    g.residual_d = nc.dram_tensor("residual_scratch", (NT, P, D), F32).ap()
    g.table_d = nc.dram_tensor("slot_table_scratch", (NSLOT + 2 * SLOTS, 1), I32).ap()
    g.y_d = nc.dram_tensor("expert_rows_scratch", (T * TOPK, D), F32).ap()
    with ExitStack() as ctx:
        def sb(name, shape, dt=F32):
            return ctx.enter_context(nc.sbuf_tensor(name, shape, dt))

        g.bank = banks(nc, ctx)
        g.ident, g.eps = sb("ident", [P, P]), sb("ln_eps", [P, 1])
        g.gates = sb("expert_gates", [P, NT * TOPK])
        g.ctl = sb("loop_control", [P, 1 + NBLK], I32)
        with ExitStack() as trunk:
            def tb(name, shape):
                return trunk.enter_context(nc.sbuf_tensor(name, shape, F32))

            g.ones, g.neg_ones, g.tri_neg, g.tri_before = (
                tb(n, [P, P]) for n in ("ones", "neg_ones", "tri_neg", "tri_before"))
            g.strict, g.strict_s, g.causal, g.causal_s = (
                tb(n, [P, P]) for n in ("strict", "strict_s", "causal", "causal_s"))
            g.sel = tb("head_selector", [H, H, P])
            g.vec = tb("feature_vectors", [P, P])
            g.state = tb("state_columns", [P, DT, 32])
            g.coef = tb("decay_coef", [P, DT])
            g.half_b = tb("half_gate_bias", [P, 2 * DT])
            g.qbias = tb("scaled_q_bias", [P, H])
            g.mkbias = tb("scaled_mk_bias", [P, 2])
            stage_constants(nc, g)
            with ExitStack() as early:
                xT = early.enter_context(nc.sbuf_tensor("xT", [P, DT, T], F32))
                stage_transpose_x(nc, g, xT)
                stage_lru(nc, g, xT)
                qT = early.enter_context(nc.sbuf_tensor("sb_qT", [P, H, T], F32))
                with ExitStack() as attend:
                    kT = attend.enter_context(nc.sbuf_tensor("sb_kT", [P, H, T], F32))
                    v_tok = attend.enter_context(nc.sbuf_tensor("sb_v", [P, NT, 512], F32))
                    stage_sb_project(nc, g, xT, qT, kT, v_tok)
                    stage_sb_prompt(nc, g, qT, kT, v_tok)
                    stage_sb_sample(nc, g, qT, kT, v_tok)
                ycT = early.enter_context(nc.sbuf_tensor("ycT", [P, H, T], F32))
                with ExitStack() as recur:
                    def rb(name, shape):
                        return recur.enter_context(nc.sbuf_tensor(name, shape, F32))

                    m = Shared()
                    m.qz, m.kT, m.k_tok = ycT, rb("ml_kT", [P, 2, T]), rb("ml_k", [P, NT, 256])
                    m.v_aug, m.o_gate = rb("ml_v", [P, NT, H, HD + 1]), rb("ml_o", [P, NT, 512])
                    m.w, m.cols = rb("ml_w_row", [H, T]), rb("ml_cols", [P, 4, NT, H])
                    m.s_old, m.norm_g = rb("ml_s_old", [P, H, 16]), rb("ml_norm", [P, 512])
                    with ExitStack() as rows:
                        m.ig = rows.enter_context(nc.sbuf_tensor("ml_ig_row", [H, T], F32))
                        m.fg = rows.enter_context(nc.sbuf_tensor("ml_fg_row", [H, T], F32))
                        stage_ml_project(nc, g, xT, m)
                        stage_ml_gates(nc, g, m)
                    stage_mlstm(nc, g, m, ycT)
                with ExitStack() as mixing:
                    mixT = mixing.enter_context(nc.sbuf_tensor("mixT", [P, DT, T], F32))
                    stage_mix(nc, g, xT, qT, ycT, mixT)
                    x1T = xT
                    stage_out(nc, g, mixT, x1T)
                stage_route(nc, g, x1T)
        stage_experts(nc, g)
        stage_combine(nc, g)


def kernel(**inputs):
    import concourse.bacc as bacc
    from concourse.bass_utils import run_bass_kernel_spmd

    names = ("x_prompt", "x_sample", "cache_sb_k", "cache_sb_v", "state_conv", "state_lru", "state_mlstm_c",
             "state_mlstm_n", "state_mlstm_m", "p_prompt", "p_sample", "w_in", "b_in", "conv_w", "conv_b",
             "lru_wr", "lru_br", "lru_wi", "lru_bi", "lru_lambda", "ml_norm_g", "w_pa", "w_pb", "w_pc", "w_out",
             "ln1_g", "ln1_b", "router_w", "router_b", "exp_w1", "exp_b1", "exp_w2", "exp_b2", "ple_w",
             "ple_gate_w", "ple_gate_b", "ln2_g", "ln2_b")
    shapes = ((1, TP, D), (NB, LS, D), (1, 1, TP, H, HD), (1, 1, TP, H, HD), (1, 1, CW - 1, D), (1, 1, D),
              (1, 1, H, QD, HD), (1, 1, H, QD), (1, 1, H), (1, NB, LS, H, HD), (1, NB, LS, H, HD),
              (1, NB, CW - 1, D), (1, NB, D), (1, NB, H, QD, HD), (1, NB, H, QD), (1, NB, H))
    nc = bacc.Bacc("TRN2", target_bir_lowering=False, num_devices=1)
    arrays = {f"in_{name}": np.ascontiguousarray(inputs[name]) for name in names}
    ins = [nc.dram_tensor(name, a.shape, mybir.dt.from_np(a.dtype), kind="ExternalInput").ap()
           for name, a in arrays.items()]
    outs = [nc.dram_tensor(f"out_{n}", shape, F32, kind="ExternalOutput").ap() for n, shape in enumerate(shapes)]
    build_program(nc, ins, outs)
    result = run_bass_kernel_spmd(nc, [arrays], core_ids=[0]).results[0]
    return tuple(result[f"out_{n}"] for n in range(len(shapes)))
```

```python
from contextlib import ExitStack, contextmanager

import numpy as np

import concourse.bass as bass
from concourse import mybir

F32 = mybir.dt.float32
I32 = mybir.dt.int32
U32 = mybir.dt.uint32
F32R = mybir.dt.float32r
ALU = mybir.AluOpType
ACT = mybir.ActivationFunctionType
AX_X = mybir.AxisListType.X

P = 128
D = 1024
DT = D // P
TP = 1024
NB, LS = 8, 16
TS = NB * LS
T = TP + TS
NT = T // P
CHUNKS = ((0, 512), (512, 1024), (1024, T))
CHUNK3 = T // 3
CHUNKS3 = tuple((i * CHUNK3, (i + 1) * CHUNK3) for i in range(3))
CW = 4
H = 4
HD = 128
QD = 64
PAST = 1024
KB = PAST // P
NE, TOPK, FF = 32, 4, 512
FT = FF // P
PLE = 256
ALPHA = 2.0 ** 0.25
LN_EPS = 1e-5
NEG = -1e30
SB_SCALE = float(HD) ** -0.5
ML_SCALE = float(QD) ** -0.5
O_AX, O_AG, O_SQ, O_SK, O_SV, O_MQ, O_MK, O_MV, O_MO, O_MI, O_MF, O_MG = (
    0, 1024, 2048, 2560, 3072, 3584, 3840, 4096, 4608, 5120, 5124, 5128)
V_BIN, V_BMG, V_CW, V_CB, V_BR, V_BI, V_LAM = 0, 40, 64, 96, 104, 112, 120
SLOTS = 192
NSLOT = T * TOPK + NE * SLOTS
MAXBLK = NSLOT // SLOTS


class Shared:
    pass


@contextmanager
def stage_semaphores(nc):
    owned = []

    def sem(name):
        owned.append(nc.alloc_semaphore(name))
        return owned[-1]

    yield sem
    nc.clear_and_free_semaphores(owned)
    nc.all_engine_barrier()


def banks(nc, ctx):
    return [ctx.enter_context(nc.psum_tensor(f"bank{i}", [P, 512], F32)) for i in range(8)]


def stage_constants(nc, g):
    with ExitStack() as ctx:
        sem = ctx.enter_context(stage_semaphores(nc))
        rows = ctx.enter_context(nc.sbuf_tensor("vector_rows", [P, P], F32))
        state_rows = ctx.enter_context(nc.sbuf_tensor("state_rows", [32, D], F32))
        sp_e = ctx.enter_context(nc.sbuf_tensor("lambda_exp", [P, DT], F32))
        ident_ready = sem("c_ident_ready")
        filled = sem("c_filled")
        masks = sem("c_masks")
        rows_in = sem("c_rows_in")
        turned = sem("c_turned")
        copied = sem("c_copied")
        lam_abs = sem("c_lam_abs")
        lam_exp = sem("c_lam_exp")
        lam_ln = sem("c_lam_ln")
        lam_sp = sem("c_lam_sp")
        block = ctx.enter_context(nc.Block())
        loads = [
            (rows[V_BIN:V_BIN + 40, :], g.b_in[0, 0:5120].rearrange("(r p) -> r p", p=P)),
            (rows[V_BMG:V_BMG + 24, :], g.b_in[0, O_MG:O_MG + 3072].rearrange("(r p) -> r p", p=P)),
            (rows[V_CW:V_CW + 32, :], g.conv_w[0].rearrange("j (r p) -> (j r) p", p=P)),
            (rows[V_CB:V_CB + 8, :], g.conv_b[0].rearrange("(r p) -> r p", p=P)),
            (rows[V_BR:V_BR + 8, :], g.lru_br[0].rearrange("(r p) -> r p", p=P)),
            (rows[V_BI:V_BI + 8, :], g.lru_bi[0].rearrange("(r p) -> r p", p=P)),
            (rows[V_LAM:V_LAM + 8, :], g.lru_lambda[0].rearrange("(r p) -> r p", p=P)),
            (state_rows[0:24, :], g.state_conv[0].rearrange("b j d -> (b j) d")),
            (state_rows[24:32, :], g.state_lru[0]),
        ]

        @block.sync
        def _(sp):
            for dst, src in loads:
                sp.dma_start(dst, src).then_inc(rows_in, 16)

        @block.gpsimd
        def _(pool):
            fills = ((g.ident, 0.0), (g.tri_neg, -1.0), (g.ones, 1.0), (g.neg_ones, -1.0),
                     (g.strict, 1.0), (g.strict_s, 1.0), (g.causal, 0.0), (g.causal_s, 0.0),
                     (g.tri_before, 1.0), (g.eps, LN_EPS))
            for tile, value in fills:
                pool.memset(tile[:], value).then_inc(filled, 1)
            pool.memset(g.sel[:], 0.0).then_inc(filled, 1)
            pool.wait_ge(filled, len(fills) + 1)
            pool.affine_select(out=g.ident[:], in_=g.ident[:], compare_op=ALU.not_equal, fill=1.0,
                               base=0, pattern=[[-1, P]], channel_multiplier=1).then_inc(ident_ready, 1)
            pool.affine_select(out=g.tri_neg[:], in_=g.tri_neg[:], compare_op=ALU.is_ge, fill=0.0,
                               base=0, pattern=[[-1, P]], channel_multiplier=1)
            pool.affine_select(out=g.tri_before[:], in_=g.tri_before[:], compare_op=ALU.is_ge, fill=0.0,
                               base=-1, pattern=[[1, P]], channel_multiplier=-1)
            pool.affine_select(out=g.strict[:], in_=g.strict[:], compare_op=ALU.is_ge, fill=0.0,
                               base=-1, pattern=[[1, P]], channel_multiplier=-1)
            pool.affine_select(out=g.strict_s[:], in_=g.strict_s[:], compare_op=ALU.is_ge, fill=0.0,
                               base=-1, pattern=[[1, P]], channel_multiplier=-1).then_inc(masks, 1)
            pool.affine_select(out=g.causal[:], in_=g.causal[:], compare_op=ALU.is_ge, fill=NEG,
                               base=0, pattern=[[1, P]], channel_multiplier=-1)
            pool.affine_select(out=g.causal_s[:], in_=g.causal_s[:], compare_op=ALU.is_ge, fill=NEG,
                               base=0, pattern=[[1, P]], channel_multiplier=-1).then_inc(masks, 1)
            pool.affine_select(out=g.sel[:], in_=g.sel[:], compare_op=ALU.not_equal, fill=1.0,
                               base=0, pattern=[[-1, H], [0, P]], channel_multiplier=1)
            pool.wait_ge(masks, 2)
            for tile, fill in ((g.strict_s, 0.0), (g.causal_s, NEG)):
                view = tile[:].rearrange("s (b t) -> s b t", t=LS)
                pool.affine_select(out=view, in_=view, compare_op=ALU.is_ge, fill=fill, base=0,
                                   pattern=[[-LS, NB], [0, LS]], channel_multiplier=1)

        @block.tensor
        def _(pe):
            pe.wait_ge(ident_ready, 1)
            pe.wait_ge(rows_in, 16 * len(loads))
            nc.tensor.transpose(g.bank[0][:, 0:P], rows[:], g.ident[:]).then_inc(turned, 1)
            for m in range(DT):
                last = nc.tensor.transpose(g.bank[1][:, m * 32:(m + 1) * 32],
                                           state_rows[:, m * P:(m + 1) * P], g.ident[0:32, 0:32])
            last.then_inc(turned, 1)

        @block.vector
        def _(dve):
            dve.wait_ge(turned, 2)
            nc.vector.tensor_copy(g.vec[:], g.bank[0][:, 0:P]).then_inc(copied, 1)
            nc.vector.tensor_copy(g.state[:], g.bank[1][:, 0:DT * 32].rearrange("p (m r) -> p m r", m=DT)
                                  ).then_inc(copied, 1)
            dve.wait_ge(copied, 2)
            lam = g.vec[:, V_LAM:V_LAM + DT]
            nc.vector.tensor_scalar(sp_e[:], lam, -1.0, None, ALU.mult).then_inc(lam_abs, 1)
            dve.wait_ge(lam_abs, 1)
            nc.vector.tensor_tensor(sp_e[:], sp_e[:], lam, ALU.max).then_inc(lam_abs, 1)
            nc.vector.tensor_scalar(g.coef[:], lam, 0.0, None, ALU.min).then_inc(lam_sp, 1)
            nc.vector.tensor_scalar(g.qbias[:], g.vec[:, O_SQ // P:O_SQ // P + H], SB_SCALE, None, ALU.mult)
            nc.vector.tensor_scalar(g.mkbias[:], g.vec[:, O_MK // P:O_MK // P + 2], ML_SCALE, None, ALU.mult)
            nc.vector.tensor_scalar(g.half_b[:], g.vec[:, V_BR:V_BR + 2 * DT], 0.5, None, ALU.mult)
            dve.wait_ge(lam_ln, 1)
            dve.wait_ge(lam_sp, 1)
            nc.vector.tensor_tensor(g.coef[:], g.coef[:], sp_e[:], ALU.subtract).then_inc(lam_sp, 1)
            dve.wait_ge(lam_sp, 2)
            nc.vector.tensor_scalar(g.coef[:], g.coef[:], 4.0, None, ALU.mult)

        @block.scalar
        def _(act):
            act.wait_ge(lam_abs, 2)
            nc.scalar.activation(sp_e[:], sp_e[:], ACT.Exp, scale=-1.0).then_inc(lam_exp, 1)
            act.wait_ge(lam_exp, 1)
            nc.scalar.activation(sp_e[:], sp_e[:], ACT.Ln, bias=1.0).then_inc(lam_ln, 1)


def stage_transpose_x(nc, g, xT):
    with ExitStack() as ctx:
        sem = ctx.enter_context(stage_semaphores(nc))
        x = ctx.enter_context(nc.sbuf_tensor("x_tokens", [P, NT, D], F32))
        x_in = [sem(f"x_in{i}") for i in range(NT)]
        turned = sem("x_turned")
        moved = [sem("x_moved_act"), sem("x_moved_dve")]
        block = ctx.enter_context(nc.Block())
        units = [(i, q) for i in range(NT) for q in range(2)]

        @block.sync
        def _(sp):
            xp = g.x_prompt[0].rearrange("(i p) d -> p i d", p=P)
            for i in range(NT - 1):
                sp.dma_start(x[:, i, :], xp[:, i, :]).then_inc(x_in[i], 16)
            sp.dma_start(x[:, NT - 1, :], g.x_sample.rearrange("b t d -> (b t) d")).then_inc(x_in[NT - 1], 16)

        @block.tensor
        def _(pe):
            for n, (i, q) in enumerate(units):
                pe.wait_ge(x_in[i], 16)
                if n >= 8:
                    pe.wait_ge(moved[n % 2], (n - 8) // 2 + 1)
                for k in range(4):
                    last = nc.tensor.transpose(g.bank[n % 8][:, k * P:(k + 1) * P],
                                               x[:, i, (4 * q + k) * P:(4 * q + k + 1) * P], g.ident[:])
                last.then_inc(turned, 1)

        def move(eng, copy, parity):
            for n, (i, q) in enumerate(units):
                if n % 2 == parity:
                    eng.wait_ge(turned, n + 1)
                    copy(xT[:, 4 * q:4 * q + 4, i * P:(i + 1) * P],
                         g.bank[n % 8][:].rearrange("p (k t) -> p k t", k=4)).then_inc(moved[parity], 1)

        @block.scalar
        def _(act):
            move(act, nc.scalar.copy, 0)

        @block.vector
        def _(dve):
            move(dve, nc.vector.tensor_copy, 1)


def stage_lru(nc, g, xT):
    with ExitStack() as ctx:
        sem = ctx.enter_context(stage_semaphores(nc))
        def sb(name, shape):
            return ctx.enter_context(nc.sbuf_tensor(name, shape, F32))

        GRP = 256
        wx = sb("w_ax", [P, 2, DT, GRP])
        wg = sb("w_ag", [P, 2, DT, GRP])
        gate_w = sb("lru_gate_w", [P, DT, 2, P])
        ext_p = sb("ext_prompt", [P, DT, CW - 1 + TP])
        ext_s = sb("ext_sample", [P, DT, NB, CW - 1 + LS])
        ua = sb("ua", [P, 2, T])
        gl = sb("gelu_gate", [P, 2, T])
        tr = sb("tanh_r", [P, T])
        ti = sb("tanh_i", [P, T])
        aa = sb("decay", [P, T])
        th = sb("tanh_log_a", [P, T])
        mu = sb("input_scale", [P, T])
        hh = sb("lru_h", [P, 2, T])
        pack = sb("state_pack", [P, DT, 36])
        outrow = sb("state_out_rows", [36, D])
        tmp8 = sb("start_terms", [P, NB])
        w_in_x = [sem(f"a_wx{i}") for i in range(4)]
        w_in_g = [sem(f"a_wg{i}") for i in range(4)]
        zeroed = sem("a_zeroed")
        gate_in = sem("a_gate_in")
        ax_ready = sem("a_ax_ready")
        ax_moved = sem("a_ax_moved")
        ag_ready = sem("a_ag_ready")
        ag_moved = sem("a_ag_moved")
        states_in = sem("a_states_in")
        conv_step = sem("a_conv_step")
        ua_ready = sem("a_ua_ready")
        ri_ready = sem("a_ri_ready")
        ri_moved = sem("a_ri_moved")
        a_ready = sem("a_decay_ready")
        square_ready = sem("a_square_ready")
        mult_ready = sem("a_mult_ready")
        bx_step = sem("a_bx_step")
        h_ready = sem("a_h_ready")
        ya_ready = sem("a_ya_ready")
        ya_out = [sem("a_ya_out0"), sem("a_ya_out1")]
        packed = sem("a_packed")
        pack_turned = sem("a_pack_turned")
        rows_ready = sem("a_rows_ready")
        states_out = sem("a_states_out")
        block = ctx.enter_context(nc.Block())
        w_in_t = g.w_in[0].rearrange("(k p) n -> p k n", p=P)

        @block.sync
        def _(sp):
            for q in range(4):
                if q >= 2:
                    sp.wait_ge(ax_ready, 2 * (q - 1))
                sp.dma_start(wx[:, q % 2], w_in_t[:, :, O_AX + q * GRP:O_AX + (q + 1) * GRP]).then_inc(w_in_x[q], 16)
                if q >= 2:
                    sp.wait_ge(ag_ready, 2 * (q - 1))
                sp.dma_start(wg[:, q % 2], w_in_t[:, :, O_AG + q * GRP:O_AG + (q + 1) * GRP]).then_inc(w_in_g[q], 16)
            for m in range(DT):
                sp.wait_ge(ya_ready, m + 1)
                sp.dma_start(g.yaT_d[m], hh[:, m % 2]).then_inc(ya_out[m % 2], 16)
            sp.wait_ge(rows_ready, 2)
            sp.dma_start(g.o_conv_p[0, 0], outrow[0:3, :]).then_inc(states_out, 16)
            sp.dma_start(g.o_conv_s[0].rearrange("b j d -> (b j) d"), outrow[3:27, :]).then_inc(states_out, 16)
            sp.dma_start(g.o_lru_p[0], outrow[27:28, :]).then_inc(states_out, 16)
            sp.dma_start(g.o_lru_s[0], outrow[28:36, :]).then_inc(states_out, 16)
            for s in ya_out:
                sp.wait_ge(s, 16 * DT // 2)
            sp.wait_ge(states_out, 64)

        @block.gpsimd
        def _(pool):
            pool.memset(gate_w[:], 0.0).then_inc(zeroed, 1)
            pool.memset(ext_p[:, :, 0:CW - 1], 0.0).then_inc(states_in, 1)
            pool.tensor_copy(ext_s[:, :, :, 0:CW - 1],
                             g.state[:, :, 0:24].rearrange("p m (b j) -> p m b j", b=NB)).then_inc(states_in, 1)
            pool.wait_ge(zeroed, 1)
            for r, w in enumerate((g.lru_wr, g.lru_wi)):
                pairs = w[0].rearrange("(m two) c d -> two c m d", two=2)
                for half in range(2):
                    lo = half * 64
                    pool.dma_start(gate_w[lo:lo + 64, :, r, lo:lo + 64], pairs[half]).then_inc(gate_in, 16)

        @block.tensor
        def _(pe):
            def project(w, bank0):
                for k in range(DT):
                    for c, (lo, hi) in enumerate(CHUNKS):
                        last = nc.tensor.matmul(g.bank[bank0 + c][:, 0:hi - lo], w[:, k, :], xT[:, k, lo:hi],
                                                start=(k == 0), stop=(k == DT - 1))
                return last

            def gates(m):
                pe.wait_ge(ua_ready, m + 1)
                for c, (lo, hi) in enumerate(CHUNKS):
                    if m or c:
                        pe.wait_ge(ri_moved, 3 * m + c)
                    nc.tensor.matmul(g.bank[6][:, 0:hi - lo], gate_w[:, m, 0, :], ua[:, m % 2, lo:hi],
                                     start=True, stop=True)
                    nc.tensor.matmul(g.bank[7][:, 0:hi - lo], gate_w[:, m, 1, :], ua[:, m % 2, lo:hi],
                                     start=True, stop=True).then_inc(ri_ready, 1)

            for m in range(DT):
                off = (m % 2) * P
                pe.wait_ge(w_in_x[m // 2], 16)
                if m:
                    pe.wait_ge(ax_moved, m)
                project(wx[:, m // 2 % 2, :, off:off + P], 0).then_inc(ax_ready, 1)
                if m == 1:
                    pe.wait_ge(gate_in, 64)
                if m:
                    gates(m - 1)
                pe.wait_ge(w_in_g[m // 2], 16)
                if m:
                    pe.wait_ge(ag_moved, m)
                project(wg[:, m // 2 % 2, :, off:off + P], 3).then_inc(ag_ready, 1)
            gates(DT - 1)
            pe.wait_ge(packed, DT + 2)
            pe.wait_ge(ri_moved, 3 * DT)
            for half in range(2):
                for k in range(4):
                    last = nc.tensor.transpose(g.bank[6 + half][0:36, k * P:(k + 1) * P],
                                               pack[:, 4 * half + k, :], g.ident[:])
                last.then_inc(pack_turned, 1)

        @block.scalar
        def _(act):
            def lru_gates(m):
                for c, (lo, hi) in enumerate(CHUNKS):
                    act.wait_ge(ri_ready, 3 * m + c + 1)
                    if m and c == 0:
                        act.wait_ge(h_ready, m)
                    nc.scalar.activation(tr[:, lo:hi], g.bank[6][:, 0:hi - lo], ACT.Tanh,
                                         bias=g.half_b[:, m:m + 1], scale=0.5)
                    nc.scalar.activation(ti[:, lo:hi], g.bank[7][:, 0:hi - lo], ACT.Tanh,
                                         bias=g.half_b[:, DT + m:DT + m + 1], scale=0.5).then_inc(ri_moved, 1)
                act.wait_ge(ri_moved, 3 * m + 3)
                nc.scalar.activation(aa[:], tr[:], ACT.Exp, bias=g.coef[:, m:m + 1], scale=g.coef[:, m:m + 1])
                nc.scalar.activation(th[:], tr[:], ACT.Tanh, bias=g.coef[:, m:m + 1],
                                     scale=g.coef[:, m:m + 1]).then_inc(a_ready, 1)
                act.wait_ge(square_ready, 2 * m + 2)
                nc.scalar.activation(mu[:], mu[:], ACT.Sqrt, scale=-1.0).then_inc(mult_ready, 1)

            for m in range(DT):
                act.wait_ge(ax_ready, m + 1)
                bias = g.vec[:, V_BIN + m:V_BIN + m + 1]
                nc.scalar.activation(ext_p[:, m, 3:3 + 512], g.bank[0][:], ACT.Identity, bias=bias)
                nc.scalar.activation(ext_p[:, m, 3 + 512:3 + 1024], g.bank[1][:], ACT.Identity, bias=bias)
                nc.scalar.activation(ext_s[:, m, :, 3:], g.bank[2][:, 0:TS].rearrange("p (b t) -> p b t", b=NB),
                                     ACT.Identity, bias=bias).then_inc(ax_moved, 1)
                if m:
                    lru_gates(m - 1)
                act.wait_ge(ag_ready, m + 1)
                if m >= 2:
                    act.wait_ge(ya_ready, m - 1)
                bias = g.vec[:, 8 + m:9 + m]
                for c, (lo, hi) in enumerate(CHUNKS):
                    last = nc.scalar.activation(gl[:, m % 2, lo:hi], g.bank[3 + c][:, 0:hi - lo],
                                                ACT.Gelu_apprx_tanh, bias=bias)
                last.then_inc(ag_moved, 1)
            lru_gates(DT - 1)

        @block.vector
        def _(dve):
            def conv(m):
                dve.wait_ge(ax_moved, m + 1)
                if m == 0:
                    dve.wait_ge(states_in, 2)
                for j in range(CW):
                    w = g.vec[:, V_CW + j * DT + m:V_CW + j * DT + m + 1]
                    up = ua[:, m % 2, 0:TP]
                    us = ua[:, m % 2, TP:T].rearrange("p (b t) -> p b t", b=NB)
                    ep, es = ext_p[:, m, j:j + TP], ext_s[:, m, :, j:j + LS]
                    if j == 0:
                        cb = g.vec[:, V_CB + m:V_CB + m + 1]
                        nc.vector.tensor_scalar(up, ep, w, cb, ALU.mult, ALU.add)
                        last = nc.vector.tensor_scalar(us, es, w, cb, ALU.mult, ALU.add)
                    else:
                        dve.wait_ge(conv_step, 3 * m + j)
                        nc.vector.scalar_tensor_tensor(out=up, in0=ep, scalar=w, in1=up, op0=ALU.mult, op1=ALU.add)
                        last = nc.vector.scalar_tensor_tensor(out=us, in0=es, scalar=w, in1=us,
                                                              op0=ALU.mult, op1=ALU.add)
                    last.then_inc(conv_step if j < CW - 1 else ua_ready, 1)

            def scan(m):
                s = m % 2
                starts = slice(TP, T, LS)
                dve.wait_ge(a_ready, m + 1)
                nc.vector.tensor_tensor(mu[:], aa[:], aa[:], ALU.mult).then_inc(square_ready, 1)
                dve.wait_ge(ua_ready, m + 1)
                nc.vector.scalar_tensor_tensor(out=ti[:], in0=ti[:], scalar=1.0, in1=ua[:, s], op0=ALU.add,
                                               op1=ALU.mult).then_inc(bx_step, 1)
                nc.vector.tensor_tensor(tmp8[:], aa[:, starts], g.state[:, m, 24:32], ALU.mult).then_inc(bx_step, 1)
                dve.wait_ge(square_ready, 2 * m + 1)
                nc.vector.scalar_tensor_tensor(out=mu[:], in0=mu[:], scalar=1.0, in1=th[:], op0=ALU.add,
                                               op1=ALU.mult).then_inc(square_ready, 1)
                dve.wait_ge(bx_step, 6 * m + 2)
                nc.vector.memset(aa[:, starts], 0.0).then_inc(bx_step, 1)
                dve.wait_ge(mult_ready, m + 1)
                nc.vector.memset(mu[:, 0:1], 1.0).then_inc(bx_step, 1)
                dve.wait_ge(bx_step, 6 * m + 4)
                nc.vector.scalar_tensor_tensor(out=ti[:], in0=ti[:], scalar=0.5, in1=mu[:], op0=ALU.mult,
                                               op1=ALU.mult).then_inc(bx_step, 1)
                dve.wait_ge(bx_step, 6 * m + 5)
                nc.vector.tensor_tensor(ti[:, starts], ti[:, starts], tmp8[:], ALU.add).then_inc(bx_step, 1)
                dve.wait_ge(bx_step, 6 * m + 6)
                if m >= 2:
                    dve.wait_ge(ya_out[s], 16 * (m // 2))
                nc.vector.tensor_tensor_scan(hh[:, s], aa[:], ti[:], 0.0, ALU.mult, ALU.add).then_inc(h_ready, 1)
                dve.wait_ge(h_ready, m + 1)
                nc.vector.tensor_copy(pack[:, m, 27:28], hh[:, s, TP - 1:TP])
                nc.vector.tensor_copy(pack[:, m, 28:36], hh[:, s, TP + LS - 1:T:LS]).then_inc(packed, 1)
                dve.wait_ge(ag_moved, m + 1)
                dve.wait_ge(packed, m + 1)
                nc.vector.tensor_tensor(hh[:, s], hh[:, s], gl[:, s], ALU.mult).then_inc(ya_ready, 1)

            for m in range(DT):
                if m >= 2:
                    dve.wait_ge(ri_ready, 3 * (m - 1))
                conv(m)
                if m:
                    scan(m - 1)
            scan(DT - 1)
            nc.vector.tensor_copy(pack[:, :, 0:3], ext_p[:, :, TP:TP + 3]).then_inc(packed, 1)
            nc.vector.tensor_copy(pack[:, :, 3:27].rearrange("p m (b j) -> p m b j", b=NB),
                                  ext_s[:, :, :, LS:LS + 3]).then_inc(packed, 1)
            for half in range(2):
                dve.wait_ge(pack_turned, half + 1)
                nc.vector.tensor_copy(outrow[:, half * 512:(half + 1) * 512],
                                      g.bank[6 + half][0:36, :]).then_inc(rows_ready, 1)


def stage_sb_project(nc, g, xT, qT, kT, v_tok):
    with ExitStack() as ctx:
        sem = ctx.enter_context(stage_semaphores(nc))
        def sb(name, shape):
            return ctx.enter_context(nc.sbuf_tensor(name, shape, F32))

        w = sb("w_sb", [P, 3, DT, 512])
        bias = sb("kv_bias", [P, 2, 512])
        k_tok = sb("k_tok", [P, 2, 512])
        w_first = [sem(f"b_w_first{k}") for k in range(DT)]
        w_loaded = [sem(f"b_w{i}") for i in range(3)]
        bias_in = sem("b_bias_in")
        prod = sem("b_prod")
        kv_moved = sem("b_kv_moved")
        q_moved = sem("b_q_moved")
        k_turned = sem("b_k_turned")
        kT_moved = sem("b_kT_moved")
        k_out = [sem("b_k_out0"), sem("b_k_out1")]
        v_out = sem("b_v_out")
        block = ctx.enter_context(nc.Block())
        w_in_t = g.w_in[0].rearrange("(k p) n -> p k n", p=P)
        NBK = 6

        @block.sync
        def _(sp):
            for s, off in enumerate((O_SK, O_SV, O_SQ)):
                if s == 0:
                    for k in range(DT):
                        sp.dma_start(w[:, s, k], w_in_t[:, k, off:off + 512]).then_inc(w_first[k], 16)
                else:
                    sp.dma_start(w[:, s], w_in_t[:, :, off:off + 512]).then_inc(w_loaded[s], 16)
                if s == 0:
                    sp.dma_start(bias[:].rearrange("p a n -> p (a n)"),
                                 g.b_in[0:1, O_SK:O_SK + 1024].broadcast_to([P, 1024])).then_inc(bias_in, 16)
            kp, vp = (t[0, 0].rearrange("(i p) h d -> i p (h d)", p=P) for t in (g.o_k_p, g.o_v_p))
            ks, vs = (t[0].rearrange("b t h d -> (b t) (h d)") for t in (g.o_k_s, g.o_v_s))
            for i in range(NT):
                sp.wait_ge(kv_moved, 2 * i + 1)
                sp.dma_start(kp[i] if i < NT - 1 else ks, k_tok[:, i % 2, :]).then_inc(k_out[i % 2], 16)
                sp.wait_ge(kv_moved, 2 * i + 2)
                sp.dma_start(vp[i] if i < NT - 1 else vs, v_tok[:, i, :]).then_inc(v_out, 16)
            sp.wait_ge(k_out[0], 16 * 5)
            sp.wait_ge(k_out[1], 16 * 4)
            sp.wait_ge(v_out, 16 * NT)

        @block.tensor
        def _(pe):
            def turn_k(i):
                pe.wait_ge(kv_moved, 2 * i + 1)
                if i >= 2:
                    pe.wait_ge(kT_moved, i - 1)
                for h in range(H):
                    last = nc.tensor.transpose(g.bank[6 + i % 2][:, h * P:(h + 1) * P],
                                               k_tok[:, i % 2, h * P:(h + 1) * P], g.ident[:])
                last.then_inc(k_turned, 1)

            n = 0
            for i in range(NT):
                for s in range(2):
                    if s:
                        pe.wait_ge(w_loaded[s], 16)
                    if n >= NBK:
                        pe.wait_ge(kv_moved, n - NBK + 1)
                    for k in range(DT):
                        if n == 0:
                            pe.wait_ge(w_first[k], 16)
                        last = nc.tensor.matmul(g.bank[n % NBK][:], xT[:, k, i * P:(i + 1) * P], w[:, s, k, :],
                                                start=(k == 0), stop=(k == DT - 1))
                    last.then_inc(prod, 1)
                    n += 1
                if i:
                    turn_k(i - 1)
            pe.wait_ge(w_loaded[2], 16)
            for h in range(H):
                for lo, hi in CHUNKS:
                    if n - NBK < 2 * NT:
                        pe.wait_ge(kv_moved, n - NBK + 1)
                    else:
                        pe.wait_ge(q_moved, n - NBK + 1 - 2 * NT)
                    for k in range(DT):
                        last = nc.tensor.matmul(g.bank[n % NBK][:, 0:hi - lo], w[:, 2, k, h * P:(h + 1) * P],
                                                xT[:, k, lo:hi], start=(k == 0), stop=(k == DT - 1))
                    last.then_inc(prod, 1)
                    n += 1
                if h == 0:
                    turn_k(NT - 1)

        @block.vector
        def _(dve):
            dve.wait_ge(bias_in, 16)
            for n in range(2 * NT):
                i, s = divmod(n, 2)
                dve.wait_ge(prod, n + 1)
                if s == 0 and i >= 2:
                    dve.wait_ge(k_turned, i - 1)
                    dve.wait_ge(k_out[i % 2], 16 * (i // 2))
                out = v_tok[:, i, :] if s else k_tok[:, i % 2, :]
                nc.vector.tensor_tensor(out, g.bank[n % NBK][:], bias[:, s, :], ALU.add).then_inc(kv_moved, 1)

        @block.scalar
        def _(act):
            def move_kT(i):
                act.wait_ge(k_turned, i + 1)
                nc.scalar.copy(kT[:, :, i * P:(i + 1) * P],
                               g.bank[6 + i % 2][:].rearrange("p (h t) -> p h t", h=H)).then_inc(kT_moved, 1)

            for i in range(NT - 1):
                move_kT(i)
            n = 2 * NT
            for h in range(H):
                for lo, hi in CHUNKS:
                    act.wait_ge(prod, n + 1)
                    nc.scalar.activation(qT[:, h, lo:hi], g.bank[n % NBK][:, 0:hi - lo], ACT.Identity,
                                         bias=g.qbias[:, h:h + 1], scale=SB_SCALE).then_inc(q_moved, 1)
                    n += 1
            move_kT(NT - 1)


def stage_sb_prompt(nc, g, qT, kT, v_tok):
    units = []
    for h in range(H):
        for c in range(2):
            blocks = list(range(4 * c + 3, -1, -1))
            for j in blocks:
                units.append((h, 2 * h + c, c, j, max(j * P - 512 * c, 0), j == blocks[0], j == 0))
    N = len(units)
    NZ, RING = 5, 4
    with ExitStack() as ctx:
        sem = ctx.enter_context(stage_semaphores(nc))
        def sb(name, shape):
            return ctx.enter_context(nc.sbuf_tensor(name, shape, F32))

        e = sb("softplus_work", [P, RING, 512])
        u = sb("softplus", [P, RING, 512])
        acc = sb("later_keys_sum", [P, 3, 512])
        w = sb("sb_weights", [P, RING, 512])
        z_ready = sem("p_z_ready")
        abs_ready = sem("p_abs_ready")
        exp_ready = sem("p_exp_ready")
        ln_ready = sem("p_ln_ready")
        u_step = sem("p_u_step")
        u_ready = sem("p_u_ready")
        s_ready = sem("p_s_ready")
        acc_ready = sem("p_acc_ready")
        w_ready = sem("p_w_ready")
        w_masked = sem("p_w_masked")
        pv_done = sem("p_pv_done")
        y_moved = sem("p_y_moved")
        block = ctx.enter_context(nc.Block())

        def diagonal(n):
            return units[n][3] >= 4 * units[n][2]

        def diagonals(n):
            return sum(diagonal(m) for m in range(n))

        def zb(n, lo=0):
            return g.bank[n % NZ][:, lo:512]

        @block.tensor
        def _(pe):
            def z(n):
                h, chain, c, j, off, first, last = units[n]
                if n >= NZ:
                    pe.wait_ge(w_ready, n - NZ + 1)
                nc.tensor.matmul(zb(n, off), kT[:, h, j * P:(j + 1) * P], qT[:, h, 512 * c + off:512 * c + 512],
                                 start=True, stop=True, skip_group_check=True).then_inc(z_ready, 1)

            def s(n):
                h, chain, c, j, off, first, last = units[n]
                pe.wait_ge(u_ready, n + 1)
                ins = nc.tensor.matmul(zb(n, off), g.tri_neg[:], u[:, n % RING, off:512], start=False, stop=True,
                                       skip_group_check=True)
                if not first:
                    pe.wait_ge(acc_ready, n)
                    off_before = units[n - 1][4]
                    ins = nc.tensor.matmul(zb(n, off_before), g.neg_ones[:], acc[:, (n - 1) % 3, off_before:512],
                                           start=False, stop=True, skip_group_check=True)
                ins.then_inc(s_ready, 1)

            def pv(n):
                h, chain, c, j, off, first, last = units[n]
                pe.wait_ge(w_ready, n + 1)
                if diagonal(n):
                    pe.wait_ge(w_masked, diagonals(n + 1))
                if first and chain >= 2:
                    pe.wait_ge(y_moved, chain - 1)
                nc.tensor.matmul(g.bank[6 + chain % 2][:, off:512], v_tok[:, j, h * P:(h + 1) * P],
                                 w[:, n % RING, off:512], start=first, stop=last,
                                 skip_group_check=True).then_inc(pv_done, 1)

            for n in range(N + 4):
                if n < N:
                    z(n)
                if 0 <= n - 2 < N:
                    s(n - 2)
                if n >= 4:
                    pv(n - 4)

        @block.vector
        def _(dve):
            def softplus(n):
                off = units[n][4]
                dve.wait_ge(ln_ready, n + 1)
                if n >= RING:
                    dve.wait_ge(s_ready, n - RING + 1)
                    dve.wait_ge(acc_ready, n - RING + 1)
                ins = nc.vector.scalar_tensor_tensor(out=u[:, n % RING, off:512], in0=zb(n, off), scalar=0.0,
                                                     in1=e[:, n % RING, off:512], op0=ALU.max, op1=ALU.add)
                if diagonal(n):
                    ins.then_inc(u_step, 1)
                    dve.wait_ge(u_step, diagonals(n + 1))
                    ins = nc.vector.tensor_tensor(u[:, n % RING, off:off + P], u[:, n % RING, off:off + P],
                                                  g.strict[:], ALU.mult)
                ins.then_inc(u_ready, 1)

            def mask_w(n):
                off = units[n][4]
                if diagonal(n):
                    dve.wait_ge(w_ready, n + 1)
                    part = w[:, n % RING, off:off + P]
                    nc.vector.scalar_tensor_tensor(out=part, in0=part, scalar=3e38, in1=g.strict[:],
                                                   op0=ALU.min, op1=ALU.mult).then_inc(w_masked, 1)

            def move_y(n):
                h, chain, c, j, off, first, last = units[n]
                if last:
                    dve.wait_ge(pv_done, n + 1)
                    nc.vector.tensor_copy(qT[:, h, 512 * c:512 * c + 512],
                                          g.bank[6 + chain % 2][:]).then_inc(y_moved, 1)

            for n in range(N + 5):
                if 0 <= n - 1 < N:
                    softplus(n - 1)
                if 0 <= n - 3 < N:
                    mask_w(n - 3)
                if n >= 5:
                    move_y(n - 5)

        @block.scalar
        def _(act):
            def log_part(n):
                off = units[n][4]
                part = e[:, n % RING, off:512]
                act.wait_ge(z_ready, n + 1)
                if n >= RING:
                    act.wait_ge(u_ready, n - RING + 1)
                nc.scalar.activation(part, zb(n, off), ACT.Abs).then_inc(abs_ready, 1)
                act.wait_ge(abs_ready, n + 1)
                nc.scalar.activation(part, part, ACT.Exp, scale=-1.0).then_inc(exp_ready, 1)
                act.wait_ge(exp_ready, n + 1)
                nc.scalar.activation(part, part, ACT.Ln, bias=1.0).then_inc(ln_ready, 1)

            def weights(n):
                off = units[n][4]
                act.wait_ge(s_ready, n + 1)
                if n >= RING:
                    act.wait_ge(pv_done, n - RING + 1)
                nc.scalar.activation(w[:, n % RING, off:512], zb(n, off), ACT.Exp).then_inc(w_ready, 1)

            nc.scalar.preload_act_table_set("natural_log_exp_and_others")
            for n in range(N + 2):
                if n < N:
                    log_part(n)
                if n >= 2:
                    weights(n - 2)

        @block.gpsimd
        def _(pool):
            for n in range(N):
                off, first = units[n][4], units[n][5]
                pool.wait_ge(u_ready, n + 1)
                if n >= 2:
                    pool.wait_ge(s_ready, n - 1)
                if first:
                    ins = pool.tensor_copy(acc[:, n % 3, off:512], u[:, n % RING, off:512])
                else:
                    before = units[n - 1][4]
                    pool.wait_ge(acc_ready, n)
                    ins = pool.tensor_tensor(acc[:, n % 3, before:512], acc[:, (n - 1) % 3, before:512],
                                             u[:, n % RING, before:512], ALU.add)
                    if off < before:
                        ins = pool.tensor_copy(acc[:, n % 3, off:before], u[:, n % RING, off:before])
                ins.then_inc(acc_ready, 1)


def stage_sb_sample(nc, g, qT, kT, v_tok):
    N = KB + 1
    HB = NB // 2
    KR = 3
    with ExitStack() as ctx:
        sem = ctx.enter_context(stage_semaphores(nc))
        def sb(name, shape):
            return ctx.enter_context(nc.sbuf_tensor(name, shape, F32))

        kc = sb("cached_k", [P, KR, HB, 512])
        vc = sb("cached_v", [P, 2, NB, 512])
        kcT = sb("cached_kT", [P, NB, H * P])
        e = sb("s_softplus_work", [P, 2, 512])
        u = sb("s_softplus", [P, 2, 512])
        acc = sb("s_later_keys_sum", [P, 2, 512])
        w = sb("s_weights", [P, 2, 512])
        k_in = [sem(f"s_k_in{i}") for i in range(KR)]
        v_in = [sem("s_v_in0"), sem("s_v_in1")]
        turned = sem("s_turned")
        turn_moved = [sem("s_turn_moved_act"), sem("s_turn_moved_dve")]
        z_first = sem("s_z_first")
        z_ready = sem("s_z_ready")
        abs_ready = sem("s_abs_ready")
        exp_ready = sem("s_exp_ready")
        ln_ready = sem("s_ln_ready")
        u_step = sem("s_u_step")
        u_ready = sem("s_u_ready")
        s_ready = sem("s_s_ready")
        acc_ready = sem("s_acc_ready")
        w_ready = sem("s_w_ready")
        w_masked = sem("s_w_masked")
        pv_done = sem("s_pv_done")
        block = ctx.enter_context(nc.Block())
        kv = [t[0].rearrange("b (j p) h d -> j p b (h d)", p=P) for t in (g.cache_k, g.cache_v)]

        @block.sync
        def _(sp):
            def load_k(n):
                for half in range(2):
                    f = 2 * (n - 1) + half
                    if f >= KR:
                        sp.wait_ge(turned, HB * (f - KR + 1))
                    sp.dma_start(kc[:, f % KR],
                                 kv[0][KB - n][:, half * HB:(half + 1) * HB, :]).then_inc(k_in[f % KR], 16)

            load_k(1)
            load_k(2)
            for n in range(1, N):
                if n + 2 < N:
                    load_k(n + 2)
                if n >= 3:
                    sp.wait_ge(pv_done, n - 1)
                sp.dma_start(vc[:, n % 2], kv[1][KB - n]).then_inc(v_in[n % 2], 16)

        @block.tensor
        def _(pe):
            def turn(n, b):
                half, r = divmod(b, HB)
                f, t = 2 * (n - 1) + half, NB * (n - 1) + b
                pe.wait_ge(k_in[f % KR], 16 * (f // KR + 1))
                if t >= 4:
                    pe.wait_ge(turn_moved[t % 2], t // 2 - 1)
                for h in range(H):
                    last = nc.tensor.transpose(g.bank[4 + t % 4][:, h * P:(h + 1) * P],
                                               kc[:, f % KR, r, h * P:(h + 1) * P], g.ident[:])
                last.then_inc(turned, 1)

            def z(n, b):
                if n >= 2 and b == 0:
                    pe.wait_ge(w_ready, n - 1)
                if n == 0:
                    if b == 0:
                        for h in range(H):
                            last = nc.tensor.matmul(g.bank[0][:, h * P:(h + 1) * P], kT[:, h, TP:T], qT[:, h, TP:T],
                                                    start=(h == 0), stop=True, skip_group_check=True)
                        last.then_inc(z_first, 1)
                    return
                pe.wait_ge(turn_moved[b % 2], (NB * (n - 1) + b) // 2 + 1)
                for h in range(H):
                    col = h * P + b * LS
                    last = nc.tensor.matmul(g.bank[n % 2][:, col:col + LS], kcT[:, b, h * P:(h + 1) * P],
                                            qT[:, h, TP + b * LS:TP + (b + 1) * LS],
                                            start=(b == 0 and h == 0), stop=True, skip_group_check=True)
                last.then_inc(z_ready, 1)

            def s(n):
                pe.wait_ge(u_ready, n + 1)
                ins = nc.tensor.matmul(g.bank[n % 2][:], g.tri_neg[:], u[:, n % 2, :], start=False, stop=True,
                                       skip_group_check=True)
                if n:
                    pe.wait_ge(acc_ready, n)
                    ins = nc.tensor.matmul(g.bank[n % 2][:], g.neg_ones[:], acc[:, (n - 1) % 2, :], start=False,
                                           stop=True, skip_group_check=True)
                ins.then_inc(s_ready, 1)

            def pv(n, b):
                out = g.bank[2]
                if b == 0:
                    pe.wait_ge(w_ready, n + 1)
                if n == 0:
                    if b == 0:
                        pe.wait_ge(w_masked, 1)
                        for h in range(H):
                            last = nc.tensor.matmul(out[:, h * P:(h + 1) * P], v_tok[:, NT - 1, h * P:(h + 1) * P],
                                                    w[:, 0, h * P:(h + 1) * P], start=(h == 0), stop=False,
                                                    skip_group_check=True)
                        last.then_inc(pv_done, 1)
                    return
                if b == 0:
                    pe.wait_ge(v_in[n % 2], 16 * ((n + 1) // 2))
                for h in range(H):
                    col = h * P + b * LS
                    last = nc.tensor.matmul(out[:, col:col + LS], vc[:, n % 2, b, h * P:(h + 1) * P],
                                            w[:, n % 2, col:col + LS], start=False, stop=(n == N - 1),
                                            skip_group_check=True)
                if b == NB - 1:
                    last.then_inc(pv_done, 1)

            for n in range(N + 2):
                for b in range(NB):
                    if n + 1 < N:
                        turn(n + 1, b)
                    if n < N:
                        z(n, b)
                    if n >= 2:
                        pv(n - 2, b)
                    if b == NB // 2 and 0 <= n - 1 < N:
                        s(n - 1)

        def move_turned(eng, copy, n, b):
            t = NB * (n - 1) + b
            eng.wait_ge(turned, t + 1)
            if n >= 2:
                eng.wait_ge(z_ready, NB * (n - 2) + b + 1)
            copy(kcT[:, b, :], g.bank[4 + t % 4][:]).then_inc(turn_moved[b % 2], 1)

        @block.vector
        def _(dve):
            mask = g.strict_s[:].unsqueeze(1).broadcast_to([P, H, P])

            def softplus(n):
                dve.wait_ge(ln_ready, n + 1)
                if n >= 2:
                    dve.wait_ge(s_ready, n - 1)
                    dve.wait_ge(acc_ready, n - 1)
                ins = nc.vector.scalar_tensor_tensor(out=u[:, n % 2], in0=g.bank[n % 2][:], scalar=0.0,
                                                     in1=e[:, n % 2], op0=ALU.max, op1=ALU.add)
                if n == 0:
                    ins.then_inc(u_step, 1)
                    dve.wait_ge(u_step, 1)
                    part = u[:, 0].rearrange("p (h t) -> p h t", h=H)
                    ins = nc.vector.tensor_tensor(part, part, mask, ALU.mult)
                ins.then_inc(u_ready, 1)

            for n in range(N + 1):
                if n:
                    softplus(n - 1)
                for b in range(1, NB, 2):
                    if n + 1 < N:
                        move_turned(dve, nc.vector.tensor_copy, n + 1, b)
                if n == 1:
                    dve.wait_ge(w_ready, 1)
                    part = w[:, 0].rearrange("p (h t) -> p h t", h=H)
                    nc.vector.scalar_tensor_tensor(out=part, in0=part, scalar=3e38, in1=mask, op0=ALU.min,
                                                   op1=ALU.mult).then_inc(w_masked, 1)
            dve.wait_ge(pv_done, N)
            nc.vector.tensor_copy(qT[:, :, TP:T], g.bank[2][:].rearrange("p (h t) -> p h t", h=H))

        @block.scalar
        def _(act):
            nc.scalar.preload_act_table_set("natural_log_exp_and_others")
            def log_part(n):
                if n:
                    act.wait_ge(z_ready, NB * n)
                else:
                    act.wait_ge(z_first, 1)
                if n >= 2:
                    act.wait_ge(u_ready, n - 1)
                nc.scalar.activation(e[:, n % 2], g.bank[n % 2][:], ACT.Abs).then_inc(abs_ready, 1)
                act.wait_ge(abs_ready, n + 1)
                nc.scalar.activation(e[:, n % 2], e[:, n % 2], ACT.Exp, scale=-1.0).then_inc(exp_ready, 1)
                act.wait_ge(exp_ready, n + 1)
                nc.scalar.activation(e[:, n % 2], e[:, n % 2], ACT.Ln, bias=1.0).then_inc(ln_ready, 1)

            def weights(n):
                act.wait_ge(s_ready, n + 1)
                if n >= 2:
                    act.wait_ge(pv_done, n - 1)
                nc.scalar.activation(w[:, n % 2], g.bank[n % 2][:], ACT.Exp).then_inc(w_ready, 1)

            for n in range(N + 1):
                if n:
                    log_part(n - 1)
                for b in range(0, NB, 2):
                    if n + 1 < N:
                        move_turned(act, nc.scalar.copy, n + 1, b)
                    if n and b == NB - 4:
                        weights(n - 1)

        @block.gpsimd
        def _(pool):
            for n in range(N):
                pool.wait_ge(u_ready, n + 1)
                if n >= 2:
                    pool.wait_ge(s_ready, n)
                if n == 0:
                    pool.tensor_copy(acc[:, 0], u[:, 0]).then_inc(acc_ready, 1)
                else:
                    pool.wait_ge(acc_ready, n)
                    pool.tensor_tensor(acc[:, n % 2], acc[:, (n - 1) % 2], u[:, n % 2],
                                       ALU.add).then_inc(acc_ready, 1)


def stage_ml_project(nc, g, xT, m):
    with ExitStack() as ctx:
        sem = ctx.enter_context(stage_semaphores(nc))
        def sb(name, shape):
            return ctx.enter_context(nc.sbuf_tensor(name, shape, F32))

        NC = 16
        w = sb("w_ml", [P, 2, DT, 512])
        w_gates = sb("w_ml_gates", [P, DT, 2, 32])
        bias = sb("ml_bias", [P, 2, 512])
        gate_bias = sb("ml_gate_bias", [H, 2])
        w_first = [sem(f"m_w_first{k}") for k in range(DT)]
        w_loaded = [sem(f"m_w{i}") for i in range(3)]
        gates_zeroed = sem("m_gates_zeroed")
        gates_in = sem("m_gates_in")
        bias_in = sem("m_bias_in")
        zeroed = sem("m_zeroed")
        prod = sem("m_prod")
        tok_moved = sem("m_tok_moved")
        feat_moved = sem("m_feat_moved")
        k_turned = sem("m_k_turned")
        k_moved = sem("m_k_moved")
        keep = sb("keep_row", [H, T])
        b, mm = sb("b_row", [H, T]), sb("m_row", [H, T])
        spare = m.k_tok[0:H].rearrange("h i d -> h (i d)")
        lf2, ig2 = spare[:, 0:T], spare[:, T:2 * T]
        m_prev = sb("m_prev", [H, NC])
        w_end = sb("w_end", [H, NC])
        tmp = sb("start_tmp", [H, NB])
        step = sem("g_step")
        keep_ready = sem("g_keep_ready")
        m0_in = sem("g_m0_in")
        f_abs = sem("g_f_abs")
        f_ln = sem("g_f_ln")
        turned = sem("g_turned")
        cols_moved = sem("g_cols_moved")
        m_out = sem("g_m_out")
        m_ready = sem("g_m_ready")
        rows_ready = sem("g_rows_ready")
        rows_exp = sem("g_rows_exp")
        sig = sem("g_sig")
        norm_in = sem("g_norm_in")
        block = ctx.enter_context(nc.Block())
        w_in_t = g.w_in[0].rearrange("(k p) n -> p k n", p=P)
        NBK = 6
        NTOK = 2 * NT
        NG = 3

        def parts(row):
            return (row[:, 0:TP].rearrange("h (c t) -> h c t", c=8),
                    row[:, TP:T].rearrange("h (c t) -> h c t", c=NB))

        @block.sync
        def _(sp):
            sp.dma_start(gate_bias[:], g.b_in[0, O_MI:O_MI + 2 * H].rearrange("(a h) -> h a", h=H),
                         allow_slow_non_contiguous=True).then_inc(gates_in, 16)
            sp.wait_ge(gates_zeroed, 1)
            for a in range(2):
                sp.dma_start(w_gates[:, :, a, 0:H], w_in_t[:, :, O_MI + a * H:O_MI + (a + 1) * H],
                             allow_slow_non_contiguous=True).then_inc(gates_in, 16)
            sp.dma_start(m_prev[:, 8:16], g.state_m[0].rearrange("b h -> h b"),
                         allow_slow_non_contiguous=True).then_inc(m0_in, 16)
            sp.dma_start(m.norm_g[:], g.ml_norm_g.broadcast_to([P, 512])).then_inc(norm_in, 16)
            for s, off in enumerate((O_MV, O_MO, O_MQ)):
                if s == 2:
                    sp.wait_ge(prod, NG + NTOK - 1)
                if s == 0:
                    for k in range(DT):
                        sp.dma_start(w[:, s, k], w_in_t[:, k, off:off + 512]).then_inc(w_first[k], 16)
                else:
                    sp.dma_start(w[:, s % 2], w_in_t[:, :, off:off + 512]).then_inc(w_loaded[s], 16)
                if s == 0:
                    sp.dma_start(bias[:].rearrange("p a n -> p (a n)"),
                                 g.b_in[0:1, O_MV:O_MV + 1024].broadcast_to([P, 1024])).then_inc(bias_in, 16)
            sp.wait_ge(m_ready, 1)
            sp.dma_start(g.o_m_p[0].rearrange("b h -> h b"), mm[:, TP - 1:TP],
                         allow_slow_non_contiguous=True).then_inc(m_out, 16)
            sp.dma_start(g.o_m_s[0].rearrange("b h -> h b"), mm[:, TP + LS - 1:T:LS],
                         allow_slow_non_contiguous=True).then_inc(m_out, 16)
            sp.wait_ge(m_out, 32)

        @block.gpsimd
        def _(pool):
            pool.memset(w_gates[:], 0.0).then_inc(gates_zeroed, 1)
            pool.memset(keep[:], 1.0).then_inc(keep_ready, 1)
            pool.wait_ge(keep_ready, 1)
            pool.memset(keep[:, 0:TP:P], 0.0)
            pool.memset(keep[:, TP:T:LS], 0.0).then_inc(keep_ready, 1)
            pool.memset(m.qz[:], 0.0).then_inc(zeroed, 1)
            pool.memset(m.v_aug[:, :, :, HD:HD + 1], 1.0)
            pool.wait_ge(norm_in, 16)
            for i in range(NT):
                pool.wait_ge(sig, i + 1)
                pool.tensor_tensor(m.o_gate[:, i, :], m.o_gate[:, i, :], m.norm_g[:], ALU.mult)

        @block.tensor
        def _(pe):
            n = 0

            def bank_free(n):
                last = n - NBK
                if 0 <= last < NG:
                    pe.wait_ge(feat_moved, last + 1)
                elif NG <= last < NG + NTOK:
                    pe.wait_ge(tok_moved, last + 1 - NG)
                elif last >= NG + NTOK:
                    pe.wait_ge(feat_moved, last + 1 - NTOK)

            def turn_gates():
                pe.wait_ge(rows_exp, 1)
                for q, row in enumerate((m.ig, lf2, m.fg, ig2)):
                    for i in range(NT):
                        col = (q * NT + i) * H
                        last = nc.tensor.transpose(g.bank[6][:, col:col + H], row[:, i * P:(i + 1) * P],
                                                   g.ident[0:H, 0:H])
                last.then_inc(turned, 1)
                for h in range(H):
                    last = nc.tensor.matmul(g.bank[7][:, h * NC:(h + 1) * NC], g.sel[:, h, :], m_prev[:],
                                            start=True, stop=True)
                last.then_inc(turned, 1)

            pe.wait_ge(gates_in, 48)
            for lo, hi in CHUNKS:
                bank_free(n)
                for k in range(DT):
                    last = nc.tensor.matmul(g.bank[n % NBK][0:64, 0:hi - lo],
                                            w_gates[:, k].rearrange("p a c -> p (a c)"), xT[:, k, lo:hi],
                                            start=(k == 0), stop=(k == DT - 1))
                last.then_inc(prod, 1)
                n += 1
            for i in range(NT):
                if i == NT - 1:
                    turn_gates()
                for s in range(2):
                    if s:
                        pe.wait_ge(w_loaded[s], 16)
                    bank_free(n)
                    for k in range(DT):
                        if n == NG:
                            pe.wait_ge(w_first[k], 16)
                        last = nc.tensor.matmul(g.bank[n % NBK][:], xT[:, k, i * P:(i + 1) * P], w[:, s, k, :],
                                                start=(k == 0), stop=(k == DT - 1))
                    last.then_inc(prod, 1)
                    n += 1
            pe.wait_ge(w_loaded[2], 16)
            for tile in (2, 3, 0, 1):
                for lo, hi in CHUNKS:
                    bank_free(n)
                    for k in range(DT):
                        last = nc.tensor.matmul(g.bank[n % NBK][:, 0:hi - lo], w[:, 0, k, tile * P:(tile + 1) * P],
                                                xT[:, k, lo:hi], start=(k == 0), stop=(k == DT - 1))
                    last.then_inc(prod, 1)
                    n += 1
            pe.wait_ge(feat_moved, NG + 6)
            pe.wait_ge(cols_moved, 2)
            for i in range(NT):
                if i >= 4:
                    pe.wait_ge(k_moved, i // 2 - 1)
                off = (i % 2) * 256
                for pair in range(2):
                    last = nc.tensor.transpose(g.bank[6 + i // 2 % 2][:, off + pair * P:off + (pair + 1) * P],
                                               m.kT[:, pair, i * P:(i + 1) * P], g.ident[:])
                if i % 2 or i == NT - 1:
                    last.then_inc(k_turned, 1)

        @block.vector
        def _(dve):
            count = [0]

            def link(ins):
                count[0] += 1
                ins.then_inc(step, 1)
                dve.wait_ge(step, count[0])

            dve.wait_ge(m0_in, 16)
            link(nc.vector.memset(m_prev[:, 0:1], 0.0))
            dve.wait_ge(f_ln, 1)
            link(nc.vector.scalar_tensor_tensor(out=m.fg[:], in0=m.fg[:], scalar=0.0, in1=b[:], op0=ALU.min,
                                                op1=ALU.subtract))
            dve.wait_ge(keep_ready, 2)
            link(nc.vector.tensor_tensor_scan(b[:], keep[:], m.fg[:], 0.0, ALU.mult, ALU.add))
            link(nc.vector.tensor_copy(lf2[:], m.fg[:]))
            link(nc.vector.tensor_copy(ig2[:], m.ig[:]))
            dve.wait_ge(m0_in, 16)
            link(nc.vector.tensor_tensor(tmp[:], m.fg[:, TP:T:LS], m_prev[:, 8:16], ALU.add))
            link(nc.vector.tensor_tensor(ig2[:, TP:T:LS], tmp[:], m.ig[:, TP:T:LS], ALU.max))
            link(nc.vector.memset(lf2[:, TP:T:LS], NEG))
            link(nc.vector.tensor_tensor_scan(mm[:], lf2[:], ig2[:], 0.0, ALU.add, ALU.max))
            nc.vector.tensor_copy(m_prev[:, 1:8], mm[:, P - 1:TP - P:P]).then_inc(m_ready, 1)
            link(nc.vector.tensor_tensor(m.ig[:], m.ig[:], b[:], ALU.subtract))
            link(nc.vector.tensor_tensor(m.w[:], b[:], mm[:], ALU.subtract))
            link(nc.vector.tensor_copy(w_end[:, 0:8], m.w[:, P - 1:TP:P]))
            link(nc.vector.tensor_copy(w_end[:, 8:16], m.w[:, TP + LS - 1:T:LS]))
            for n, (o, a, c) in enumerate(zip(parts(lf2), parts(m.w), (m_prev[:, 0:8], m_prev[:, 8:16]))):
                nc.vector.tensor_tensor(o, a, c.unsqueeze(2).broadcast_to(list(a.shape)), ALU.add)
            for o, a, c in zip(parts(ig2), parts(m.ig), (w_end[:, 0:8], w_end[:, 8:16])):
                link(nc.vector.tensor_tensor(o, a, c.unsqueeze(2).broadcast_to(list(a.shape)), ALU.add))
            nc.vector.tensor_tensor(m_prev[:], m_prev[:], w_end[:], ALU.add).then_inc(rows_ready, 1)
            dve.wait_ge(bias_in, 16)
            for n in range(NG, NG + NTOK):
                i, s = divmod(n - NG, 2)
                dve.wait_ge(prod, n + 1)
                if s == 0:
                    nc.vector.tensor_tensor(m.v_aug[:, i, :, 0:HD],
                                            g.bank[n % NBK][:].rearrange("p (h e) -> p h e", h=H),
                                            bias[:, 0, :].rearrange("p (h e) -> p h e", h=H),
                                            ALU.add).then_inc(tok_moved, 1)
                else:
                    nc.vector.tensor_tensor(m.o_gate[:, i, :], g.bank[n % NBK][:], bias[:, 1, :],
                                            ALU.add).then_inc(tok_moved, 1)
            dve.wait_ge(turned, 2)
            nc.vector.tensor_copy(m.cols[:].rearrange("p q i h -> p (q i h)"), g.bank[6][:, 0:4 * NT * H]
                                  ).then_inc(cols_moved, 1)
            nc.vector.tensor_copy(m.s_old[:].rearrange("p h c -> p (h c)"), g.bank[7][:, 0:H * NC]
                                  ).then_inc(cols_moved, 1)
            for t in range(5):
                dve.wait_ge(k_turned, t + 1)
                tiles = 2 if t < 4 else 1
                nc.vector.tensor_copy(m.k_tok[:, 2 * t:2 * t + tiles, :],
                                      g.bank[6 + t % 2][:, 0:tiles * 256].rearrange("p (i d) -> p i d", i=tiles)
                                      ).then_inc(k_moved, 1)

        @block.scalar
        def _(act):
            n = 0
            for lo, hi in CHUNKS:
                act.wait_ge(prod, n + 1)
                for a, row in enumerate((m.ig, m.fg)):
                    last = nc.scalar.activation(row[:, lo:hi], g.bank[n % NBK][32 * a:32 * a + H, 0:hi - lo],
                                                ACT.Identity, bias=gate_bias[:, a:a + 1])
                last.then_inc(feat_moved, 1)
                n += 1
            act.wait_ge(feat_moved, NG)
            nc.scalar.activation(b[:], m.fg[:], ACT.Abs).then_inc(f_abs, 1)
            act.wait_ge(f_abs, 1)
            nc.scalar.activation(b[:], b[:], ACT.Exp, scale=-1.0).then_inc(f_abs, 1)
            act.wait_ge(f_abs, 2)
            nc.scalar.activation(b[:], b[:], ACT.Ln, bias=1.0).then_inc(f_ln, 1)
            act.wait_ge(rows_ready, 1)
            nc.scalar.activation(lf2[:], lf2[:], ACT.Exp)
            nc.scalar.activation(ig2[:], ig2[:], ACT.Exp)
            nc.scalar.activation(m_prev[:], m_prev[:], ACT.Exp)
            nc.scalar.activation(m.fg[:], mm[:], ACT.Exp, scale=-1.0).then_inc(rows_exp, 1)
            for i in range(NT):
                act.wait_ge(tok_moved, 2 * i + 2)
                nc.scalar.activation(m.o_gate[:, i, :], m.o_gate[:, i, :], ACT.Sigmoid).then_inc(sig, 1)
            n = NG + NTOK
            act.wait_ge(zeroed, 1)
            for tile in (2, 3, 0, 1):
                for lo, hi in CHUNKS:
                    act.wait_ge(prod, n + 1)
                    ps = g.bank[n % NBK][:, 0:hi - lo]
                    if tile >= 2:
                        last = nc.scalar.activation(m.kT[:, tile - 2, lo:hi], ps, ACT.Identity,
                                                    bias=g.mkbias[:, tile - 2:tile - 1], scale=ML_SCALE)
                    else:
                        col = V_BIN + O_MQ // P + tile
                        for half in range(2):
                            r = slice(64 * half, 64 * half + 64)
                            last = nc.scalar.activation(m.qz[r, 2 * tile + half, lo:hi], ps[r, :], ACT.Identity,
                                                        bias=g.vec[r, col:col + 1])
                    last.then_inc(feat_moved, 1)
                    n += 1


def stage_mlstm(nc, g, m, ycT):
    U, S_IN, E_M, G_W = range(4)
    A = HD + 1
    with ExitStack() as ctx:
        sem = ctx.enter_context(stage_semaphores(nc))
        def sb(name, shape):
            return ctx.enter_context(nc.sbuf_tensor(name, shape, F32))

        c_state = sb("c_state", [P, 2, A])
        cs = sb("c_sample", [P, NB, 2, A])
        qs = sb("q_by_request", [P, H, NB, P])
        dexp = sb("pair_weights", [P, H, P])
        wqk = sb("wqk", [P, H, P])
        kg = sb("weighted_k", [P, 2, 256])
        kgb = sb("weighted_k_by_request", [P, NB, 256])
        inter = sb("inter", [P, H, A])
        num = sb("num", [P, H, A])
        den = sb("den", [P, 3, H])
        hc = sb("hc", [P, NT, 512])
        stats = sb("hc_stats", [P, NT, H, 6])
        mv = sb("hc_mean_var", [P, NT, H, 2])
        rstd = sb("hc_rstd", [P, NT, H, 1])
        seg = sb("request_mask", [P, NB])
        c_in = sem("r_c_in")
        filled = sem("r_filled")
        qs_ready = sem("r_qs_ready")
        c_zero = sem("r_c_zero")
        w_bank = sem("r_w_bank")
        s_bank = sem("r_s_bank")
        dexp_ready = sem("r_dexp_ready")
        wqk_ready = sem("r_wqk_ready")
        kg_ready = sem("r_kg_ready")
        inter_prod = sem("r_inter_prod")
        inter_ready = sem("r_inter_ready")
        intra_prod = sem("r_intra_prod")
        num_ready = sem("r_num_ready")
        c_prod = sem("r_c_prod")
        c_ready = sem("r_c_ready")
        step = sem("r_step")
        var_ready = sem("r_var_ready")
        std_ready = sem("r_std_ready")
        yc_ready = sem("r_yc_ready")
        yc_turned = sem("r_yc_turned")
        yc_moved = sem("r_yc_moved")
        states_out = sem("r_states_out")
        block = ctx.enter_context(nc.Block())

        @block.sync
        def _(sp):
            for two in range(2):
                r = slice(64 * two, 64 * two + 64)
                for pair in range(2):
                    sp.dma_start(cs[r, :, pair, 0:HD], g.state_c[0, :, 2 * pair + two].rearrange("b d e -> d b e")
                                 ).then_inc(c_in, 16)
                    sp.dma_start(cs[r, :, pair, HD], g.state_n[0, :, 2 * pair + two].rearrange("b d -> d b"),
                                 allow_slow_non_contiguous=True).then_inc(c_in, 16)
            sp.wait_ge(c_ready, 8)
            for two in range(2):
                r = slice(64 * two, 64 * two + 64)
                sp.dma_start(g.o_c_p[0, 0, two::2].rearrange("q d e -> d q e"), c_state[r, :, 0:HD]
                             ).then_inc(states_out, 16)
                sp.dma_start(g.o_n_p[0, 0, two::2].rearrange("q d -> d q"), c_state[r, :, HD],
                             allow_slow_non_contiguous=True).then_inc(states_out, 16)
            sp.wait_ge(c_ready, 8 + NB)
            for two in range(2):
                r = slice(64 * two, 64 * two + 64)
                for pair in range(2):
                    sp.dma_start(g.o_c_s[0, :, 2 * pair + two].rearrange("b d e -> d b e"), cs[r, :, pair, 0:HD]
                                 ).then_inc(states_out, 16)
                    sp.dma_start(g.o_n_s[0, :, 2 * pair + two].rearrange("b d -> d b"), cs[r, :, pair, HD],
                                 allow_slow_non_contiguous=True).then_inc(states_out, 16)
            sp.wait_ge(states_out, 16 * 12)

        @block.gpsimd
        def _(pool):
            pool.memset(c_state[:], 0.0).then_inc(c_zero, 1)
            pool.memset(seg[:], 1.0).then_inc(filled, 1)
            pool.memset(qs[:], 0.0).then_inc(filled, 1)
            pool.wait_ge(filled, 2)
            pool.affine_select(out=seg[:], in_=seg[:], compare_op=ALU.is_ge, fill=0.0, base=0,
                               pattern=[[-LS, NB]], channel_multiplier=1).then_inc(filled, 1)
            pool.wait_ge(filled, 3)
            pool.affine_select(out=seg[:], in_=seg[:], compare_op=ALU.is_ge, fill=0.0, base=LS - 1,
                               pattern=[[LS, NB]], channel_multiplier=-1).then_inc(filled, 1)
            for b in range(NB):
                last = pool.tensor_copy(qs[:, :, b, b * LS:(b + 1) * LS], m.qz[:, :, TP + b * LS:TP + (b + 1) * LS])
            last.then_inc(qs_ready, 1)
            for i in range(NT):
                if i >= 2:
                    pool.wait_ge(c_prod, i - 1)
                pool.tensor_tensor(kg[:, i % 2].rearrange("p (h d) -> p h d", h=H),
                                   m.k_tok[:, i, :].rearrange("p (h d) -> p h d", h=H),
                                   m.cols[:, G_W, i, :].unsqueeze(2).broadcast_to([P, H, QD]),
                                   ALU.mult).then_inc(kg_ready, 1)
            pool.wait_ge(kg_ready, NT)
            pool.wait_ge(filled, 4)
            for b in range(NB):
                last = pool.tensor_scalar(kgb[:, b], kg[:, (NT - 1) % 2], seg[:, b:b + 1], None, ALU.mult)
            last.then_inc(kg_ready, 1)

        @block.tensor
        def _(pe):
            def scores(i):
                cols = slice(i * P, (i + 1) * P)
                mask = g.causal_s if i == NT - 1 else g.causal
                if i:
                    pe.wait_ge(dexp_ready, i)
                for h in range(H):
                    out = g.bank[0][:, h * P:(h + 1) * P]
                    nc.tensor.matmul(out, g.sel[:, h, :], m.w[:, cols], start=True, stop=False)
                    last = nc.tensor.matmul(out, g.ident[:], mask[:], start=False, stop=True)
                last.then_inc(w_bank, 1)
                if i:
                    pe.wait_ge(wqk_ready, i)
                for h in range(H):
                    last = nc.tensor.matmul(g.bank[1][:, h * P:(h + 1) * P], m.kT[:, h // 2, cols],
                                            m.qz[:, h, cols], start=True, stop=True)
                last.then_inc(s_bank, 1)

            scores(0)
            for i in range(NT):
                cols = slice(i * P, (i + 1) * P)
                if i:
                    pe.wait_ge(inter_ready, i)
                    if i < NT - 1:
                        pe.wait_ge(c_ready, i)
                    else:
                        pe.wait_ge(c_in, 16 * 8)
                        pe.wait_ge(qs_ready, 1)
                else:
                    pe.wait_ge(c_zero, 1)
                for h in range(H):
                    out = g.bank[2 + h // 2][:, (h % 2) * A:(h % 2 + 1) * A]
                    if i < NT - 1:
                        last = nc.tensor.matmul(out, m.qz[:, h, cols], c_state[:, h // 2, :], start=True, stop=True)
                    else:
                        for b in range(NB):
                            last = nc.tensor.matmul(out, qs[:, h, b, :], cs[:, b, h // 2, :],
                                                    start=(b == 0), stop=(b == NB - 1))
                last.then_inc(inter_prod, 1)
                if i < NT - 1:
                    pe.wait_ge(kg_ready, i + 1)
                    if i:
                        pe.wait_ge(c_ready, i)
                    for h in range(H):
                        last = nc.tensor.matmul(g.bank[6 + h // 2][:, (h % 2) * A:(h % 2 + 1) * A],
                                                kg[:, i % 2, (h // 2) * P:(h // 2 + 1) * P], m.v_aug[:, i, h, :],
                                                start=True, stop=True)
                    last.then_inc(c_prod, 1)
                if i + 1 < NT:
                    scores(i + 1)
                pe.wait_ge(wqk_ready, i + 1)
                if i:
                    pe.wait_ge(num_ready, i)
                for h in range(H):
                    last = nc.tensor.matmul(g.bank[4 + h // 2][:, (h % 2) * A:(h % 2 + 1) * A], wqk[:, h, :],
                                            m.v_aug[:, i, h, :], start=True, stop=True)
                last.then_inc(intra_prod, 1)
            pe.wait_ge(kg_ready, NT + 1)
            pe.wait_ge(inter_ready, NT)
            for b in range(NB):
                if b == 0:
                    pe.wait_ge(c_ready, 8)
                if b == 1:
                    pe.wait_ge(dexp_ready, NT)
                if b >= 2:
                    pe.wait_ge(c_ready, 8 + b - 1)
                for h in range(H):
                    last = nc.tensor.matmul(g.bank[(6, 0)[b % 2] + h // 2][:, (h % 2) * A:(h % 2 + 1) * A],
                                            kgb[:, b, (h // 2) * P:(h // 2 + 1) * P], m.v_aug[:, NT - 1, h, :],
                                            start=True, stop=True)
                last.then_inc(c_prod, 1)
            for i in range(NT):
                pe.wait_ge(yc_ready, i + 1)
                if i >= 2:
                    pe.wait_ge(yc_moved, i - 1)
                for h in range(H):
                    last = nc.tensor.transpose(g.bank[2 + i % 2][:, h * P:(h + 1) * P],
                                               hc[:, i, h * P:(h + 1) * P], g.ident[:])
                last.then_inc(yc_turned, 1)

        @block.scalar
        def _(act):
            for i in range(NT):
                act.wait_ge(w_bank, i + 1)
                if i:
                    act.wait_ge(wqk_ready, i)
                for h in range(H):
                    last = nc.scalar.activation(dexp[:, h, :], g.bank[0][:, h * P:(h + 1) * P], ACT.Exp,
                                                bias=m.cols[:, U, i, h:h + 1])
                last.then_inc(dexp_ready, 1)
                act.wait_ge(inter_prod, i + 1)
                if i:
                    act.wait_ge(num_ready, i)
                for h in range(H):
                    last = nc.scalar.activation(inter[:, h, :], g.bank[2 + h // 2][:, (h % 2) * A:(h % 2 + 1) * A],
                                                ACT.Copy, scale=m.cols[:, S_IN, i, h:h + 1])
                last.then_inc(inter_ready, 1)
            act.wait_ge(var_ready, 1)
            nc.scalar.activation(rstd[:], mv[:, :, :, 1:2], ACT.Sqrt).then_inc(std_ready, 1)
            for i in range(NT):
                act.wait_ge(yc_turned, i + 1)
                nc.scalar.copy(ycT[:, :, i * P:(i + 1) * P],
                               g.bank[2 + i % 2][:].rearrange("p (h t) -> p h t", h=H)).then_inc(yc_moved, 1)

        @block.vector
        def _(dve):
            count = [0]

            def link(ins):
                count[0] += 1
                ins.then_inc(step, 1)
                dve.wait_ge(step, count[0])

            def new_state(state, c, bank0):
                for h in range(H):
                    r = slice(64 * (h % 2), 64 * (h % 2) + 64)
                    last = nc.vector.scalar_tensor_tensor(
                        out=state[r, h // 2, :], in0=state[r, h // 2, :], scalar=m.s_old[r, h, c:c + 1],
                        in1=g.bank[bank0 + h // 2][r, (h % 2) * A:(h % 2 + 1) * A], op0=ALU.mult, op1=ALU.add)
                last.then_inc(c_ready, 1)

            for i in range(NT):
                dve.wait_ge(dexp_ready, i + 1)
                dve.wait_ge(s_bank, i + 1)
                if i:
                    dve.wait_ge(intra_prod, i)
                nc.vector.tensor_tensor(wqk[:].rearrange("p h t -> p (h t)"), dexp[:].rearrange("p h t -> p (h t)"),
                                        g.bank[1][:], ALU.mult).then_inc(wqk_ready, 1)
                if i < NT - 1:
                    dve.wait_ge(c_prod, i + 1)
                    if i:
                        dve.wait_ge(c_ready, i)
                    new_state(c_state, i, 6)
                dve.wait_ge(inter_ready, i + 1)
                dve.wait_ge(intra_prod, i + 1)
                for pair in range(2):
                    last = nc.vector.tensor_tensor(num[:, 2 * pair:2 * pair + 2, :].rearrange("p h a -> p (h a)"),
                                                   inter[:, 2 * pair:2 * pair + 2, :].rearrange("p h a -> p (h a)"),
                                                   g.bank[4 + pair][:, 0:2 * A], ALU.add)
                last.then_inc(num_ready, 1)
                dve.wait_ge(num_ready, i + 1)
                link(nc.vector.tensor_scalar(den[:, 0], num[:, :, HD], -1.0, None, ALU.mult))
                link(nc.vector.tensor_tensor(den[:, 1], den[:, 0], num[:, :, HD], ALU.max))
                link(nc.vector.tensor_tensor(den[:, 0], den[:, 1], m.cols[:, E_M, i, :], ALU.max))
                link(nc.vector.reciprocal(den[:, 2], den[:, 0]))
                link(nc.vector.tensor_tensor(hc[:, i, :].rearrange("p (h e) -> p h e", h=H), num[:, :, 0:HD],
                                             den[:, 2].unsqueeze(2).broadcast_to([P, H, HD]), ALU.mult))
                for h in range(H):
                    last = nc.vector.bn_stats(stats[:, i, h, :], hc[:, i, h * P:(h + 1) * P])
                link(last)
                for h in range(H):
                    last = nc.vector.bn_aggr(mv[:, i, h, :], stats[:, i, h, :])
                if i == NT - 1:
                    link(last)
            for b in range(NB):
                dve.wait_ge(c_prod, 8 + b + 1)
                new_state(cs[:, b], 8 + b, (6, 0)[b % 2])
            nc.vector.tensor_scalar(mv[:, :, :, 1:2], mv[:, :, :, 1:2], LN_EPS, None, ALU.add).then_inc(var_ready, 1)
            dve.wait_ge(std_ready, 1)
            link(nc.vector.reciprocal(rstd[:], rstd[:]))
            for i in range(NT):
                for h in range(H):
                    part = hc[:, i, h * P:(h + 1) * P]
                    last = nc.vector.tensor_scalar(part, part, mv[:, i, h, 0:1], rstd[:, i, h, :], ALU.subtract,
                                                   ALU.mult)
                link(last)
                nc.vector.tensor_tensor(hc[:, i, :], hc[:, i, :], m.o_gate[:, i, :], ALU.mult).then_inc(yc_ready, 1)


def stage_mix(nc, g, xT, yT):
    PAIRS = [(r, m) for r in (1, 2, 0) for m in range(DT)]
    units = [(r, m, c) for r, m in PAIRS for c in range(len(CHUNKS3))]
    C = len(CHUNKS3)
    NSET, RING, WR = 4, 4, 3
    with ExitStack() as ctx:
        sem = ctx.enter_context(stage_semaphores(nc))
        def sb(name, shape, dt=F32):
            return ctx.enter_context(nc.sbuf_tensor(name, shape, dt))

        x_hi = sb("xT_high", [P, DT, T], F32R)
        x_lo = sb("xT_low", [P, DT, T], F32R)
        wg = sb("w_gates", [P, WR, DT, P])
        wg_hi = sb("w_gates_high", [P, 2, DT, P], F32R)
        wg_lo = sb("w_gates_low", [P, 2, DT, P], F32R)
        wp = sb("w_proj", [P, WR, DT, P])
        sig = sb("gate_sigmoid", [P, RING, CHUNK3])
        yb_done, yc_done = C * DT, 2 * C * DT
        ya_in = [sem("x_ya_in0"), sem("x_ya_in1")]
        wg_in = [sem(f"x_wg_in{i}") for i in range(WR)]
        wp_in = [sem(f"x_wp_in{i}") for i in range(WR)]
        x_high = sem("x_x_high")
        x_split = sem("x_x_split")
        w_high = sem("x_w_high")
        w_split = sem("x_w_split")
        prod = sem("x_prod")
        sig_ready = sem("x_sig_ready")
        mul_ready = sem("x_mul_ready")
        add_ready = sem("x_add_ready")
        block = ctx.enter_context(nc.Block())
        mixT = xT
        SRC = ((g.w_pa, DT, 0), (g.w_pb, H, 0), (g.w_pc, H, H))

        def adds(n):
            return max(n - C * DT, 0)

        @block.sync
        def _(sp):
            w_in_t = g.w_in[0].rearrange("(k p) n -> p k n", p=P)
            for j, (r, m) in enumerate(PAIRS):
                if j >= WR:
                    sp.wait_ge(w_split, j - WR + 1)
                sp.dma_start(wg[:, j % WR], w_in_t[:, :, O_MG + r * D + m * P:O_MG + r * D + (m + 1) * P]
                             ).then_inc(wg_in[j % WR], 16)
                if j >= WR:
                    sp.wait_ge(prod, C * (j - WR + 1))
                w, kn, _ = SRC[r]
                sp.dma_start(wp[:, j % WR, 0:kn, :], w[0].rearrange("(k p) n -> p k n", p=P)[:, :, m * P:(m + 1) * P]
                             ).then_inc(wp_in[j % WR], 16)
                for half, done in enumerate((yb_done, yc_done)):
                    if C * (j - WR + 1) == done:
                        sp.dma_start(yT[:, half * H:(half + 1) * H, :],
                                     g.yaT_d.rearrange("k p t -> p k t")[:, half * H:(half + 1) * H, :]
                                     ).then_inc(ya_in[half], 16)

        @block.tensor
        def _(pe):
            for n, (r, m, c) in enumerate(units):
                lo, hi = c * CHUNK3, (c + 1) * CHUNK3
                j = n // C
                if n >= NSET:
                    pe.wait_ge(mul_ready, n - NSET + 1)
                gate, proj = g.bank[2 * (n % NSET)][:, 0:CHUNK3], g.bank[2 * (n % NSET) + 1][:, 0:CHUNK3]

                def project():
                    if c == 0:
                        pe.wait_ge(wp_in[j % WR], 16 * (j // WR + 1))
                    _, kn, first = SRC[r]
                    for k in range(kn):
                        if r == 0 and m == 0 and c == 0 and k % H == 0:
                            pe.wait_ge(ya_in[k // H], 16)
                        ins = nc.tensor.matmul(proj, wp[:, j % WR, k, :], yT[:, first + k, lo:hi], start=(k == 0),
                                               stop=(k == kn - 1))
                    return ins

                if n < C:
                    project()
                if c == 0:
                    pe.wait_ge(w_split, j + 1)
                for k in range(DT):
                    if n == 0:
                        pe.wait_ge(x_split, k + 1)
                    w_h, w_l = wg_hi[:, j % 2, k, :], wg_lo[:, j % 2, k, :]
                    nc.tensor.matmul(gate, w_h, x_hi[:, k, lo:hi], start=(k == 0), stop=False)
                    nc.tensor.matmul(gate, w_h, x_lo[:, k, lo:hi], start=False, stop=False)
                    last = nc.tensor.matmul(gate, w_l, x_hi[:, k, lo:hi], start=False, stop=(k == DT - 1))
                if n >= C:
                    last = project()
                last.then_inc(prod, 1)

        @block.scalar
        def _(act):
            def w_high_part(j):
                act.wait_ge(wg_in[j % WR], 16 * (j // WR + 1))
                if j >= 2:
                    act.wait_ge(prod, C * (j - 1))
                nc.scalar.copy(wg_hi[:, j % 2], wg[:, j % WR]).then_inc(w_high, 1)

            w_high_part(0)
            for k in range(DT):
                nc.scalar.copy(x_hi[:, k, :], xT[:, k, :]).then_inc(x_high, 1)
            w_high_part(1)
            for n, (r, m, c) in enumerate(units):
                act.wait_ge(prod, n + 1)
                if n >= RING:
                    act.wait_ge(mul_ready, n - RING + 1)
                    if adds(n - RING + 1):
                        act.wait_ge(add_ready, adds(n - RING + 1))
                nc.scalar.activation(sig[:, n % RING, :], g.bank[2 * (n % NSET)][:, 0:CHUNK3], ACT.Sigmoid,
                                     bias=g.vec[:, V_BMG + r * DT + m:V_BMG + r * DT + m + 1]).then_inc(sig_ready, 1)
                if c == C - 1 and n // C + 2 < len(PAIRS):
                    w_high_part(n // C + 2)

        @block.vector
        def _(dve):
            def w_low_part(j):
                dve.wait_ge(w_high, j + 1)
                nc.vector.tensor_tensor(wg_lo[:, j % 2], wg[:, j % WR], wg_hi[:, j % 2].bitcast(F32),
                                        ALU.subtract).then_inc(w_split, 1)

            w_low_part(0)
            for k in range(DT):
                dve.wait_ge(x_high, k + 1)
                nc.vector.tensor_tensor(x_lo[:, k, :], xT[:, k, :], x_hi[:, k, :].bitcast(F32),
                                        ALU.subtract).then_inc(x_split, 1)
            w_low_part(1)
            for n, (r, m, c) in enumerate(units):
                dve.wait_ge(sig_ready, n + 1)
                if n < C * DT:
                    dve.wait_ge(x_split, DT)
                out = mixT[:, m, c * CHUNK3:(c + 1) * CHUNK3] if n < C * DT else sig[:, n % RING, :]
                nc.vector.tensor_tensor(out, sig[:, n % RING, :], g.bank[2 * (n % NSET) + 1][:, 0:CHUNK3],
                                        ALU.mult).then_inc(mul_ready, 1)
                if c == C - 1 and n // C + 2 < len(PAIRS):
                    w_low_part(n // C + 2)

        @block.gpsimd
        def _(pool):
            for n, (r, m, c) in enumerate(units):
                lo, hi = c * CHUNK3, (c + 1) * CHUNK3
                if n >= C * DT:
                    pool.wait_ge(mul_ready, n + 1)
                    pool.tensor_tensor(mixT[:, m, lo:hi], mixT[:, m, lo:hi], sig[:, n % RING, :],
                                       ALU.add).then_inc(add_ready, 1)


def stage_out(nc, g, mixT, x1T):
    R = 3
    with ExitStack() as ctx:
        sem = ctx.enter_context(stage_semaphores(nc))
        def sb(name, shape):
            return ctx.enter_context(nc.sbuf_tensor(name, shape, F32))

        w = sb("w_out_sb", [P, DT, D])
        x = sb("x_residual", [P, R, D])
        norm = sb("ln1_scale_shift", [P, 2, D])
        zero = sb("zero_row", [1, D])
        stats = sb("ln1_stats", [P, R, 2, 6])
        mv = sb("ln1_mean_var", [P, R, 2])
        w_first = [sem(f"o_w_first{k}") for k in range(DT)]
        w_second = sem("o_w_second")
        x_in = [sem(f"o_x_in{i}") for i in range(R)]
        norm_in = sem("o_norm_in")
        prod = sem("o_prod")
        sum_ready = sem("o_sum_ready")
        stat_ready = sem("o_stat_ready")
        var_ready = sem("o_var_ready")
        std_ready = sem("o_std_ready")
        rstd_ready = sem("o_rstd_ready")
        hat_ready = sem("o_hat_ready")
        scaled = sem("o_scaled")
        x1_ready = sem("o_x1_ready")
        x1_out = [sem(f"o_x1_out{i}") for i in range(R)]
        turned = sem("o_turned")
        moved = sem("o_moved")
        zero_ready = sem("o_zero_ready")
        zero_out = sem("o_zero_out")
        block = ctx.enter_context(nc.Block())

        @block.sync
        def _(sp):
            wv = g.w_out[0].rearrange("(k p) n -> p k n", p=P)
            xp = g.x_prompt[0].rearrange("(i p) d -> i p d", p=P)
            for k in range(DT):
                sp.dma_start(w[:, k, 0:512], wv[:, k, 0:512]).then_inc(w_first[k], 16)
            sp.dma_start(w[:, :, 512:D], wv[:, :, 512:D]).then_inc(w_second, 16)
            for i in range(NT):
                if i >= R:
                    sp.wait_ge(x1_out[i % R], 16 * (i // R))
                    sp.wait_ge(turned, 2 * (i - R + 1))
                src = xp[i] if i < NT - 1 else g.x_sample.rearrange("b t d -> (b t) d")
                sp.dma_start(x[:, i % R, :], src).then_inc(x_in[i % R], 16)
                if i == 0:
                    for a, v in enumerate((g.ln1_g, g.ln1_b)):
                        sp.dma_start(norm[:, a, :], v.broadcast_to([P, D])).then_inc(norm_in, 16)

        @block.tensor
        def _(pe):
            def turn(i):
                pe.wait_ge(x1_ready, i + 1)
                for half in range(2):
                    n = 2 * i + half
                    if n >= 4:
                        pe.wait_ge(moved, n - 3)
                    for k in range(4):
                        last = nc.tensor.transpose(g.bank[4 + n % 4][:, k * P:(k + 1) * P],
                                                   x[:, i % R, (4 * half + k) * P:(4 * half + k + 1) * P], g.ident[:])
                    last.then_inc(turned, 1)

            for i in range(NT + 2):
                if i < NT:
                    for half in range(2):
                        n = 2 * i + half
                        if half:
                            pe.wait_ge(w_second, 16)
                        if n >= 4:
                            pe.wait_ge(sum_ready, n - 3)
                        for k in range(DT):
                            if n == 0:
                                pe.wait_ge(w_first[k], 16)
                            last = nc.tensor.matmul(g.bank[n % 4][:], mixT[:, k, i * P:(i + 1) * P],
                                                    w[:, k, half * 512:(half + 1) * 512], start=(k == 0),
                                                    stop=(k == DT - 1))
                        last.then_inc(prod, 1)
                if i >= 2:
                    turn(i - 2)

        @block.vector
        def _(dve):
            for i in range(NT):
                s = i % R
                dve.wait_ge(x_in[s], 16 * (i // R + 1))
                for half in range(2):
                    n = 2 * i + half
                    part = x[:, s, half * 512:(half + 1) * 512]
                    dve.wait_ge(prod, n + 1)
                    nc.vector.scalar_tensor_tensor(out=part, in0=part, scalar=ALPHA, in1=g.bank[n % 4][:],
                                                   op0=ALU.mult, op1=ALU.add).then_inc(sum_ready, 1)
                for half in range(2):
                    dve.wait_ge(sum_ready, 2 * i + half + 1)
                    nc.vector.bn_stats(stats[:, s, half, :], x[:, s, half * 512:(half + 1) * 512]
                                       ).then_inc(stat_ready, 1)
                dve.wait_ge(stat_ready, 2 * i + 2)
                nc.vector.bn_aggr(mv[:, s, :], stats[:, s].rearrange("p a b -> p (a b)")).then_inc(var_ready, 1)
                dve.wait_ge(std_ready, i + 1)
                nc.vector.reciprocal(mv[:, s, 1:2], mv[:, s, 1:2]).then_inc(rstd_ready, 1)
                dve.wait_ge(rstd_ready, i + 1)
                nc.vector.tensor_scalar(x[:, s, :], x[:, s, :], mv[:, s, 0:1], mv[:, s, 1:2], ALU.subtract,
                                        ALU.mult).then_inc(hat_ready, 1)

        @block.scalar
        def _(act):
            def move(i):
                for half in range(2):
                    n = 2 * i + half
                    act.wait_ge(turned, n + 1)
                    nc.scalar.copy(x1T[:, 4 * half:4 * half + 4, i * P:(i + 1) * P],
                                   g.bank[4 + n % 4][:].rearrange("p (k t) -> p k t", k=4)).then_inc(moved, 1)

            for i in range(NT + 1):
                if i < NT:
                    act.wait_ge(var_ready, i + 1)
                    nc.scalar.activation(mv[:, i % R, 1:2], mv[:, i % R, 1:2], ACT.Sqrt,
                                         bias=g.eps[:]).then_inc(std_ready, 1)
                if i >= 1:
                    act.wait_ge(x1_ready, i)
                    act.dma_start(g.x1_d[(i - 1) * P:i * P, :], x[:, (i - 1) % R, :]).then_inc(x1_out[(i - 1) % R], 16)
                if i >= 2:
                    move(i - 2)
            move(NT - 1)
            act.wait_ge(zero_ready, 1)
            act.dma_start(g.x1_d[T:T + 1, :], zero[:]).then_inc(zero_out, 16)
            for s in x1_out:
                act.wait_ge(s, 16 * (NT // R))
            act.wait_ge(zero_out, 16)

        @block.gpsimd
        def _(pool):
            pool.memset(zero[:], 0.0).then_inc(zero_ready, 1)
            pool.wait_ge(norm_in, 32)
            for i in range(NT):
                pool.wait_ge(hat_ready, i + 1)
                pool.tensor_tensor(x[:, i % R, :], x[:, i % R, :], norm[:, 0, :], ALU.mult).then_inc(scaled, 1)
                pool.wait_ge(scaled, i + 1)
                pool.tensor_tensor(x[:, i % R, :], x[:, i % R, :], norm[:, 1, :], ALU.add).then_inc(x1_ready, 1)


def stage_route(nc, g, x1T):
    R = 3
    with ExitStack() as ctx:
        sem = ctx.enter_context(stage_semaphores(nc))
        def sb(name, shape, dt=F32):
            return ctx.enter_context(nc.sbuf_tensor(name, shape, dt))

        rw = sb("router_w_sb", [P, DT, NE])
        rb = sb("router_bias", [P, NE])
        lg = sb("logits", [P, NT, NE])
        top = sb("top8", [P, NT, 8])
        top_i = sb("top8_index", [P, NT, 8], U32)
        top_f = sb("top8_index_f", [P, NT, TOPK])
        eid = sb("expert_ids", [P, NE])
        one_hot = sb("one_hot", [P, NT, TOPK, NE])
        picked = sb("picked", [P, NT, NE])
        rank = sb("rank", [P, NT, NE])
        before = sb("picked_before_tile", [P, NT + 1, NE])
        blocks = sb("blocks", [P, 4, NE])
        gsum = sb("gate_sum", [P, NT, 1])
        dest_f = sb("dest_f", [P, NT * TOPK])
        bid = sb("block_ids", [P, MAXBLK])
        cmp = sb("block_compare", [P, MAXBLK, NE])
        ctl_f = sb("control_f", [P, 1 + MAXBLK])
        code = sb("pick_codes", [P, NT, TOPK], I32)
        dest = sb("pick_slots", [P, NT * TOPK], I32)
        fill = sb("unused_slots", [P, NSLOT // 64], I32)
        wg = sb("ple_gate_w_sb", [P, DT, D])
        wp = sb("ple_w_sb", [P, 2, D])
        bg = sb("ple_gate_bias", [P, D])
        p_tok = sb("p_tokens", [P, NT, PLE])
        pT = sb("pT", [P, 2, T])
        x1 = sb("x1_rows", [P, R, D])
        t = sb("ple_work", [P, 3, 512])
        rw_in = sem("t_rw_in")
        w_in = sem("t_w_in")
        p_in = sem("t_p_in")
        x1_in = [sem(f"t_x1_in{i}") for i in range(R)]
        ids_ready = sem("t_ids_ready")
        fill_out = sem("t_fill_out")
        logit_prod = sem("t_logit_prod")
        step = sem("t_step")
        picked_ready = sem("t_picked_ready")
        rank_prod = sem("t_rank_prod")
        diff_ready = sem("t_diff_ready")
        gate_exp = sem("t_gate_exp")
        dest_ready = sem("t_dest_ready")
        scattered = sem("t_scattered")
        p_turned = sem("t_p_turned")
        p_moved = sem("t_p_moved")
        prod = sem("t_prod")
        biased = sem("t_biased")
        sig_ready = sem("t_sig_ready")
        mul_ready = sem("t_mul_ready")
        res_ready = sem("t_res_ready")
        res_out = [sem(f"t_res_out{i}") for i in range(R)]
        block = ctx.enter_context(nc.Block())
        units = [(i, half) for i in range(NT) for half in range(2)]

        @block.sync
        def _(sp):
            sp.dma_start(rw[:], g.router_w[0].rearrange("(k p) e -> p k e", p=P)).then_inc(rw_in, 16)
            sp.dma_start(rb[:], g.router_b.broadcast_to([P, NE])).then_inc(rw_in, 16)
            sp.dma_start(p_tok[:, 0:NT - 1, :], g.p_prompt[0, 0].rearrange("(i p) d -> p i d", p=P)
                         ).then_inc(p_in, 16)
            sp.dma_start(p_tok[:, NT - 1, :], g.p_sample[0].rearrange("b t d -> (b t) d")).then_inc(p_in, 16)
            sp.dma_start(wg[:], g.ple_gate_w[0].rearrange("(k p) n -> p k n", p=P)).then_inc(w_in, 16)
            sp.dma_start(wp[:], g.ple_w[0].rearrange("(k p) n -> p k n", p=P)).then_inc(w_in, 16)
            sp.dma_start(bg[:], g.ple_gate_b.broadcast_to([P, D])).then_inc(w_in, 16)
            sp.wait_ge(ids_ready, 1)
            sp.dma_start(g.table_d.rearrange("(p c) o -> p (c o)", p=64), fill[0:64, :]).then_inc(fill_out, 16)
            for i in range(NT):
                if i >= R:
                    sp.wait_ge(res_out[i % R], 16 * (i // R))
                sp.dma_start(x1[:, i % R, :], g.x1_d[i * P:(i + 1) * P, :]).then_inc(x1_in[i % R], 16)

        @block.gpsimd
        def _(pool):
            pool.memset(fill[:], T * TOPK).then_inc(ids_ready, 1)
            pool.iota(code[:], pattern=[[P * TOPK, NT], [1, TOPK]], base=0, channel_multiplier=TOPK)
            pool.iota(eid[:], pattern=[[1, NE]], base=0, channel_multiplier=0, allow_small_or_imprecise_dtypes=True)
            pool.iota(bid[:], pattern=[[1, MAXBLK]], base=0, channel_multiplier=0,
                      allow_small_or_imprecise_dtypes=True).then_inc(ids_ready, 1)
            pool.wait_ge(fill_out, 16)
            pool.wait_ge(ids_ready, 2)
            pool.wait_ge(dest_ready, 1)
            for i in range(NT):
                for k in range(TOPK):
                    c = i * TOPK + k
                    pool.indirect_dma_start(
                        out=g.table_d, out_offset=bass.IndirectOffsetOnAxis(ap=dest[:, c:c + 1], axis=0),
                        in_=code[:, i, k:k + 1], in_offset=None).then_inc(scattered, 16)
            pool.wait_ge(scattered, 16 * NT * TOPK)

        @block.tensor
        def _(pe):
            pe.wait_ge(rw_in, 32)
            for i in range(NT):
                for k in range(DT):
                    last = nc.tensor.matmul(g.bank[0][:, i * NE:(i + 1) * NE], x1T[:, k, i * P:(i + 1) * P],
                                            rw[:, k, :], start=(k == 0), stop=(k == DT - 1))
            last.then_inc(logit_prod, 1)
            pe.wait_ge(p_in, 32)
            for i in range(NT):
                if i >= 4:
                    pe.wait_ge(p_moved, i // 2 - 1)
                for k in range(2):
                    last = nc.tensor.transpose(g.bank[6 + i // 2 % 2][:, (k * 2 + i % 2) * P:(k * 2 + i % 2 + 1) * P],
                                               p_tok[:, i, k * P:(k + 1) * P], g.ident[:])
                if i % 2 or i == NT - 1:
                    last.then_inc(p_turned, 1)
            pe.wait_ge(w_in, 48)
            pe.wait_ge(p_moved, 5)
            for n, (i, half) in enumerate(units):
                if n == 6:
                    pe.wait_ge(picked_ready, 1)
                    nc.tensor.matmul(g.bank[0][:, 0:NT * NE], g.tri_before[:], picked[:].rearrange("p i e -> p (i e)"),
                                     start=True, stop=True).then_inc(rank_prod, 1)
                    nc.tensor.matmul(g.bank[1][:, 0:NT * NE], g.ones[:], picked[:].rearrange("p i e -> p (i e)"),
                                     start=True, stop=True).then_inc(rank_prod, 1)
                if n >= 3:
                    pe.wait_ge(mul_ready, n - 2)
                gate, proj = g.bank[2 + 2 * (n % 3)], g.bank[3 + 2 * (n % 3)]
                cols = slice(half * 512, (half + 1) * 512)
                for k in range(DT):
                    nc.tensor.matmul(gate[:], x1T[:, k, i * P:(i + 1) * P], wg[:, k, cols], start=(k == 0),
                                     stop=(k == DT - 1))
                for k in range(2):
                    last = nc.tensor.matmul(proj[:], pT[:, k, i * P:(i + 1) * P], wp[:, k, cols], start=(k == 0),
                                            stop=(k == 1))
                last.then_inc(prod, 1)

        @block.scalar
        def _(act):
            for c in range(5):
                n = min(2, NT - 2 * c)
                act.wait_ge(p_turned, c + 1)
                nc.scalar.copy(pT[:, :, 2 * c * P:(2 * c + n) * P],
                               g.bank[6 + c % 2][:].rearrange("p (k t) -> p k t", k=2)[:, :, 0:n * P]
                               ).then_inc(p_moved, 1)
            act.wait_ge(diff_ready, 1)
            nc.scalar.activation(g.gates[:], g.gates[:], ACT.Exp).then_inc(gate_exp, 1)
            for n, (i, half) in enumerate(units):
                act.wait_ge(biased, n + 1)
                nc.scalar.activation(t[:, n % 3, :], t[:, n % 3, :], ACT.Sigmoid).then_inc(sig_ready, 1)
                if half:
                    act.wait_ge(res_ready, n + 1)
                    act.dma_start(g.residual_d[i], x1[:, i % R, :]).then_inc(res_out[i % R], 16)
            for s in res_out:
                act.wait_ge(s, 16 * (NT // R))

        @block.vector
        def _(dve):
            count = [0]

            def link(ins):
                count[0] += 1
                ins.then_inc(step, 1)
                dve.wait_ge(step, count[0])

            def add_bias(n):
                half = n % 2
                if n == 0:
                    dve.wait_ge(w_in, 48)
                dve.wait_ge(prod, n + 1)
                nc.vector.tensor_tensor(t[:, n % 3, :], g.bank[2 + 2 * (n % 3)][:],
                                        bg[:, half * 512:(half + 1) * 512], ALU.add).then_inc(biased, 1)

            def add_residual(n):
                i, half = units[n]
                dve.wait_ge(sig_ready, n + 1)
                nc.vector.tensor_tensor(t[:, n % 3, :], t[:, n % 3, :], g.bank[3 + 2 * (n % 3)][:],
                                        ALU.mult).then_inc(mul_ready, 1)
                dve.wait_ge(mul_ready, n + 1)
                dve.wait_ge(x1_in[i % R], 16 * (i // R + 1))
                part = x1[:, i % R, half * 512:(half + 1) * 512]
                nc.vector.scalar_tensor_tensor(out=part, in0=part, scalar=ALPHA, in1=t[:, n % 3, :], op0=ALU.mult,
                                               op1=ALU.add).then_inc(res_ready, 1)

            def pick():
                dve.wait_ge(logit_prod, 1)
                link(nc.vector.tensor_tensor(lg[:], g.bank[0][:, 0:NT * NE].rearrange("p (i e) -> p i e", i=NT),
                                             rb[:].unsqueeze(1).broadcast_to([P, NT, NE]), ALU.add))
                for i in range(NT):
                    last = nc.vector.max(top[:, i, :], lg[:, i, :])
                link(last)
                for i in range(NT):
                    last = nc.vector.max_index(top_i[:, i, :], top[:, i, :], lg[:, i, :])
                link(last)
                link(nc.vector.tensor_copy(top_f[:], top_i[:, :, 0:TOPK]))
                nc.vector.tensor_tensor(g.gates[:].rearrange("p (i k) -> p i k", k=TOPK), top[:, :, 0:TOPK],
                                        top[:, :, 0:1].broadcast_to([P, NT, TOPK]),
                                        ALU.subtract).then_inc(diff_ready, 1)
                dve.wait_ge(ids_ready, 2)
                flat = one_hot[:].rearrange("p i k e -> p (i k) e")
                link(nc.vector.tensor_tensor(flat, eid[:].unsqueeze(1).broadcast_to([P, NT * TOPK, NE]),
                                             top_f[:].rearrange("p i k -> p (i k)").unsqueeze(2).broadcast_to(
                                                 [P, NT * TOPK, NE]), ALU.is_equal))
                link(nc.vector.tensor_tensor(picked[:], one_hot[:, :, 0, :], one_hot[:, :, 1, :], ALU.add))
                link(nc.vector.tensor_tensor(picked[:], picked[:], one_hot[:, :, 2, :], ALU.add))
                nc.vector.tensor_tensor(picked[:], picked[:], one_hot[:, :, 3, :], ALU.add).then_inc(picked_ready, 1)
                dve.wait_ge(gate_exp, 1)
                gv = g.gates[:].rearrange("p (i k) -> p i k", k=TOPK)
                link(nc.vector.tensor_reduce(gsum[:], gv, AX_X, ALU.add))
                link(nc.vector.reciprocal(gsum[:], gsum[:]))
                nc.vector.tensor_tensor(gv, gv, gsum[:].broadcast_to([P, NT, TOPK]), ALU.mult)

            def place():
                dve.wait_ge(rank_prod, 2)
                link(nc.vector.memset(before[:, 0, :], 0.0))
                for i in range(NT):
                    link(nc.vector.tensor_tensor(before[:, i + 1, :], before[:, i, :],
                                                 g.bank[1][:, i * NE:(i + 1) * NE], ALU.add))
                link(nc.vector.tensor_tensor(rank[:], before[:, 0:NT, :],
                                             g.bank[0][:, 0:NT * NE].rearrange("p (i e) -> p i e", i=NT), ALU.add))
                nblk, upto, base, one = (blocks[:, a, :] for a in range(4))
                count_e = before[:, NT, :]
                link(nc.vector.memset(one, 1.0))
                link(nc.vector.tensor_scalar(nblk, count_e, 0.0, None, ALU.is_gt))
                for j in range(1, T // SLOTS):
                    link(nc.vector.scalar_tensor_tensor(out=nblk, in0=count_e, scalar=float(j * SLOTS), in1=nblk,
                                                        op0=ALU.is_gt, op1=ALU.add))
                link(nc.vector.tensor_tensor_scan(upto, one, nblk, 0.0, ALU.mult, ALU.add))
                link(nc.vector.tensor_tensor(base, upto, nblk, ALU.subtract))
                link(nc.vector.tensor_scalar(base, base, float(SLOTS), None, ALU.mult))
                link(nc.vector.tensor_tensor(rank[:], rank[:], base.unsqueeze(1).broadcast_to([P, NT, NE]), ALU.add))
                for k in range(TOPK):
                    last = nc.vector.tensor_tensor(one_hot[:, :, k, :], one_hot[:, :, k, :], rank[:], ALU.mult)
                link(last)
                link(nc.vector.tensor_reduce(dest_f[:], one_hot[:].rearrange("p i k e -> p (i k) e"), AX_X, ALU.add))
                nc.vector.tensor_copy(dest[:], dest_f[:]).then_inc(dest_ready, 1)
                link(nc.vector.tensor_tensor(cmp[:], upto.unsqueeze(1).broadcast_to([P, MAXBLK, NE]),
                                             bid[:].unsqueeze(2).broadcast_to([P, MAXBLK, NE]), ALU.is_le))
                link(nc.vector.tensor_reduce(ctl_f[:, 1:], cmp[:], AX_X, ALU.add))
                link(nc.vector.tensor_scalar(ctl_f[:, 1:], ctl_f[:, 1:], float(NE - 1), None, ALU.min))
                link(nc.vector.tensor_scalar(bid[:, 0::2], bid[:, 0::2], upto[:, NE - 1:NE], None, ALU.is_lt))
                link(nc.vector.tensor_reduce(ctl_f[:, 0:1], bid[:, 0::2], AX_X, ALU.add))
                link(nc.vector.tensor_scalar(ctl_f[:, 0:1], ctl_f[:, 0:1], 1.0, None, ALU.subtract))
                link(nc.vector.tensor_copy(g.ctl[:], ctl_f[:]))

            pick()
            for n in range(len(units) + 1):
                if n < len(units):
                    add_bias(n)
                if n == 7:
                    place()
                if n:
                    add_residual(n - 1)


def stage_experts(nc, g):
    S0, S1 = P, SLOTS - P
    ROWS = ((0, S0), (S0, S1))
    HF = FF // 2
    OUTS = ((6, 1, 0), (7, 1, 1), (4, 0, 0), (5, 0, 1))
    with ExitStack() as ctx:
        sem = ctx.enter_context(stage_semaphores(nc))
        def sb(name, shape, dt=F32):
            return ctx.enter_context(nc.sbuf_tensor(name, shape, dt))

        w1 = sb("expert_w1", [P, 2, DT, 2, HF])
        w2 = sb("expert_w2", [P, FT, D])
        w1_lo = sb("expert_w1_low", [P, 2, DT, 2, HF], F32R)
        w2_lo = sb("expert_w2_low", [P, FT, D], F32R)
        w1_hi = sb("expert_w1_high", [P, 2, DT, 2, HF], F32R)
        w2_hi = sb("expert_w2_high", [P, FT, D], F32R)
        b2 = sb("expert_b2", [P, 2, D])
        b1T = sb("expert_b1T", [P, NE, DT])
        b1 = sb("expert_b1", [P, 2, DT])
        code = sb("slot_codes", [P, 2], I32)
        out_code = sb("slot_codes_out", [P, 2, 2], I32)
        idx = sb("slot_tokens", [P, 2], I32)
        xg = sb("slot_rows", [P, 2, D])
        xgT = sb("slot_rowsT", [P, 2, DT, 2, SLOTS], F32R)
        gt = sb("gate_part", [P, 2, SLOTS])
        up = sb("up_part", [P, 2, SLOTS])
        low = sb("low_part_and_bias", [P, 2, 2, SLOTS])
        act_t = sb("expert_act", [P, 2, SLOTS])
        act_hi = sb("expert_act_high", [P, FT, SLOTS], F32R)
        act_lo = sb("expert_act_low", [P, FT, SLOTS], F32R)
        y = sb("expert_y", [P, 2, D])
        b1_rows = y[:, 0, 0:2 * P].rearrange("p (a c) -> p a c", a=2)
        b1_in = sem("e_b1_in")
        idx_ready = sem("e_idx_ready")
        codes_kept = sem("e_codes_kept")
        b1_turned = sem("e_b1_turned")
        b1_moved = sem("e_b1_moved")
        b1_picked = sem("e_b1_picked")
        idx_in, xg_in, y_out = (sem(f"e_{n}") for n in ("idx_in", "xg_in", "y_out"))
        w1_in = [sem(f"e_w1_in{pair}") for pair in range(2)]
        w2_in = sem("e_w2_in")
        t_ready = sem("e_t_ready")
        t_high = sem("e_t_high")
        t_moved = sem("e_t_moved")
        w1_high = sem("e_w1_high")
        w1_split = sem("e_w1_split")
        w1_last_split = sem("e_w1_last_split")
        w1_all_split = sem("e_w1_all_split")
        w2_high = sem("e_w2_high")
        w2_split = sem("e_w2_split")
        h_ready = sem("e_h_ready")
        h_free = sem("e_h_free")
        low_ready = sem("e_low_ready")
        gate_sum = sem("e_gate_sum")
        clipped = sem("e_clipped")
        up_step = sem("e_up_step")
        sig_ready = sem("e_sig_ready")
        glu_step = sem("e_glu_step")
        act_ready = sem("e_act_ready")
        act_high = sem("e_act_high")
        act_split = sem("e_act_split")
        y_ready = sem("e_y_ready")
        y_free = sem("e_y_free")
        y_left = sem("e_y_left")
        waits_passed = sem("e_waits_passed")
        block = ctx.enter_context(nc.Block())

        def full_turns(eng):
            return eng.value_load(g.ctl[0:1, 0:1], min_val=T * TOPK // SLOTS // 2 - 1, max_val=MAXBLK // 2 - 1)

        def each_block(eng, step):
            last = full_turns(eng)
            with eng.Fori(0, last, 1) as it:
                for par in range(2):
                    step(2 * it + par, par, 2)
            for par in range(2):
                step(2 * last + par, par, 1 - par)

        def expert_of(eng, n):
            return eng.value_load(g.ctl[0:1, bass.ds(n + 1, 1)], min_val=0, max_val=NE - 1)

        def w1_chunk(tile, f):
            return tile[:, f // 2, :, :, f % 2 * P:(f % 2 + 1) * P]

        @block.sync
        def _(sp):
            def load_w1(e, pair):
                src = g.exp_w1[0][bass.ds(e, 1)].rearrange("o (k p) n -> p (o k) n", p=P)
                for part in range(2):
                    lo = part * FF + pair * HF
                    sp.dma_start(w1[:, pair, :, part, :], src[:, :, lo:lo + HF]).then_inc(w1_in[pair], 16)

            def load_w2(e):
                sp.dma_start(w2[:], g.exp_w2[0][bass.ds(e, 1)].rearrange("o (k p) n -> p (o k) n", p=P)
                             ).then_inc(w2_in, 16)

            def load_b2(e, par):
                sp.dma_start(b2[:, par, :], g.exp_b2[0][bass.ds(e, 1)].broadcast_to([P, D])).then_inc(w2_in, 16)

            for half in range(2):
                sp.dma_start(b1_rows[:, half, :], g.exp_b1[0].rearrange("e (f p) -> (e f) p", p=P)
                             [half * P:(half + 1) * P, :]).then_inc(b1_in, 16)
            e = expert_of(sp, 0)
            load_w1(e, 0)
            sp.wait_ge(xg_in, 32)
            load_w1(e, 1)
            load_w2(e)
            load_b2(e, 0)
            e = expert_of(sp, 1)
            sp.wait_ge(w1_split, 2)
            load_w1(e, 0)
            sp.wait_ge(w1_all_split, 1)
            load_w1(e, 1)

            def step(n, par, ahead):
                if ahead:
                    e = expert_of(sp, n + 1)
                    sp.wait_ge(w2_split, 4 * n + 4)
                    load_w2(e)
                    sp.wait_ge(y_free, 4 * n + 4)
                    load_b2(e, 1 - par)
                if ahead == 2:
                    e = expert_of(sp, n + 2)
                    sp.wait_ge(w1_split, 3 * n + 5)
                    load_w1(e, 0)
                    sp.wait_ge(w1_all_split, n + 2)
                    load_w1(e, 1)

            each_block(sp, step)

        @block.gpsimd
        def _(pool):
            def wait(semaphore, value):
                pool.wait_ge(semaphore, value)
                pool.nop().then_inc(waits_passed, 1)

            def gather(n):
                for r, (lo, rows) in enumerate(ROWS):
                    pool.dma_start(code[0:rows, r:r + 1],
                                   g.table_d[bass.ds(n * SLOTS + lo, rows)]).then_inc(idx_in, 16)
                wait(idx_in, 32 * n + 32)
                for r, (lo, rows) in enumerate(ROWS):
                    pool.tensor_scalar(idx[0:rows, r:r + 1], code[0:rows, r:r + 1], -1.5, 0.25, ALU.add,
                                       ALU.mult).then_inc(idx_ready, 1)
                wait(idx_ready, 2 * n + 2)
                for r, (lo, rows) in enumerate(ROWS):
                    pool.indirect_dma_start(
                        out=xg[0:rows, r, :], out_offset=None, in_=g.x1_d,
                        in_offset=bass.IndirectOffsetOnAxis(ap=idx[0:rows, r:r + 1], axis=0)
                    ).then_inc(xg_in, 16)

            def keep_codes(n, par):
                for r, (lo, rows) in enumerate(ROWS):
                    pool.tensor_copy(out_code[0:rows, par, r:r + 1], code[0:rows, r:r + 1]).then_inc(codes_kept, 1)
                wait(codes_kept, 2 * n + 2)

            def w1_last_low_part(m):
                wait(w1_high, 4 * m + FT)
                pool.tensor_tensor(w1_chunk(w1_lo, FT - 1), w1_chunk(w1, FT - 1),
                                   w1_chunk(w1_hi, FT - 1).bitcast(F32), ALU.subtract).then_inc(w1_last_split, 1)
                wait(w1_last_split, m + 1)
                wait(w1_split, 3 * m + 3)
                pool.nop().then_inc(w1_all_split, 1)

            pool.nop().then_inc(y_left, 1)
            gather(0)
            pool.wait_ge(t_ready, 4)
            keep_codes(0, 0)
            gather(1)
            w1_last_low_part(0)

            def step(n, par, ahead):
                if ahead:
                    wait(t_ready, 4 * n + 8)
                    keep_codes(n + 1, 1 - par)
                    if ahead == 2:
                        gather(n + 2)
                    w1_last_low_part(n + 1)
                wait(y_free, 4 * n + 8)
                for r, (lo, rows) in enumerate(ROWS):
                    pool.indirect_dma_start(
                        out=g.y_d, out_offset=bass.IndirectOffsetOnAxis(ap=out_code[0:rows, par, r:r + 1], axis=0),
                        in_=y[0:rows, r, :], in_offset=None, bounds_check=T * TOPK - 1, oob_is_err=False
                    ).then_inc(y_out, 16)
                wait(y_out, 32 * n + 32)
                pool.nop().then_inc(y_left, 1)

            each_block(pool, step)

        @block.tensor
        def _(pe):
            def turn_rows(m, q):
                pe.wait_ge(xg_in, 32 * m + 32)
                pe.wait_ge(t_moved, 4 * m + q + 1)
                for k in range(2):
                    for r, (lo, rows) in enumerate(ROWS):
                        f = 2 * q + k
                        last = nc.tensor.transpose(
                            g.bank[q % 2][:, k * SLOTS + lo:k * SLOTS + lo + rows],
                            xg[0:rows, r, f * P:(f + 1) * P], g.ident[0:rows, 0:rows])
                last.then_inc(t_ready, 1)

            for s, credits in ((t_moved, 2), (h_free, 2), (y_free, 4)):
                nc.tensor.nop().then_inc(s, credits)
            pe.wait_ge(b1_in, 32)
            for half in range(2):
                last = nc.tensor.transpose(g.bank[2][:, half * P:(half + 1) * P], b1_rows[:, half, :], g.ident[:])
            last.then_inc(b1_turned, 1)
            pe.wait_ge(b1_moved, 1)
            for q in range(4):
                turn_rows(0, q)

            def step(n, par, ahead):
                n4 = 4 * n
                for f in range(FT):
                    if f < FT - 1:
                        pe.wait_ge(w1_split, 3 * n + f + 1)
                    else:
                        pe.wait_ge(w1_last_split, n + 1)
                    pe.wait_ge(h_free, n4 + f + 1)
                    if f == 1:
                        pe.wait_ge(y_free, n4 + 4)
                    for part in range(2):
                        out = g.bank[2 + f % 2 * 2 + part]
                        for k in range(DT):
                            if f == 0 and part == 0 and k % 2 == 0:
                                pe.wait_ge(t_moved, n4 + k // 2 + 3)
                            hi, lo = (w1_chunk(tile, f)[:, k, part, :] for tile in (w1_hi, w1_lo))
                            nc.tensor.matmul(out[:, 0:2 * SLOTS], hi, xgT[:, par, k].rearrange("p a s -> p (a s)"),
                                             start=(k == 0), stop=(k == DT - 1), skip_group_check=True)
                            last = nc.tensor.matmul(out[:, 0:SLOTS], lo, xgT[:, par, k, 0, :], start=False,
                                                    stop=(k == DT - 1), skip_group_check=True)
                    last.then_inc(h_ready, 1)
                    if ahead:
                        turn_rows(n + 1, f)
                for f in range(FT):
                    pe.wait_ge(w2_split, n4 + f + 1)
                    pe.wait_ge(act_split, n4 + f + 1)
                    for bank, r, half in OUTS:
                        lo, rows = ROWS[r]
                        if f == 0 and bank == 4:
                            pe.wait_ge(h_free, n4 + 6)
                        out, cols = g.bank[bank][0:rows, :], slice(half * 512, (half + 1) * 512)
                        a_hi, a_lo = act_hi[:, f, lo:lo + rows], act_lo[:, f, lo:lo + rows]
                        nc.tensor.matmul(out, a_hi, w2_hi[:, f, cols], start=(f == 0), stop=False)
                        nc.tensor.matmul(out, a_hi, w2_lo[:, f, cols], start=False, stop=False)
                        last = nc.tensor.matmul(out, a_lo, w2_hi[:, f, cols], start=False, stop=(f == FT - 1))
                        if f == FT - 1:
                            last.then_inc(y_ready, 1)

            each_block(pe, step)

        @block.scalar
        def _(act):
            def w1_high_part(f, m):
                act.wait_ge(w1_in[f // 2], 32 * m + 32)
                nc.scalar.copy(w1_chunk(w1_hi, f), w1_chunk(w1, f)).then_inc(w1_high, 1)

            def rows_high_part(par, m, q):
                act.wait_ge(t_ready, 4 * m + q + 1)
                nc.scalar.copy(xgT[:, par, 2 * q:2 * q + 2, 0, :],
                               g.bank[q % 2][:, 0:2 * SLOTS].rearrange("p (k s) -> p k s", k=2)).then_inc(t_high, 1)

            for f in range(FT):
                w1_high_part(f, 0)
                if f == 0:
                    for q in range(4):
                        rows_high_part(0, 0, q)

            def step(n, par, ahead):
                n4 = 4 * n
                for f in range(FT):
                    act.wait_ge(h_ready, n4 + f + 1)
                    act.wait_ge(b1_picked, n + 1)
                    for part in range(2):
                        last = nc.scalar.activation(low[:, f % 2, part, :],
                                                    g.bank[2 + 2 * (f % 2) + part][:, SLOTS:2 * SLOTS],
                                                    ACT.Identity, bias=b1[:, par, part * FT + f:part * FT + f + 1])
                    last.then_inc(low_ready, 1)
                    act.wait_ge(clipped, n4 + f + 1)
                    nc.scalar.activation(low[:, f % 2, 0, :], gt[:, f % 2, :], ACT.Sigmoid,
                                         scale=1.702).then_inc(sig_ready, 1)
                    act.wait_ge(w2_in, 32 * n + 32)
                    nc.scalar.copy(w2_hi[:, f, :], w2[:, f, :]).then_inc(w2_high, 1)
                    act.wait_ge(act_ready, n4 + f + 1)
                    nc.scalar.copy(act_hi[:, f, :], act_t[:, f % 2, :]).then_inc(act_high, 1)
                    if ahead:
                        rows_high_part(1 - par, n + 1, f)
                if ahead:
                    for f in range(FT):
                        w1_high_part(f, n + 1)

            each_block(act, step)

        @block.vector
        def _(dve):
            def w1_low_part(f, m4):
                dve.wait_ge(w1_high, m4 + f + 1)
                nc.vector.tensor_tensor(w1_chunk(w1_lo, f), w1_chunk(w1, f), w1_chunk(w1_hi, f).bitcast(F32),
                                        ALU.subtract).then_inc(w1_split, 1)

            def rows_low_part(par, m, q):
                dve.wait_ge(t_high, 4 * m + q + 1)
                hi, lo = (xgT[:, par, 2 * q:2 * q + 2, a, :] for a in range(2))
                nc.vector.tensor_tensor(lo, g.bank[q % 2][:, 0:2 * SLOTS].rearrange("p (k s) -> p k s", k=2),
                                        hi.bitcast(F32), ALU.subtract).then_inc(t_moved, 1)

            dve.wait_ge(b1_turned, 1)
            nc.vector.tensor_copy(b1T[:].rearrange("p e f -> p (e f)"), g.bank[2][:, 0:2 * P]).then_inc(b1_moved, 1)
            dve.wait_ge(b1_moved, 1)
            for f in range(FT - 1):
                w1_low_part(f, 0)
                if f == 0:
                    for q in range(4):
                        rows_low_part(0, 0, q)

            def step(n, par, ahead):
                n4 = 4 * n
                e = expert_of(dve, n)
                nc.vector.tensor_copy(b1[:, par, :], b1T[:, bass.ds(e, 1), :].rearrange("p o f -> p (o f)")
                                      ).then_inc(b1_picked, 1)
                dve.wait_ge(b1_picked, n + 1)
                for f in range(FT):
                    s = f % 2
                    dve.wait_ge(h_ready, n4 + f + 1)
                    gate, lift = g.bank[2 + 2 * s], g.bank[3 + 2 * s]
                    dve.wait_ge(low_ready, n4 + f + 1)
                    nc.vector.tensor_tensor(gt[:, s, :], gate[:, 0:SLOTS], low[:, s, 0, :], ALU.add
                                            ).then_inc(gate_sum, 1)
                    nc.vector.tensor_tensor(up[:, s, :], lift[:, 0:SLOTS], low[:, s, 1, :], ALU.add
                                            ).then_inc(h_free, 1)
                    dve.wait_ge(gate_sum, n4 + f + 1)
                    nc.vector.tensor_scalar(gt[:, s, :], gt[:, s, :], 7.0, None, ALU.min).then_inc(clipped, 1)
                    dve.wait_ge(h_free, n4 + f + 3)
                    nc.vector.tensor_scalar(up[:, s, :], up[:, s, :], 7.0, -7.0, ALU.min, ALU.max
                                            ).then_inc(up_step, 1)
                    dve.wait_ge(clipped, n4 + f + 1)
                    dve.wait_ge(up_step, n4 + f + 1)
                    nc.vector.scalar_tensor_tensor(out=up[:, s, :], in0=up[:, s, :], scalar=1.0, in1=gt[:, s, :],
                                                   op0=ALU.add, op1=ALU.mult).then_inc(glu_step, 1)
                    dve.wait_ge(glu_step, n4 + f + 1)
                    dve.wait_ge(sig_ready, n4 + f + 1)
                    nc.vector.tensor_tensor(act_t[:, s, :], up[:, s, :], low[:, s, 0, :],
                                            ALU.mult).then_inc(act_ready, 1)
                    dve.wait_ge(w2_high, n4 + f + 1)
                    nc.vector.tensor_tensor(w2_lo[:, f, :], w2[:, f, :],
                                            w2_hi[:, f, :].bitcast(F32), ALU.subtract).then_inc(w2_split, 1)
                    dve.wait_ge(act_high, n4 + f + 1)
                    nc.vector.tensor_tensor(act_lo[:, f, :], act_t[:, s, :], act_hi[:, f, :].bitcast(F32),
                                            ALU.subtract).then_inc(act_split, 1)
                    if ahead:
                        rows_low_part(1 - par, n + 1, f)
                if ahead:
                    for f in range(FT - 2):
                        w1_low_part(f, n4 + 4)
                dve.wait_ge(y_left, n + 1)
                for u, (bank, r, half) in enumerate(OUTS):
                    rows = ROWS[r][1]
                    dve.wait_ge(y_ready, n4 + u + 1)
                    cols = slice(half * 512, (half + 1) * 512)
                    nc.vector.tensor_tensor(y[0:rows, r, cols], g.bank[bank][0:rows, :],
                                            b2[0:rows, par, cols], ALU.add).then_inc(y_free, 1)
                if ahead:
                    w1_low_part(FT - 2, n4 + 4)

            each_block(dve, step)


def stage_combine(nc, g):
    with ExitStack() as ctx:
        sem = ctx.enter_context(stage_semaphores(nc))
        def sb(name, shape):
            return ctx.enter_context(nc.sbuf_tensor(name, shape, F32))

        res = sb("residual", [P, NT, D])
        rows = sb("expert_rows", [P, NT, TOPK, D])
        norm = sb("ln2_scale_shift", [P, 2, D])
        stats = sb("ln2_stats", [P, NT, 2, 6])
        mv = sb("ln2_mean_var", [P, NT, 2])
        shift = sb("ln2_shift", [P, NT, 1])
        norm_in = sem("k_norm_in")
        res_in = [sem(f"k_res_in{i}") for i in range(NT)]
        rows_in = [sem(f"k_rows_in{i}") for i in range(NT)]
        first_ready = sem("k_first_ready")
        first_added = sem("k_first_added")
        added = sem("k_added")
        stat_ready = sem("k_stat_ready")
        var_ready = sem("k_var_ready")
        std_ready = sem("k_std_ready")
        rstd_ready = sem("k_rstd_ready")
        shift_ready = sem("k_shift_ready")
        hat_ready = sem("k_hat_ready")
        scaled = sem("k_scaled")
        y_ready = sem("k_y_ready")
        y_out = sem("k_y_out")
        block = ctx.enter_context(nc.Block())

        @block.sync
        def _(sp):
            for i in range(NT):
                sp.dma_start(res[:, i, :], g.residual_d[i]).then_inc(res_in[i], 16)
                sp.dma_start(rows[:, i], g.y_d[i * P * TOPK:(i + 1) * P * TOPK, :].rearrange(
                    "(p k) d -> p k d", k=TOPK)).then_inc(rows_in[i], 16)
                if i == 0:
                    for a, v in enumerate((g.ln2_g, g.ln2_b)):
                        sp.dma_start(norm[:, a, :], v.broadcast_to([P, D])).then_inc(norm_in, 16)
            yp = g.o_y_p[0].rearrange("(i p) d -> i p d", p=P)
            for i in range(NT):
                sp.wait_ge(y_ready, i + 1)
                dst = yp[i] if i < NT - 1 else g.o_y_s.rearrange("b t d -> (b t) d")
                sp.dma_start(dst, res[:, i, :]).then_inc(y_out, 16)
            sp.wait_ge(y_out, 16 * NT)

        @block.vector
        def _(dve):
            def add_rows(i):
                dve.wait_ge(first_added, i + 1)
                for k in range(1, TOPK):
                    c = i * TOPK + k
                    nc.vector.scalar_tensor_tensor(out=res[:, i, :], in0=rows[:, i, k, :], scalar=g.gates[:, c:c + 1],
                                                   in1=res[:, i, :], op0=ALU.mult, op1=ALU.add).then_inc(added, 1)
                    dve.wait_ge(added, (TOPK - 1) * i + k)
                for half in range(2):
                    nc.vector.bn_stats(stats[:, i, half, :], res[:, i, half * 512:(half + 1) * 512]
                                       ).then_inc(stat_ready, 1)
                dve.wait_ge(stat_ready, 2 * i + 2)
                nc.vector.bn_aggr(mv[:, i, :], stats[:, i].rearrange("p a b -> p (a b)")).then_inc(var_ready, 1)
                dve.wait_ge(std_ready, i + 1)
                nc.vector.reciprocal(mv[:, i, 1:2], mv[:, i, 1:2]).then_inc(rstd_ready, 1)
                dve.wait_ge(rstd_ready, i + 1)
                nc.vector.scalar_tensor_tensor(out=shift[:, i, :], in0=mv[:, i, 0:1], scalar=-1.0, in1=mv[:, i, 1:2],
                                               op0=ALU.mult, op1=ALU.mult).then_inc(shift_ready, 1)

            def scale(i):
                dve.wait_ge(hat_ready, i + 1)
                nc.vector.tensor_tensor(res[:, i, :], res[:, i, :], norm[:, 0, :], ALU.mult
                                        ).then_inc(scaled, 1)

            dve.wait_ge(norm_in, 32)
            for i in range(NT + 1):
                if i < NT:
                    add_rows(i)
                if i:
                    scale(i - 1)

        @block.gpsimd
        def _(pool):
            def add_first(i):
                pool.wait_ge(first_ready, i + 1)
                pool.wait_ge(res_in[i], 16)
                pool.tensor_tensor(res[:, i, :], res[:, i, :], rows[:, i, 0, :], ALU.add
                                   ).then_inc(first_added, 1)

            pool.wait_ge(norm_in, 32)
            for i in range(-2, NT):
                if i + 2 < NT:
                    add_first(i + 2)
                if i >= 0:
                    pool.wait_ge(scaled, i + 1)
                    pool.tensor_tensor(res[:, i, :], res[:, i, :], norm[:, 1, :], ALU.add).then_inc(y_ready, 1)

        @block.scalar
        def _(act):
            def gate_first(i):
                act.wait_ge(rows_in[i], 16)
                nc.scalar.activation(rows[:, i, 0, :], rows[:, i, 0, :], ACT.Copy,
                                     scale=g.gates[:, i * TOPK:i * TOPK + 1]).then_inc(first_ready, 1)

            for i in range(-3, NT):
                if i + 3 < NT:
                    gate_first(i + 3)
                if i >= 0:
                    act.wait_ge(var_ready, i + 1)
                    nc.scalar.activation(mv[:, i, 1:2], mv[:, i, 1:2], ACT.Sqrt, bias=g.eps[:]).then_inc(std_ready, 1)
                    act.wait_ge(shift_ready, i + 1)
                    nc.scalar.activation(res[:, i, :], res[:, i, :], ACT.Identity, bias=shift[:, i, :],
                                         scale=mv[:, i, 1:2]).then_inc(hat_ready, 1)




def build_program(nc, i, o):
    g = Shared()
    (g.x_prompt, g.x_sample, g.cache_k, g.cache_v, g.state_conv, g.state_lru, g.state_c, g.state_n,
     g.state_m, g.p_prompt, g.p_sample, g.w_in, g.b_in, g.conv_w, g.conv_b, g.lru_wr, g.lru_br,
     g.lru_wi, g.lru_bi, g.lru_lambda, g.ml_norm_g, g.w_pa, g.w_pb, g.w_pc, g.w_out, g.ln1_g, g.ln1_b,
     g.router_w, g.router_b, g.exp_w1, g.exp_b1, g.exp_w2, g.exp_b2, g.ple_w, g.ple_gate_w,
     g.ple_gate_b, g.ln2_g, g.ln2_b) = i
    (g.o_y_p, g.o_y_s, g.o_k_p, g.o_v_p, g.o_conv_p, g.o_lru_p, g.o_c_p, g.o_n_p, g.o_m_p, g.o_k_s,
     g.o_v_s, g.o_conv_s, g.o_lru_s, g.o_c_s, g.o_n_s, g.o_m_s) = o
    g.yaT_d = nc.dram_tensor("yaT_scratch", (DT, P, T), F32).ap()
    g.x1_d = nc.dram_tensor("x1_scratch", (T + 1, D), F32).ap()
    g.residual_d = nc.dram_tensor("residual_scratch", (NT, P, D), F32).ap()
    g.table_d = nc.dram_tensor("slot_table_scratch", (NSLOT, 1), I32).ap()
    g.y_d = nc.dram_tensor("expert_rows_scratch", (T * TOPK, D), F32).ap()
    with ExitStack() as ctx:
        def sb(name, shape, dt=F32):
            return ctx.enter_context(nc.sbuf_tensor(name, shape, dt))

        g.bank = banks(nc, ctx)
        g.ident, g.eps = sb("ident", [P, P]), sb("ln_eps", [P, 1])
        g.gates = sb("expert_gates", [P, NT * TOPK])
        g.ctl = sb("loop_control", [P, 1 + MAXBLK], I32)
        with ExitStack() as trunk:
            def tb(name, shape):
                return trunk.enter_context(nc.sbuf_tensor(name, shape, F32))

            g.ones, g.neg_ones, g.tri_neg, g.tri_before = (
                tb(n, [P, P]) for n in ("ones", "neg_ones", "tri_neg", "tri_before"))
            g.strict, g.strict_s, g.causal, g.causal_s = (
                tb(n, [P, P]) for n in ("strict", "strict_s", "causal", "causal_s"))
            g.sel = tb("head_selector", [H, H, P])
            g.vec = tb("feature_vectors", [P, P])
            g.state = tb("state_columns", [P, DT, 32])
            g.coef = tb("decay_coef", [P, DT])
            g.half_b = tb("half_gate_bias", [P, 2 * DT])
            g.qbias = tb("scaled_q_bias", [P, H])
            g.mkbias = tb("scaled_mk_bias", [P, 2])
            stage_constants(nc, g)
            with ExitStack() as early:
                xT = early.enter_context(nc.sbuf_tensor("xT", [P, DT, T], F32))
                stage_transpose_x(nc, g, xT)
                stage_lru(nc, g, xT)
                yT = early.enter_context(nc.sbuf_tensor("yT", [P, 2 * H, T], F32))
                qT, ycT = yT[:, 0:H, :], yT[:, H:2 * H, :]
                with ExitStack() as attend:
                    kT = attend.enter_context(nc.sbuf_tensor("sb_kT", [P, H, T], F32))
                    v_tok = attend.enter_context(nc.sbuf_tensor("sb_v", [P, NT, 512], F32))
                    stage_sb_project(nc, g, xT, qT, kT, v_tok)
                    stage_sb_prompt(nc, g, qT, kT, v_tok)
                    stage_sb_sample(nc, g, qT, kT, v_tok)
                with ExitStack() as recur:
                    def rb(name, shape):
                        return recur.enter_context(nc.sbuf_tensor(name, shape, F32))

                    m = Shared()
                    m.qz, m.kT, m.k_tok = ycT, rb("ml_kT", [P, 2, T]), rb("ml_k", [P, NT, 256])
                    m.v_aug, m.o_gate = rb("ml_v", [P, NT, H, HD + 1]), rb("ml_o", [P, NT, 512])
                    m.w, m.cols = rb("ml_w_row", [H, T]), rb("ml_cols", [P, 4, NT, H])
                    m.s_old, m.norm_g = rb("ml_s_old", [P, H, 16]), rb("ml_norm", [P, 512])
                    with ExitStack() as rows:
                        m.ig = rows.enter_context(nc.sbuf_tensor("ml_ig_row", [H, T], F32))
                        m.fg = rows.enter_context(nc.sbuf_tensor("ml_fg_row", [H, T], F32))
                        stage_ml_project(nc, g, xT, m)
                    stage_mlstm(nc, g, m, ycT)
                mixT, x1T = xT, yT
                stage_mix(nc, g, xT, yT)
                stage_out(nc, g, mixT, x1T)
                stage_route(nc, g, x1T)
        stage_experts(nc, g)
        stage_combine(nc, g)


def kernel(**inputs):
    import concourse.bacc as bacc
    from concourse.bass_utils import run_bass_kernel_spmd

    names = ("x_prompt", "x_sample", "cache_sb_k", "cache_sb_v", "state_conv", "state_lru", "state_mlstm_c",
             "state_mlstm_n", "state_mlstm_m", "p_prompt", "p_sample", "w_in", "b_in", "conv_w", "conv_b",
             "lru_wr", "lru_br", "lru_wi", "lru_bi", "lru_lambda", "ml_norm_g", "w_pa", "w_pb", "w_pc", "w_out",
             "ln1_g", "ln1_b", "router_w", "router_b", "exp_w1", "exp_b1", "exp_w2", "exp_b2", "ple_w",
             "ple_gate_w", "ple_gate_b", "ln2_g", "ln2_b")
    shapes = ((1, TP, D), (NB, LS, D), (1, 1, TP, H, HD), (1, 1, TP, H, HD), (1, 1, CW - 1, D), (1, 1, D),
              (1, 1, H, QD, HD), (1, 1, H, QD), (1, 1, H), (1, NB, LS, H, HD), (1, NB, LS, H, HD),
              (1, NB, CW - 1, D), (1, NB, D), (1, NB, H, QD, HD), (1, NB, H, QD), (1, NB, H))
    nc = bacc.Bacc("TRN2", target_bir_lowering=False, num_devices=1)
    arrays = {f"in_{name}": np.ascontiguousarray(inputs[name]) for name in names}
    ins = [nc.dram_tensor(name, a.shape, mybir.dt.from_np(a.dtype), kind="ExternalInput").ap()
           for name, a in arrays.items()]
    outs = [nc.dram_tensor(f"out_{n}", shape, F32, kind="ExternalOutput").ap() for n, shape in enumerate(shapes)]
    build_program(nc, ins, outs)
    result = run_bass_kernel_spmd(nc, [arrays], core_ids=[0]).results[0]
    return tuple(result[f"out_{n}"] for n in range(len(shapes)))
```
